# Optimizing a Trainium2 kernel written in Bass

```python
import math
import jax, jax.numpy as jnp
from jax import lax
import numpy as np

D_MODEL = 1024
BATCH = 1
SEQ = 512
DEPTH = 2

CHUNK = 64
MEM_LEN = 256
EPS = 1e-6
NEG = -1e30
N_NORMS = 9

A_HEADS = 8
A_KV_HEADS = 2
A_GROUP = A_HEADS // A_KV_HEADS
A_HEAD_DIM = 64
A_WIDTH = A_HEADS * A_HEAD_DIM
A_KV_WIDTH = A_KV_HEADS * A_HEAD_DIM
WINDOW = 128
WIN_CHUNKS = WINDOW // CHUNK
BAND = WIN_CHUNKS * CHUNK

B_GROUPS = 4
B_WIDTH = D_MODEL // 2
B_GROUP_DIM = B_WIDTH // B_GROUPS
SGU_LEN = 128

AB_IN = A_WIDTH + 2 * A_KV_WIDTH + 2 * B_WIDTH
AB_OUT = A_WIDTH + B_WIDTH

C_HEADS = 4
C_KEY_DIM = D_MODEL // 2
C_VAL_DIM = D_MODEL
C_DK = C_KEY_DIM // C_HEADS
C_DV = C_VAL_DIM // C_HEADS
GATE_RANK = 16
GATE_TAU = 16.0
C_IN = 2 * C_KEY_DIM + 2 * C_VAL_DIM + GATE_RANK

X_HEADS = 4
X_HEAD_DIM = D_MODEL // X_HEADS

D_FF = 4 * D_MODEL

N_EVEN = (DEPTH + 1) // 2
N_ODD = DEPTH // 2

kernel_name = "hybrid_swa_sgu_gla_macaron_encoder"

def rmsnorm(x, g):
    xf = x.astype(jnp.float32)
    y = xf * lax.rsqrt(jnp.mean(xf * xf, axis=-1, keepdims=True) + EPS) * g.astype(jnp.float32)
    return y.astype(x.dtype)

def swiglu(h, w_in, w_out):
    gate, up = jnp.split(h @ w_in, 2, axis=-1)
    return (jax.nn.silu(gate) * up) @ w_out

def alibi_slopes(n):
    return np.asarray(2.0 ** (-8.0 * np.arange(1, n + 1) / n), np.float32)

def sliding_window_sink_attention(q, k, v, sink):
    b, s = q.shape[:2]
    nc = s // CHUNK
    f32 = jnp.float32
    qc = q.reshape(b, nc, CHUNK, A_KV_HEADS, A_GROUP, A_HEAD_DIM).astype(f32)

    def band(t):
        tc = t.reshape(b, nc, CHUNK, A_KV_HEADS, A_HEAD_DIM)
        pad = jnp.pad(tc, ((0, 0), (WIN_CHUNKS - 1, 0), (0, 0), (0, 0), (0, 0)))
        return jnp.concatenate([pad[:, w:w + nc] for w in range(WIN_CHUNKS)], axis=2).astype(f32)

    kb, vb = band(k), band(v)
    scores = jnp.einsum('bcqhgd,bckhd->bhgcqk', qc, kb) * (A_HEAD_DIM ** -0.5)
    qi = np.arange(CHUNK)[:, None] + (WIN_CHUNKS - 1) * CHUNK
    kj = np.arange(BAND)[None, :]
    dist = np.abs(qi - kj).astype(np.float32)
    slopes = alibi_slopes(A_HEADS).reshape(A_KV_HEADS, A_GROUP)
    bias = -slopes[:, :, None, None, None] * dist
    key_chunk = np.arange(nc)[:, None] - (WIN_CHUNKS - 1) + np.arange(BAND)[None, :] // CHUNK
    valid = (key_chunk >= 0)[:, None, :]
    scores = jnp.where(valid, scores + bias, NEG)
    sink_l = sink.astype(f32).reshape(1, A_KV_HEADS, A_GROUP, 1, 1, 1)
    m = jnp.maximum(jnp.max(scores, axis=-1, keepdims=True), sink_l)
    p = jnp.exp(scores - m)
    denom = jnp.sum(p, axis=-1, keepdims=True) + jnp.exp(sink_l - m)
    out = jnp.einsum('bhgcqk,bckhd->bcqhgd', p / denom, vb)
    return out.reshape(b, s, A_WIDTH)

def chunked_spatial_gating(u, v, w_s, b_s, norm_g):
    b, s = u.shape[:2]
    f32 = jnp.float32
    vf = v.astype(f32)
    mu = jnp.mean(vf, axis=-1, keepdims=True)
    var = jnp.mean(jnp.square(vf - mu), axis=-1, keepdims=True)
    vn = (vf - mu) * lax.rsqrt(var + EPS) * norm_g.astype(f32)
    vn = vn.reshape(b, s // SGU_LEN, SGU_LEN, B_GROUPS, B_GROUP_DIM)
    pos_chunk = np.arange(SGU_LEN) // CHUNK
    mask = pos_chunk[None, :] <= pos_chunk[:, None]
    w = jnp.where(mask, w_s.astype(f32), 0.0)
    mixed = jnp.einsum('gij,bnjgc->bnigc', w, vn) + jnp.transpose(b_s.astype(f32))[:, :, None]
    return (u.astype(f32) * mixed.reshape(b, s, B_WIDTH)).astype(u.dtype)

def mixer_ab(h, w_in, sink, sgu_w, sgu_b, sgu_g, w_out):
    b, s = h.shape[:2]
    splits = [A_WIDTH, A_WIDTH + A_KV_WIDTH, A_WIDTH + 2 * A_KV_WIDTH, A_WIDTH + 2 * A_KV_WIDTH + B_WIDTH]
    q, k, v, u, vg = jnp.split(h @ w_in, splits, axis=-1)
    ya = sliding_window_sink_attention(q.reshape(b, s, A_HEADS, A_HEAD_DIM),
                                       k.reshape(b, s, A_KV_HEADS, A_HEAD_DIM),
                                       v.reshape(b, s, A_KV_HEADS, A_HEAD_DIM), sink)
    yb = chunked_spatial_gating(u, vg, sgu_w, sgu_b, sgu_g)
    return jnp.concatenate([ya.astype(h.dtype), yb], axis=-1) @ w_out

def gated_linear_attention(h, w_in, gate_w, gate_b, head_g, w_out):
    b, s = h.shape[:2]
    nc = s // CHUNK
    f32 = jnp.float32
    splits = [C_KEY_DIM, 2 * C_KEY_DIM, 2 * C_KEY_DIM + C_VAL_DIM, 2 * C_KEY_DIM + 2 * C_VAL_DIM]
    q, k, v, r, g_lr = jnp.split(h @ w_in, splits, axis=-1)
    log_a = jax.nn.log_sigmoid((g_lr @ gate_w + gate_b).astype(f32)) / GATE_TAU
    shp_k = (b, nc, CHUNK, C_HEADS, C_DK)
    bcum = jnp.cumsum(log_a.reshape(shp_k), axis=2)
    qf = q.astype(f32).reshape(shp_k) * (C_DK ** -0.5)
    kf = k.astype(f32).reshape(shp_k)
    vf = v.astype(f32).reshape(b, nc, CHUNK, C_HEADS, C_DV)
    q_dec = qf * jnp.exp(bcum)
    k_inv = kf * jnp.exp(-bcum)
    b_last = bcum[:, :, -1:]
    k_end = kf * jnp.exp(b_last - bcum)
    causal = np.tril(np.ones((CHUNK, CHUNK), bool))
    att = jnp.where(causal, jnp.einsum('bclhk,bcmhk->bchlm', q_dec, k_inv), 0.0)
    o_intra = jnp.einsum('bchlm,bcmhv->bclhv', att, vf)

    def step(state, inp):
        qd, ke, vc, dec = inp
        o = jnp.einsum('blhk,bhkv->blhv', qd, state)
        state = dec[..., None] * state + jnp.einsum('blhk,blhv->bhkv', ke, vc)
        return state, o

    xs = (jnp.moveaxis(q_dec, 1, 0), jnp.moveaxis(k_end, 1, 0), jnp.moveaxis(vf, 1, 0),
          jnp.moveaxis(jnp.exp(b_last[:, :, 0]), 1, 0))
    _, o_inter = lax.scan(step, jnp.zeros((b, C_HEADS, C_DK, C_DV), f32), xs)
    o = (o_intra + jnp.moveaxis(o_inter, 0, 1)).reshape(b, s, C_HEADS, C_DV)
    o = o * lax.rsqrt(jnp.mean(o * o, axis=-1, keepdims=True) + EPS) * head_g.astype(f32).reshape(C_HEADS, C_DV)
    y = (o.reshape(b, s, C_VAL_DIM) * jax.nn.silu(r.astype(f32))).astype(h.dtype)
    return y @ w_out

def memory_cross_attention(h, mem_n, w_q, w_kv, w_o):
    b, s = h.shape[:2]
    f32 = jnp.float32
    q = (h @ w_q).reshape(b, s, X_HEADS, X_HEAD_DIM).astype(f32)
    k, v = jnp.split(mem_n @ w_kv, 2, axis=-1)
    k = k.reshape(b, -1, X_HEADS, X_HEAD_DIM).astype(f32)
    v = v.reshape(b, -1, X_HEADS, X_HEAD_DIM).astype(f32)
    p = jax.nn.softmax(jnp.einsum('bshd,bmhd->bhsm', q, k) * (X_HEAD_DIM ** -0.5), axis=-1)
    o = jnp.einsum('bhsm,bmhd->bshd', p, v).reshape(b, s, D_MODEL).astype(h.dtype)
    return o @ w_o

def _w(key, shape, fan_in):
    return jax.random.normal(key, shape, jnp.float32) * (fan_in ** -0.5)

def setup_inputs(seed: int = 0) -> dict:
    key = jax.random.key(seed)
    ks = jax.random.split(key, 24)
    f32 = jnp.float32
    return {
        "x": jax.random.normal(ks[0], (BATCH, SEQ, D_MODEL), f32),
        "mem": jax.random.normal(ks[1], (BATCH, MEM_LEN, D_MODEL), f32),
        "norm_g": 1.0 + 0.05 * jax.random.normal(ks[2], (DEPTH, N_NORMS, D_MODEL), f32),
        "ffn1_w_in": _w(ks[3], (DEPTH, D_MODEL, 2 * D_FF), D_MODEL),
        "ffn1_w_out": _w(ks[4], (DEPTH, D_FF, D_MODEL), D_FF),
        "ffn2_w_in": _w(ks[5], (DEPTH, D_MODEL, 2 * D_FF), D_MODEL),
        "ffn2_w_out": _w(ks[6], (DEPTH, D_FF, D_MODEL), D_FF),
        "xattn_w_q": _w(ks[7], (DEPTH, D_MODEL, D_MODEL), D_MODEL),
        "xattn_w_kv": _w(ks[8], (DEPTH, D_MODEL, 2 * D_MODEL), D_MODEL),
        "xattn_w_o": _w(ks[9], (DEPTH, D_MODEL, D_MODEL), D_MODEL),
        "ab_w_in": _w(ks[10], (N_EVEN, D_MODEL, AB_IN), D_MODEL),
        "ab_sink": 0.5 * jax.random.normal(ks[11], (N_EVEN, A_HEADS), f32),
        "ab_sgu_w": _w(ks[12], (N_EVEN, B_GROUPS, SGU_LEN, SGU_LEN), SGU_LEN),
        "ab_sgu_b": 1.0 + 0.01 * jax.random.normal(ks[13], (N_EVEN, B_GROUPS, SGU_LEN), f32),
        "ab_sgu_norm_g": 1.0 + 0.05 * jax.random.normal(ks[14], (N_EVEN, B_WIDTH), f32),
        "ab_w_out": _w(ks[15], (N_EVEN, AB_OUT, D_MODEL), AB_OUT),
        "c_w_in": _w(ks[16], (N_ODD, D_MODEL, C_IN), D_MODEL),
        "c_gate_w": _w(ks[17], (N_ODD, GATE_RANK, C_KEY_DIM), GATE_RANK),
        "c_gate_b": 0.1 * jax.random.normal(ks[18], (N_ODD, C_KEY_DIM), f32),
        "c_head_norm_g": 1.0 + 0.05 * jax.random.normal(ks[19], (N_ODD, C_VAL_DIM), f32),
        "c_w_out": _w(ks[20], (N_ODD, C_VAL_DIM, D_MODEL), C_VAL_DIM),
    }

def reference(x, mem, norm_g, ffn1_w_in, ffn1_w_out, ffn2_w_in, ffn2_w_out,
              xattn_w_q, xattn_w_kv, xattn_w_o,
              ab_w_in, ab_sink, ab_sgu_w, ab_sgu_b, ab_sgu_norm_g, ab_w_out,
              c_w_in, c_gate_w, c_gate_b, c_head_norm_g, c_w_out):
    for i in range(DEPTH):
        g = norm_g[i]
        x = x + 0.5 * rmsnorm(swiglu(rmsnorm(x, g[0]), ffn1_w_in[i], ffn1_w_out[i]), g[1])
        h = rmsnorm(x, g[2])
        j = i // 2
        if i % 2 == 0:
            y = mixer_ab(h, ab_w_in[j], ab_sink[j], ab_sgu_w[j], ab_sgu_b[j], ab_sgu_norm_g[j], ab_w_out[j])
        else:
            y = gated_linear_attention(h, c_w_in[j], c_gate_w[j], c_gate_b[j], c_head_norm_g[j], c_w_out[j])
        x = x + rmsnorm(y, g[3])
        mem_n = rmsnorm(mem, g[4])
        x = x + rmsnorm(memory_cross_attention(rmsnorm(x, g[5]), mem_n,
                                               xattn_w_q[i], xattn_w_kv[i], xattn_w_o[i]), g[6])
        x = x + 0.5 * rmsnorm(swiglu(rmsnorm(x, g[7]), ffn2_w_in[i], ffn2_w_out[i]), g[8])
    return x


_drawn_inputs = setup_inputs


def setup_inputs(seed=0):
    import zlib

    import numpy as np

    out = dict(_drawn_inputs(seed))
    spreads = {}
    factors = {}
    for name, (base, spread) in spreads.items():
        noise = np.random.default_rng([zlib.crc32(name.encode()), seed]).standard_normal(out[name].shape)
        drawn = base * np.exp(spread * noise) if base else spread * noise
        out[name] = __import__('jax').numpy.asarray(drawn.astype(out[name].dtype))
    for name, factor in factors.items():
        out[name] = (out[name] * factor).astype(out[name].dtype)
    return out
```

```python
from contextlib import ExitStack

import numpy as np

import concourse.bass as bass
from concourse import mybir

F32 = mybir.dt.float32
F32R = mybir.dt.float32r
BF16 = mybir.dt.bfloat16
U32 = mybir.dt.uint32
ALU = mybir.AluOpType
ACT = mybir.ActivationFunctionType
AX = mybir.AxisListType

P = 128
D = 1024
KT = D // P
T = 512
TT = T // P
MEM = 256
MT = MEM // P
FF = 4 * D
FC = FF // P
LAYERS = 2
NORMS = 9
EPS = 1e-6
CHUNK = 64
NCH = T // CHUNK
UNIT = 2048
RING = 4
RAW = 2
AHEAD = 2
A_HEADS, A_DIM = 8, 64
AB_WIDTH = 512
SGU_GROUPS = 4
G_HEADS, G_DK, G_DV = 4, 128, 256
G_RANK = 16
X_HEADS = 4
NEG = -1e30
CREDIT = RING
GAIN_ROWS = LAYERS * NORMS * KT + SGU_GROUPS + KT

C_ID, C_CUM, C_END, C_MASK, C_BIAS0, C_BIAS = 0, 128, 256, 384, 512, 1024
C_ALL = 1536


def constant_table():
    c = np.zeros((P, C_ALL), np.float32)
    row, col = np.arange(P)[:, None], np.arange(P)[None, :]
    same = row // CHUNK == col // CHUNK
    c[:, C_ID:C_ID + P] = row == col
    c[:, C_CUM:C_CUM + P] = (same & (row <= col)) / 16.0
    c[:, C_END:C_END + P] = (same & (row > col)) / 16.0
    c[:, C_MASK:C_MASK + P] = same & (row <= col)
    slopes = (2.0 ** (-8.0 * np.arange(1, A_HEADS + 1) / A_HEADS)).astype(np.float32)
    q = np.arange(P) % CHUNK
    for kv in range(2):
        for pair in range(2):
            group = 2 * kv + pair
            head = 4 * kv + 2 * pair + np.arange(P) // CHUNK
            dist = np.abs(q[:, None] + CHUNK - np.arange(P)[None, :]).astype(np.float32)
            c[:, C_BIAS + group * P:C_BIAS + (group + 1) * P] = -slopes[head][:, None] * dist
            first = np.abs(q[:, None] - np.arange(P)[None, :]).astype(np.float32)
            bias = np.where(np.arange(P)[None, :] < CHUNK, -slopes[head][:, None] * first, NEG)
            c[:, C_BIAS0 + group * P:C_BIAS0 + (group + 1) * P] = bias
    return c


class Phase:

    def __init__(self, name, unit, norm_in, norm_out, layer, index, nth):
        self.name, self.unit, self.norm_in, self.norm_out = name, unit, norm_in, norm_out
        self.layer, self.index = layer, index
        self.tile = TT * index
        self.nth = nth


def trunk_kernel(nc, x_in, mem_in, norm_g, f1_in, f1_out, f2_in, f2_out, xq_w, xkv_w, xo_w,
                 ab_in, ab_sink, sgu_w, sgu_b, sgu_g, ab_out, c_in, c_gate_w, c_gate_b,
                 c_head_g, c_out, constants, out, stop=None):
    phases = []
    unit = LAYERS * 8
    for layer in range(LAYERS):
        mixer = ("ab", 7 + 4) if layer % 2 == 0 else ("gla", 12 + 4)
        for name, n, pre, post in (("ffn", 48, 0, 1), (*mixer, 2, 3), ("xattn", 8, 5, 6),
                                   ("ffn", 48, 7, 8)):
            nth = sum(ph.name == name for ph in phases)
            phases.append(Phase(name, unit, pre, post, layer, len(phases), nth))
            unit += n
    phases = phases[:stop]
    if stop is not None and stop < 8:
        unit = phases[-1].unit + {"ffn": 48, "ab": 11, "gla": 16, "xattn": 8}[phases[-1].name]
    UNITS = unit
    LAST = len(phases) - 1

    with ExitStack() as ctx:
        def sb(name, shape, dt=F32):
            return ctx.enter_context(nc.sbuf_tensor(name, shape, dt))

        def sem(name):
            return ctx.enter_context(nc.semaphore(name))

        x_res = sb("x_res", [P, TT, D])
        operand_high = sb("operand_high", [P, KT, T], F32R)
        operand_low = sb("operand_low", [P, KT, T], F32R)
        hidden = sb("hidden", [P, FC, T])
        raw_weights = sb("raw_weights", [P, RAW, UNIT])
        high_weights = sb("high_weights", [P, RING, UNIT], F32R)
        low_weights = sb("low_weights", [P, RING, UNIT], F32R)
        post_gain = sb("post_gain", [P, D])
        silu_buf = sb("silu_buf", [P, D])
        square_junk = sb("square_junk", [P, D], BF16)
        identity = sb("identity", [P, P])
        gain_cols = sb("gain_cols", [P, GAIN_ROWS])
        stats = sb("stats", [P, 128])
        ss_y, ss_x = stats[:, 0:4], stats[:, 4:8]
        rstd_y, rstd_x, neg_half = stats[:, 12:16], stats[:, 16:20], stats[:, 20:24]
        credit = sb("credit", [P, 2 * CREDIT])
        small = stats[:, 24:128]
        banks = ctx.enter_context(nc.psum_tensor("banks", [P, 8, T], F32))
        silu = silu_buf[:].rearrange("p (b n) -> p b n", b=2)

        flat = hidden[:].rearrange("p c n -> p (c n)")
        scaled = flat[:, 0:TT * D].rearrange("p (t n) -> p t n", t=TT)

        def parts(start, *sizes):
            found = []
            for size in sizes:
                n = size if isinstance(size, int) else size[0] * size[1]
                a = flat[:, start:start + n]
                found.append(a if isinstance(size, int) else a.rearrange("p (a b) -> p a b", a=size[0]))
                start += n
            assert start <= FC * T, start
            return found

        mem_nat, mem_scaled = parts(0, (MT, D), (MT, D))
        gain_rows, *mem_kv = parts(2 * MT * D, (2, P), *[KT * MEM] * (2 * LAYERS))
        (qT, uT, vg, kT, v_win, probs0, probs1, probsT0, probsT1, bias_tab, sgu_raw, sguT, sgu_bias,
         yb, sink) = parts(0, (4, T), (4, T), (TT, T), T, (7, P), (4, P), (4, P), T, T, (2, T),
                           (4, P), (4, P), (4, P), (4, T), 4)
        probs, probsT = (probs0, probs1), (probsT0, probsT1)
        (gq, gk, gr, gv, loga, exp0, exp1, exp2, gmask, gcum, gend, decay) = parts(
            0, (G_HEADS, T), (G_HEADS, T), (KT, T), (TT, D), (TT, T), T, T, T, P, P, P,
            (G_HEADS, NCH))
        exps = (exp0, exp1, exp2)
        gate_raw = silu_buf[:, 0:KT * G_RANK].rearrange("p (k n) -> p k n", k=KT)
        gate_w = silu_buf[:, P:P + T]
        g_nat, gT, z_tmp = exp1.rearrange("p (t n) -> p t n", t=TT), exp0, (exp2, exp1)
        states = silu_buf[:].rearrange("p (s n) -> p s n", s=4)
        att = (exp0, exp1)
        o_nat = exp2.rearrange("p (b n) -> p b n", b=2)
        xq, xk, xv, xp0, xp1, xpT = parts(0, (KT, T), (KT, MEM), (MT, D), (X_HEADS, MEM),
                                          (X_HEADS, MEM), (KT, T))
        xp = (xp0, xp1)

        key_store = nc.dram_tensor("key_store", (LAYERS, P, KT * MEM), F32, kind="Internal").ap()
        value_store = nc.dram_tensor("value_store", (LAYERS, P, MT * D), F32, kind="Internal").ap()

        raw_landed = [sem(f"raw_landed{i}") for i in range(RAW)]
        high_done, low_done, unit_used = sem("high_done"), sem("low_done"), sem("unit_used")
        x_loaded, mem_loaded, table_loaded, out_stored = (
            sem("x_loaded"), sem("mem_loaded"), sem("table_loaded"), sem("out_stored"))
        half_set = sem("half_set")
        gains_turned, gains_ready = sem("gains_turned"), sem("gains_ready")
        mem_sq, mem_rstd, mem_scaled_done, mem_turned = (
            sem("mem_sq"), sem("mem_rstd"), sem("mem_scaled_done"), sem("mem_turned"))
        mem_high, mem_low, mem_evac, kv_stored = (
            sem("mem_high"), sem("mem_low"), sem("mem_evac"), sem("kv_stored"))
        pool_step, dve_step, act_step = sem("pool_step"), sem("dve_step"), sem("act_step")
        steps = {"pool": 0, "dve": 0, "act": 0}
        y_done, y_sq, y_rstd, x_new, gain_loaded = (
            sem("y_done"), sem("y_sq"), sem("y_rstd"), sem("x_new"), sem("gain_loaded"))
        x_sq, x_rstd, x_scaled, x_turned, x_high, x_low = (
            sem("x_sq"), sem("x_rstd"), sem("x_scaled"), sem("x_turned"), sem("x_high"), sem("x_low"))
        gate_done, silu_done, hidden_done, act_high, act_low = (
            sem("gate_done"), sem("silu_done"), sem("hidden_done"), sem("act_high"),
            sem("act_low"))
        AB = {n: sem("ab_" + n) for n in (
            "in_evac", "tables", "masked", "stat_done", "ln_rstd", "ln_done", "sguT_psum",
            "sguT_ready", "mixed", "yb_done", "yb_high", "scores", "shifted", "exped",
            "normed", "p_turned", "p_evac", "attended", "out_high", "out_low")}
        GL = {n: sem("gla_" + n) for n in (
            "in_evac", "tables", "cleared", "g_done", "g_copied", "g_turned", "gT_ready",
            "z_done", "z_copied", "z_abs", "z_log", "log_ready", "cum_done", "exp_done", "dec_done",
            "kend_made", "kend_turned", "kend_ready", "att_done", "att_ready", "kv_done", "state_ready", "o_done",
            "o_sq", "o_rstd", "o_scaled", "o_turned", "y_ready", "out_high", "out_low")}
        XA = {n: sem("x_att_" + n) for n in (
            "kv_loaded", "in_evac", "scores", "maxed", "exped", "normed", "p_turned",
            "p_evac", "attended", "out_high", "out_low")}
        block = ctx.enter_context(nc.Block())

        in_pieces = {ph.unit + i for ph in phases if ph.name == "ab" for i in (0, 1, 7, 8)}

        def landed(u):
            return sum(64 if v in in_pieces else 32 for v in range(u % RAW, u + 1, RAW))

        AB_TABLES = 16 * (2 + 1 + SGU_GROUPS + A_HEADS)

        def gain_col(layer, norm, kt):
            c = (layer * NORMS + norm) * KT + kt
            return gain_cols[:, c:c + 1]

        def sgu_gain(g):
            c = LAYERS * NORMS * KT + g
            return gain_cols[:, c:c + 1]

        def head_gain(c):
            c += LAYERS * NORMS * KT + SGU_GROUPS
            return gain_cols[:, c:c + 1]

        def token_banks(tt):
            return banks[:, 2 * tt:2 * tt + 2, :].rearrange("p b n -> p (b n)")

        @block.sync
        def _(sp):
            sp.dma_start(mem_nat, mem_in[0].rearrange("(t p) n -> p t n", p=P)).then_inc(mem_loaded, 16)
            sp.dma_start(identity[:], constants[:, C_ID:C_ID + P]).then_inc(table_loaded, 16)
            rows = norm_g.rearrange("l k (c p) -> (l k c) p", p=P)
            n = LAYERS * NORMS * KT
            sp.dma_start(gain_rows[:, 0, :], rows[0:P, :]).then_inc(table_loaded, 16)
            sp.dma_start(gain_rows[0:n - P, 1, :], rows[P:n, :]).then_inc(table_loaded, 16)
            sp.dma_start(gain_rows[n - P:n - P + SGU_GROUPS, 1, :],
                         sgu_g[0].rearrange("(g p) -> g p", p=P)).then_inc(table_loaded, 16)
            sp.dma_start(gain_rows[n - P + SGU_GROUPS:GAIN_ROWS - P, 1, :],
                         c_head_g[0].rearrange("(g p) -> g p", p=P)).then_inc(table_loaded, 16)

            def load(u, first, second, more=0):
                if u >= RAW:
                    sp.wait_ge(low_done, u - RAW + 1 + more)
                slot = raw_weights[:, u % RAW, :]
                for (dst, src) in (first(slot), second(slot)):
                    sp.dma_start(dst, src).then_inc(raw_landed[u % RAW], 16)

            def columns(u, w, c0):
                src = w.rearrange("(k p) n -> p k n", p=P)[:, :, c0:c0 + 2 * P]
                h = KT // 2
                grid = lambda slot: slot.rearrange("p (k n) -> p k n", k=KT)
                load(u, lambda s: (grid(s)[:, 0:h, :], src[:, 0:h, :]),
                     lambda s: (grid(s)[:, h:KT, :], src[:, h:KT, :]))

            def rows_of(u, w, r0, more=0, step=0):
                def half(k):
                    start = r0 + k * P + step
                    src = w[start:start + P, :] if isinstance(start, int) else w[bass.ds(start, P), :]
                    return lambda s: (s[:, k * D:(k + 1) * D], src)
                load(u, half(0), half(1), more)

            for layer in range(LAYERS):
                for i in range(8):
                    columns(8 * layer + i, xkv_w[layer], 256 * i)
                    if layer == 0 and i == 1:
                        sp.dma_start(x_res[:], x_in[0].rearrange("(t p) n -> p t n", p=P))\
                          .then_inc(x_loaded, 16)
            for ph in phases:
                u = ph.unit
                if ph.name == "ffn":
                    w_in, w_out = ((f1_in, f1_out), (f2_in, f2_out))[ph.nth % 2]
                    src = w_in[ph.layer].rearrange("(k p) (two n) -> p k two n", p=P, two=2)
                    grid = lambda slot, h: slot.rearrange("p (h k n) -> p h k n", h=2, k=KT)[:, h]
                    with sp.Fori(0, FC // RING) as it:
                        for k in range(RING):
                            c = it * (RING * P) + k * P
                            load(u + k, lambda s: (grid(s, 0), src[:, :, 0, bass.ds(c, P)]),
                                 lambda s: (grid(s, 1), src[:, :, 1, bass.ds(c, P)]), it * RING)
                    u += FC
                    with sp.Fori(0, FC // 2 // RING) as it:
                        for k in range(RING):
                            rows_of(u + k, w_out[ph.layer], 2 * P * k, it * RING, it * (RING * 2 * P))
                elif ph.name == "ab":
                    w = ab_in[0].rearrange("(k p) n -> p k n", p=P)
                    for i in range(2):
                        sp.wait_ge(low_done, u + i - RAW + 1)
                        slot = raw_weights[:, (u + i) % RAW, :].rearrange("p (k h n) -> p k h n", k=KT, h=4)
                        for h in range(2):
                            for kv in range(2):
                                c = (4 * kv + 2 * i + h) * A_DIM
                                sp.dma_start(slot[:, :, 2 * h + kv, :], w[:, :, c:c + A_DIM])\
                                  .then_inc(raw_landed[(u + i) % RAW], 16)
                    for i in range(2, 7):
                        columns(u + i, ab_in[0], 256 * i)
                    for i in range(2):
                        v = u + 7 + i
                        sp.wait_ge(low_done, v - RAW + 1)
                        for k in range(2):
                            for kv in range(2):
                                r = (4 * kv + 2 * i + k) * A_DIM
                                sp.dma_start(raw_weights[kv * A_DIM:(kv + 1) * A_DIM, v % RAW, k * D:(k + 1) * D],
                                             ab_out[0][r:r + A_DIM, :]).then_inc(raw_landed[v % RAW], 16)
                    for i in range(2, 4):
                        rows_of(u + 7 + i, ab_out[0], 256 * i)
                elif ph.name == "gla":
                    for i in range(12):
                        columns(u + i, c_in[0], 256 * i)
                    for i in range(4):
                        rows_of(u + 12 + i, c_out[0], 256 * i)
                else:
                    for i in range(4):
                        columns(u + i, xq_w[ph.layer], 256 * i)
                    for i in range(4):
                        rows_of(u + 4 + i, xo_w[ph.layer], 256 * i)
            for tt in range(TT):
                sp.wait_ge(x_new, phases[-1].tile + tt + 1)
                sp.dma_start(out[0, tt * P:(tt + 1) * P, :], x_res[:, tt, :]).then_inc(out_stored, 16)
            sp.wait_ge(out_stored, 16 * TT)

        @block.gpsimd
        def _(pool):
            def rsqrt(rstd, ss, count, done, quarter=1.0):
                pool.tensor_scalar(rstd, ss, quarter / count, quarter * EPS,
                                   ALU.mult, ALU.add).then_inc(pool_step, 1)
                steps["pool"] += 1
                pool.wait_ge(pool_step, steps["pool"])
                pool.tensor_tensor(rstd, rstd, neg_half[:, 0:rstd.shape[1]],
                                   ALU.pow).then_inc(done, 1)

            pool.memset(neg_half, -0.5).then_inc(half_set, 1)
            pool.wait_ge(half_set, 1)

            pool.wait_ge(mem_sq, MT)
            rsqrt(small[:, 0:MT], ss_y[:, 0:MT], D, mem_rstd)

            def x_norm(base):
                for tt in range(TT):
                    pool.wait_ge(x_sq, base + tt + 1)
                    rsqrt(rstd_x[:, tt:tt + 1], ss_x[:, tt:tt + 1], D, x_rstd)

            x_norm(0)
            for i in range(2 * LAYERS):
                pool.wait_ge(mem_evac, 4 * (i + 1))
                store = (key_store, value_store)[i % 2]
                pool.dma_start(store[i // 2], mem_kv[i]).then_inc(kv_stored, 16)

            for ph in phases:
                if ph.index:
                    pool.wait_ge(x_new, ph.tile)
                row = norm_g[ph.layer, ph.norm_out:ph.norm_out + 1, :]
                pool.dma_start(post_gain[:], row.broadcast_to([P, D])).then_inc(gain_loaded, 16)
                if ph.name == "ab":
                    for t, c in ((0, C_BIAS0), (1, C_BIAS)):
                        pool.dma_start(bias_tab[:, t, :], constants[:, c:c + T]).then_inc(AB["tables"], 16)
                    pool.dma_start(sgu_raw, sgu_w[0].rearrange("g i j -> i g j")).then_inc(AB["tables"], 16)
                    for g in range(SGU_GROUPS):
                        pool.dma_start(sgu_bias[:, g, :], sgu_b[0, g:g + 1, :].broadcast_to([P, P]))\
                            .then_inc(AB["tables"], 16)
                    for kv in range(2):
                        for pair in range(2):
                            for e in range(2):
                                head = 4 * kv + 2 * pair + e
                                pool.dma_start(sink[e * 64:(e + 1) * 64, 2 * kv + pair:2 * kv + pair + 1],
                                               ab_sink[0:1, head:head + 1].broadcast_to([64, 1]))\
                                    .then_inc(AB["tables"], 16)
                    pool.wait_ge(AB["stat_done"], 1)
                    rsqrt(small[:, 12:16], small[:, 8:12], 1.0, AB["ln_rstd"])
                elif ph.name == "gla":
                    for dst, c in ((gmask, C_MASK), (gcum, C_CUM), (gend, C_END)):
                        pool.dma_start(dst, constants[:, c:c + P]).then_inc(GL["tables"], 16)
                    pool.dma_start(gate_raw, c_in[0].rearrange("(k p) n -> p k n", p=P)
                                   [:, :, 3072:3072 + G_RANK]).then_inc(GL["tables"], 16)
                    pool.dma_start(gate_w[0:G_RANK, :], c_gate_w[0]).then_inc(GL["tables"], 16)
                    pool.dma_start(gate_w[G_RANK:G_RANK + 1, :], c_gate_b[0:1, :]).then_inc(GL["tables"], 16)
                    for h in range(G_HEADS):
                        pool.wait_ge(GL["o_sq"], TT * (h + 1))
                        rsqrt(small[:, 4 * (h % 2):4 * (h % 2) + 4], small[:, 8 + 4 * (h % 2):12 + 4 * (h % 2)],
                              G_DV, GL["o_rstd"])
                elif ph.name == "xattn":
                    if ph.nth == 0:
                        pool.wait_ge(kv_stored, 16 * 2 * LAYERS)
                    pool.dma_start(xk.rearrange("p a b -> p (a b)"), key_store[ph.layer]).then_inc(XA["kv_loaded"], 16)
                    pool.dma_start(xv.rearrange("p a b -> p (a b)"), value_store[ph.layer]).then_inc(XA["kv_loaded"], 16)
                for tt in range(TT):
                    pool.wait_ge(y_sq, ph.tile + tt + 1)
                    rsqrt(rstd_y[:, tt:tt + 1], ss_y[:, tt:tt + 1], D, y_rstd,
                          4.0 if ph.name == "ffn" else 1.0)
                    if ph.index < LAST:
                        pool.wait_ge(x_sq, ph.tile + TT + tt + 1)
                        rsqrt(rstd_x[:, tt:tt + 1], ss_x[:, tt:tt + 1], D, x_rstd)

        @block.scalar
        def _(act):
            def split_high(u, more=0):
                if isinstance(more, int) and u >= UNITS:
                    return
                act.wait_ge(raw_landed[u % RAW], landed(u) + 16 * more)
                if u >= RING:
                    act.wait_ge(unit_used, u - RING + 1 + more)
                act.activation(high_weights[:, u % RING, :], raw_weights[:, u % RAW, :], ACT.Copy)\
                   .then_inc(high_done, 1)

            def square_x(base, tt):
                act.activation(square_junk[:], x_res[:, tt, :], ACT.Square,
                               accum_out=ss_x[:, tt:tt + 1]).then_inc(x_sq, 1)

            def operand_high_of(ph, tt):
                act.wait_ge(x_turned, ph.tile + tt + 1)
                for kt in range(KT):
                    last = act.activation(operand_high[:, kt, tt * P:(tt + 1) * P],
                                          token_banks(tt)[:, kt * P:(kt + 1) * P], ACT.Copy,
                                          scale=gain_col(ph.layer, ph.norm_in, kt))
                last.then_inc(x_high, 1)

            def boundary(ph):
                nxt = phases[ph.index + 1] if ph.index < LAST else None
                for tt in range(TT):
                    act.wait_ge(y_done, ph.tile + tt + 1)
                    if nxt and tt:
                        act.wait_ge(x_sq, nxt.tile + tt)
                    elif tt:
                        act.wait_ge(y_sq, ph.tile + tt)
                    act.activation(square_junk[:], token_banks(tt), ACT.Square,
                                   accum_out=ss_y[:, tt:tt + 1]).then_inc(y_sq, 1)
                    if nxt and tt >= 2:
                        operand_high_of(nxt, tt - 2)
                    if nxt:
                        act.wait_ge(x_new, ph.tile + tt + 1)
                        square_x(nxt.tile, tt)
                if nxt:
                    operand_high_of(nxt, TT - 2)
                    operand_high_of(nxt, TT - 1)

            act.wait_ge(table_loaded, 80)
            for k in range(CREDIT):
                act.activation(credit[:, k:k + 1], identity[:, k:k + 1], ACT.Copy).then_inc(silu_done, 1)
            act.wait_ge(mem_loaded, 16)
            for mt in range(MT):
                if mt:
                    act.wait_ge(mem_sq, mt)
                act.activation(square_junk[:], mem_nat[:, mt, :], ACT.Square,
                               accum_out=ss_y[:, mt:mt + 1]).then_inc(mem_sq, 1)
            act.wait_ge(gains_turned, 1)
            act.activation(gain_cols[:], banks[:, 7, 0:GAIN_ROWS], ACT.Copy).then_inc(gains_ready, 1)
            act.wait_ge(gains_ready, 1)
            for mt in range(MT):
                act.wait_ge(mem_turned, mt + 1)
                for layer in range(LAYERS):
                    for kt in range(KT):
                        c = layer * MEM + mt * P
                        last = act.activation(operand_high[:, kt, c:c + P],
                                              token_banks(mt)[:, kt * P:(kt + 1) * P], ACT.Copy,
                                              scale=gain_col(layer, 4, kt))
                last.then_inc(mem_high, 1)
            for u in range(AHEAD):
                split_high(u)
            act.wait_ge(x_loaded, 16)
            act.wait_ge(mem_sq, MT)
            for tt in range(TT):
                if tt:
                    act.wait_ge(x_sq, tt)
                square_x(0, tt)
            for u in range(8 * LAYERS):
                split_high(u + AHEAD)
                act.wait_ge(unit_used, u + 1)
                i, half = divmod(u, 4)
                src = banks[:, u % 4, :].rearrange("p (a n) -> p a n", a=2)
                if i % 2 == 0:
                    dst = mem_kv[i].rearrange("p (a n) -> p a n", a=KT)[:, 2 * half:2 * half + 2, :]
                else:
                    dst = mem_kv[i].rearrange("p (a n) -> p a n", a=MT)[:, :, half * MEM:(half + 1) * MEM]
                act.activation(dst, src, ACT.Copy).then_inc(mem_evac, 1)
            for tt in range(TT):
                operand_high_of(phases[0], tt)

            def ffn(ph):
                n0, u = ph.nth * FC, ph.unit
                with act.Fori(0, FC // RING) as it:
                    for k in range(RING):
                        split_high(u + k + AHEAD, it * RING)
                        act.wait_ge(gate_done, n0 + k + 1 + it * RING)
                        act.wait_ge(hidden_done, CREDIT + n0 + k - 1 + it * RING)
                        act.activation(silu[:, k % 2, :], banks[:, 2 * k, :], ACT.Silu)\
                           .then_inc(silu_done, 1)
                u += FC
                def pair(k, more=0):
                    if isinstance(more, int):
                        src = hidden[:, 2 * (k + more):2 * (k + more) + 2, :]
                    else:
                        src = hidden[:, bass.ds(more * 2 + 2 * k, 2), :]
                    act.activation(operand_high[:, 2 * (k % 4):2 * (k % 4) + 2, :], src, ACT.Copy)\
                       .then_inc(act_high, 1)
                act.wait_ge(unit_used, u)
                act.wait_ge(hidden_done, CREDIT + n0 + FC)
                for k in range(AHEAD):
                    pair(k)
                with act.Fori(0, FC // 2 // RING - 1) as it:
                    for k in range(RING):
                        split_high(u + k + AHEAD, it * RING)
                        act.wait_ge(unit_used, u + k + AHEAD - RING + 1 + it * RING)
                        pair(k + AHEAD, it * RING)
                for v in range(FC // 2 - RING, FC // 2):
                    split_high(u + v + AHEAD)
                    if v + AHEAD < FC // 2:
                        act.wait_ge(unit_used, u + v + AHEAD - RING + 1)
                        pair(v + AHEAD)

            def inputs(ph, count, evac, evacuate):
                for v in range(count):
                    split_high(ph.unit + v + AHEAD)
                    act.wait_ge(unit_used, ph.unit + v + 1)
                    evacuate(v, evac)

            def outputs(ph, start):
                for v in range(start, start + 4):
                    split_high(ph.unit + v + AHEAD)

            def pair_of_banks(b):
                return banks[:, 2 * b:2 * b + 2, :]

            def window(ph):
                def evacuate(v, evac):
                    if v < 2:
                        act.activation(qT.rearrange("p a b -> p (a b)").rearrange(
                                           "p (c j n) -> p j c n", c=NCH, j=4)[:, 2 * v:2 * v + 2, :, :],
                                       pair_of_banks(v).rearrange("p j (c n) -> p j c n", c=NCH),
                                       ACT.Copy).then_inc(evac, 1)
                    elif v == 2:
                        act.activation(kT, banks[:, 4, :], ACT.Copy)
                        act.activation(v_win.rearrange("p a b -> p (a b)")[:, 0:T], banks[:, 5, :], ACT.Copy)
                        act.activation(v_win.rearrange("p a b -> p (a b)")[:, T:7 * P],
                                       banks[:, 6, 0:3 * P], ACT.Copy).then_inc(evac, 1)
                    elif v < 5:
                        act.activation(uT[:, 2 * v - 6:2 * v - 4, :], pair_of_banks(v - 3), ACT.Copy).then_inc(evac, 1)
                    else:
                        act.activation(vg[:, :, (v - 5) * 256:(v - 4) * 256],
                                       pair_of_banks(v - 3).rearrange("p b (t n) -> p (b t) n", n=256),
                                       ACT.Copy).then_inc(evac, 1)
                inputs(ph, 7, AB["in_evac"], evacuate)
                act.wait_ge(AB["sguT_psum"], 1)
                act.activation(sguT.rearrange("p a b -> p (a b)"), banks[:, 6, :], ACT.Copy)\
                   .then_inc(AB["sguT_ready"], 1)
                for g in range(SGU_GROUPS):
                    act.wait_ge(AB["yb_done"], g + 1)
                    act.activation(operand_high[:, 4 + g, :], yb[:, g, :], ACT.Copy).then_inc(AB["yb_high"], 1)
                for c in range(NCH):
                    b = c % 2
                    act.wait_ge(AB["shifted"], c + 1)
                    neg_max, sink_gap, total, sink_exp = (
                        small[:, 32 + 16 * b + 4 * i:36 + 16 * b + 4 * i] for i in range(4))
                    act.activation(sink_exp, sink_gap, ACT.Exp)
                    for g in range(4):
                        last = act.activation(probs[b][:, g, :], probs[b][:, g, :], ACT.Exp,
                                              bias=neg_max[:, g:g + 1], accum_out=total[:, g:g + 1])
                    last.then_inc(AB["exped"], 1)
                    act.wait_ge(AB["p_turned"], c + 1)
                    act.activation(probsT[b], banks[:, 4 + b, :], ACT.Copy).then_inc(AB["p_evac"], 1)
                    if c:
                        attended(c - 1)
                attended(NCH - 1)
                outputs(ph, 7)

            def attended(c):
                    b = c % 2
                    act.wait_ge(AB["attended"], c + 1)
                    for kv in range(2):
                        rows = slice(kv * 64, kv * 64 + 64)
                        last = act.activation(
                            operand_high[rows, 0:4, c * CHUNK:(c + 1) * CHUNK],
                            banks[rows, 6 + b, kv * 256:(kv + 1) * 256].rearrange("p (j q) -> p j q", j=4),
                            ACT.Copy)
                    last.then_inc(AB["out_high"], 1)

            def gated(ph):
                def evacuate(v, evac):
                    src = pair_of_banks(v % 4)
                    if v < 4:
                        dst = (gq, gk)[v // 2][:, 2 * (v % 2):2 * (v % 2) + 2, :]
                        act.activation(dst, src, ACT.Copy).then_inc(evac, 1)
                    elif v < 8:
                        act.activation(gv[:, :, (v - 4) * 256:(v - 3) * 256],
                                       src.rearrange("p b (t n) -> p (b t) n", n=256), ACT.Copy).then_inc(evac, 1)
                    else:
                        act.activation(gr[:, 2 * v - 16:2 * v - 14, :], src, ACT.Silu).then_inc(evac, 1)
                inputs(ph, 12, GL["in_evac"], evacuate)
                act.wait_ge(GL["g_done"], 1)
                act.wait_ge(GL["cleared"], 1)
                act.activation(g_nat[:, :, 0:G_RANK],
                               banks[:, 0, 0:TT * G_RANK].rearrange("p (t n) -> p t n", t=TT), ACT.Copy)\
                   .then_inc(GL["g_copied"], 1)
                act.wait_ge(GL["g_turned"], 1)
                act.activation(gT, banks[:, 1, :], ACT.Copy).then_inc(GL["gT_ready"], 1)
                for tt in range(TT):
                    act.wait_ge(GL["z_done"], tt + 1)
                    act.activation(loga[:, tt, :], banks[:, 2 + tt, :], ACT.Copy).then_inc(GL["z_copied"], 1)
                for tt in range(TT):
                    act.wait_ge(GL["z_abs"], tt + 1)
                    act.activation(z_tmp[tt % 2], z_tmp[tt % 2], ACT.Exp, scale=-1.0).then_inc(act_step, 1)
                    steps["act"] += 1
                    act.wait_ge(act_step, steps["act"])
                    act.activation(z_tmp[tt % 2], z_tmp[tt % 2], ACT.Ln, bias=1.0).then_inc(GL["z_log"], 1)
                for h in range(G_HEADS):
                    act.wait_ge(GL["cum_done"], h + 1)
                    if h:
                        act.wait_ge(GL["kend_turned"], h)
                        act.wait_ge(GL["dec_done"], h)
                    act.activation(exps[0], banks[:, 0, :], ACT.Exp)
                    act.activation(exps[1], banks[:, 0, :], ACT.Exp, scale=-1.0)
                    act.activation(exps[2], banks[:, 1, :], ACT.Exp).then_inc(GL["exp_done"], 1)
                    act.wait_ge(GL["kend_turned"], h + 1)
                    act.activation(loga[:, :, h * P:(h + 1) * P],
                                   banks[:, 2, :].rearrange("p (t n) -> p t n", t=TT), ACT.Copy)\
                       .then_inc(GL["kend_ready"], 1)
                for h in range(G_HEADS):
                    for tt in range(TT):
                        act.wait_ge(GL["o_done"], h * TT + tt // 2 * 2 + 2)
                        if h + tt:
                            act.wait_ge(GL["o_sq"], h * TT + tt)
                        ss = small[:, 8 + 4 * (h % 2) + tt:9 + 4 * (h % 2) + tt]
                        act.activation(square_junk[:, 0:G_DV], banks[:, 6 + tt // 2, 256 * (tt % 2):256 * (tt % 2) + 256],
                                       ACT.Square, accum_out=ss).then_inc(GL["o_sq"], 1)
                    for j in range(2):
                        c = 2 * h + j
                        act.wait_ge(GL["y_ready"], c + 1)
                        act.activation(operand_high[:, c, :], gr[:, c, :], ACT.Copy).then_inc(GL["out_high"], 1)
                outputs(ph, 12)

            def cross(ph):
                base = 4 * ph.nth
                def evacuate(v, evac):
                    act.activation(xq[:, 2 * v:2 * v + 2, :], pair_of_banks(v), ACT.Copy).then_inc(evac, 1)
                for v in range(4):
                    split_high(ph.unit + v + AHEAD)
                    act.wait_ge(unit_used, ph.unit + v + 1)
                    evacuate(v, XA["in_evac"])
                for tt in range(TT):
                    b = tt % 2
                    neg_max, total = small[:, 8 * b:8 * b + 4], small[:, 8 * b + 4:8 * b + 8]
                    act.wait_ge(XA["maxed"], base + tt + 1)
                    if base + tt >= 2:
                        act.wait_ge(XA["p_turned"], base + tt - 1)
                    for h in range(X_HEADS):
                        last = act.activation(xp[b][:, h, :], token_banks(tt)[:, h * MEM:(h + 1) * MEM], ACT.Exp,
                                              bias=neg_max[:, h:h + 1], scale=(D // X_HEADS) ** -0.5,
                                              accum_out=total[:, h:h + 1])
                    last.then_inc(XA["exped"], 1)
                    if tt:
                        cross_turned(base, tt - 1)
                cross_turned(base, TT - 1)
                for j in range(KT):
                    act.wait_ge(XA["attended"], 8 * ph.nth + j + 1)
                    act.activation(operand_high[:, j, :], banks[:, j, :], ACT.Copy).then_inc(XA["out_high"], 1)
                outputs(ph, 4)

            def cross_turned(base, tt):
                act.wait_ge(XA["p_turned"], base + tt + 1)
                act.activation(xpT[:, :, tt * P:(tt + 1) * P],
                               token_banks(tt).rearrange("p (a n) -> p a n", a=KT), ACT.Copy)\
                   .then_inc(XA["p_evac"], 1)

            for ph in phases:
                {"ffn": ffn, "ab": window, "gla": gated, "xattn": cross}[ph.name](ph)
                boundary(ph)

        @block.vector
        def _(dve):
            def step(instruction):
                instruction.then_inc(dve_step, 1)
                steps["dve"] += 1
                dve.wait_ge(dve_step, steps["dve"])

            def split_low(u, more=0):
                if isinstance(more, int) and u >= UNITS:
                    return
                dve.wait_ge(high_done, u + 1 + more)
                dve.tensor_tensor(low_weights[:, u % RING, :], raw_weights[:, u % RAW, :],
                                  high_weights[:, u % RING, :].bitcast(F32), ALU.subtract)\
                   .then_inc(low_done, 1)

            def scale_x(ph, tt):
                dve.wait_ge(x_rstd, ph.tile + tt + 1)
                dve.tensor_scalar(scaled[:, tt, :], x_res[:, tt, :], rstd_x[:, tt:tt + 1], None,
                                  ALU.mult).then_inc(x_scaled, 1)

            def operand_low_of(ph, tt):
                dve.wait_ge(x_high, ph.tile + tt + 1)
                for kt in range(KT):
                    cols = slice(tt * P, (tt + 1) * P)
                    last = dve.scalar_tensor_tensor(
                        operand_low[:, kt, cols], token_banks(tt)[:, kt * P:(kt + 1) * P],
                        gain_col(ph.layer, ph.norm_in, kt), operand_high[:, kt, cols].bitcast(F32),
                        ALU.mult, ALU.subtract)
                last.then_inc(x_low, 1)

            def boundary(ph):
                nxt = phases[ph.index + 1] if ph.index < LAST else None
                dve.wait_ge(gain_loaded, 16 * (ph.index + 1))
                for tt in range(TT):
                    dve.wait_ge(y_rstd, ph.tile + tt + 1)
                    step(dve.scalar_tensor_tensor(token_banks(tt), token_banks(tt), rstd_y[:, tt:tt + 1],
                                                  post_gain[:], ALU.mult, ALU.mult))
                    dve.tensor_tensor(x_res[:, tt, :], token_banks(tt), x_res[:, tt, :], ALU.add)\
                       .then_inc(x_new, 1)
                    if nxt and tt >= 2:
                        operand_low_of(nxt, tt - 2)
                    if nxt:
                        scale_x(nxt, tt)
                if nxt:
                    operand_low_of(nxt, TT - 2)
                    operand_low_of(nxt, TT - 1)

            for k in range(CREDIT):
                dve.memset(credit[:, CREDIT + k:CREDIT + k + 1], 0.0).then_inc(hidden_done, 1)
            for mt in range(MT):
                dve.wait_ge(mem_rstd, 1)
                dve.tensor_scalar(mem_scaled[:, mt, :], mem_nat[:, mt, :], small[:, mt:mt + 1], None,
                                  ALU.mult).then_inc(mem_scaled_done, 1)
            for mt in range(MT):
                dve.wait_ge(mem_high, mt + 1)
                for layer in range(LAYERS):
                    for kt in range(KT):
                        c = slice(layer * MEM + mt * P, layer * MEM + (mt + 1) * P)
                        last = dve.scalar_tensor_tensor(
                            operand_low[:, kt, c], token_banks(mt)[:, kt * P:(kt + 1) * P],
                            gain_col(layer, 4, kt), operand_high[:, kt, c].bitcast(F32),
                            ALU.mult, ALU.subtract)
                last.then_inc(mem_low, 1)
            for u in range(AHEAD):
                split_low(u)
            dve.wait_ge(mem_turned, MT)
            for tt in range(TT):
                scale_x(phases[0], tt)
            for u in range(8 * LAYERS):
                split_low(u + AHEAD)
            for tt in range(TT):
                operand_low_of(phases[0], tt)
            dve.wait_ge(kv_stored, 16 * 2 * LAYERS)

            def ffn(ph):
                n0, u = ph.nth * FC, ph.unit
                with dve.Fori(0, FC // RING) as it:
                    for k in range(RING):
                        split_low(u + k + AHEAD, it * RING)
                        dve.wait_ge(silu_done, CREDIT + n0 + k + 1 + it * RING)
                        dve.wait_ge(unit_used, u + k + 1 + it * RING)
                        dve.tensor_tensor(hidden[:, bass.ds(it * RING + k, 1), :],
                                          silu[:, k % 2:k % 2 + 1, :], banks[:, 2 * k + 1:2 * k + 2, :],
                                          ALU.mult).then_inc(hidden_done, 1)
                u += FC
                a0 = ph.nth * (FC // 2)
                def pair(k, more=0):
                    dve.wait_ge(act_high, a0 + k + 1 + more)
                    if isinstance(more, int):
                        src = hidden[:, 2 * (k + more):2 * (k + more) + 2, :]
                    else:
                        src = hidden[:, bass.ds(more * 2 + 2 * k, 2), :]
                    part_of = slice(2 * (k % 4), 2 * (k % 4) + 2)
                    dve.tensor_tensor(operand_low[:, part_of, :], src,
                                      operand_high[:, part_of, :].bitcast(F32), ALU.subtract)\
                       .then_inc(act_low, 1)
                for k in range(AHEAD):
                    pair(k)
                with dve.Fori(0, FC // 2 // RING - 1) as it:
                    for k in range(RING):
                        split_low(u + k + AHEAD, it * RING)
                        pair(k + AHEAD, it * RING)
                for v in range(FC // 2 - RING, FC // 2):
                    split_low(u + v + AHEAD)
                    if v + AHEAD < FC // 2:
                        pair(v + AHEAD)

            def window(ph):
                for v in range(7):
                    split_low(ph.unit + v + AHEAD)
                dve.wait_ge(AB["in_evac"], 7)
                raw_stats, mean_var = small[:, 20:26], small[:, 26:28]
                for tt in range(TT):
                    step(dve.bn_stats(raw_stats, vg[:, tt, :]))
                    step(dve.bn_aggr(mean_var, raw_stats))
                    step(dve.tensor_copy(small[:, 16 + tt:17 + tt], mean_var[:, 0:1]))
                    step(dve.tensor_copy(small[:, 8 + tt:9 + tt], mean_var[:, 1:2]))
                dve.memset(small[:, 28:29], 0.0).then_inc(AB["stat_done"], 1)
                dve.wait_ge(AB["sguT_ready"], 1)
                dve.memset(sguT[64:P, :, 0:64], 0.0).then_inc(AB["masked"], 1)
                dve.wait_ge(AB["ln_rstd"], 1)
                for tt in range(TT):
                    dve.tensor_scalar(vg[:, tt, :], vg[:, tt, :], small[:, 16 + tt:17 + tt],
                                      small[:, 12 + tt:13 + tt], ALU.subtract, ALU.mult)\
                       .then_inc(AB["ln_done"], 1)
                dve.wait_ge(AB["tables"], AB_TABLES)
                for c in range(2):
                    biased(c)
                for g in range(SGU_GROUPS):
                    dve.wait_ge(AB["mixed"], g + 1)
                    step(dve.scalar_tensor_tensor(
                        yb[:, g, :].rearrange("p (t n) -> p t n", t=TT),
                        banks[:, 4 + g, :].rearrange("p (t n) -> p t n", t=TT), sgu_gain(g),
                        sgu_bias[:, g:g + 1, :].broadcast_to([P, TT, P]), ALU.mult, ALU.add))
                    dve.tensor_tensor(yb[:, g, :], yb[:, g, :], uT[:, g, :], ALU.mult).then_inc(AB["yb_done"], 1)
                for g in range(SGU_GROUPS):
                    dve.wait_ge(AB["yb_high"], g + 1)
                    dve.tensor_tensor(operand_low[:, 4 + g, :], yb[:, g, :],
                                      operand_high[:, 4 + g, :].bitcast(F32), ALU.subtract)\
                       .then_inc(AB["out_low"], 1)
                for c in range(NCH):
                    b = c % 2
                    dve.wait_ge(AB["exped"], c + 1)
                    neg_max, sink_gap, total, sink_exp = (
                        small[:, 32 + 16 * b + 4 * i:36 + 16 * b + 4 * i] for i in range(4))
                    step(dve.tensor_tensor(total, total, sink_exp, ALU.add))
                    step(dve.reciprocal(total, total))
                    for g in range(4):
                        last = dve.tensor_scalar(probs[b][:, g, :], probs[b][:, g, :], total[:, g:g + 1],
                                                 None, ALU.mult)
                    last.then_inc(AB["normed"], 1)
                    if c + 2 < NCH:
                        dve.wait_ge(AB["p_turned"], c + 1)
                        biased(c + 2)
                    if c:
                        attended_low(c - 1)
                attended_low(NCH - 1)
                for v in range(7, 11):
                    split_low(ph.unit + v + AHEAD)

            def attended_low(c):
                    b = c % 2
                    dve.wait_ge(AB["out_high"], c + 1)
                    for kv in range(2):
                        rows, cols = slice(kv * 64, kv * 64 + 64), slice(c * CHUNK, (c + 1) * CHUNK)
                        last = dve.tensor_tensor(
                            operand_low[rows, 0:4, cols],
                            banks[rows, 6 + b, kv * 256:(kv + 1) * 256].rearrange("p (j q) -> p j q", j=4),
                            operand_high[rows, 0:4, cols].bitcast(F32), ALU.subtract)
                    last.then_inc(AB["out_low"], 1)

            def biased(c):
                b = c % 2
                neg_max, sink_gap, total, sink_exp = (
                    small[:, 32 + 16 * b + 4 * i:36 + 16 * b + 4 * i] for i in range(4))
                dve.wait_ge(AB["scores"], c + 1)
                step(dve.scalar_tensor_tensor(
                    probs[b].rearrange("p (k n) q -> p k (n q)", k=2), banks[:, 2 * b:2 * b + 2, 0:256],
                    A_DIM ** -0.5, bias_tab[:, min(c, 1), :].rearrange("p (k n) -> p k n", k=2),
                    ALU.mult, ALU.add))
                step(dve.tensor_reduce(neg_max, probs[b], AX.X, ALU.max))
                step(dve.tensor_tensor(neg_max, neg_max, sink, ALU.max))
                step(dve.tensor_tensor(sink_gap, sink, neg_max, ALU.subtract))
                dve.tensor_scalar(neg_max, neg_max, -1.0, None, ALU.mult).then_inc(AB["shifted"], 1)

            def gated(ph):
                for v in range(12):
                    split_low(ph.unit + v + AHEAD)
                step(dve.memset(exp1, 0.0))
                dve.memset(g_nat[:, :, G_RANK:G_RANK + 1], 1.0).then_inc(GL["cleared"], 1)
                def absolute(tt):
                    dve.wait_ge(GL["z_copied"], tt + 1)
                    if tt >= 2:
                        dve.wait_ge(GL["log_ready"], tt - 1)
                    dve.scalar_tensor_tensor(z_tmp[tt % 2], loga[:, tt, :], -1.0, loga[:, tt, :],
                                             ALU.mult, ALU.max).then_inc(GL["z_abs"], 1)
                absolute(0)
                absolute(1)
                for tt in range(TT):
                    dve.wait_ge(GL["z_log"], tt + 1)
                    dve.scalar_tensor_tensor(loga[:, tt, :], loga[:, tt, :], 0.0, z_tmp[tt % 2], ALU.min,
                                             ALU.subtract).then_inc(GL["log_ready"], 1)
                    if tt + 2 < TT:
                        absolute(tt + 2)
                for h in range(G_HEADS):
                    dve.wait_ge(GL["exp_done"], h + 1)
                    dve.tensor_copy(decay[:, h, :], exps[0].rearrange("p (c n) -> p c n", c=NCH)[:, :, CHUNK - 1])
                    dve.tensor_tensor(exps[2], exps[2], gk[:, h, :], ALU.mult).then_inc(GL["kend_made"], 1)
                    dve.tensor_tensor(gk[:, h, :], gk[:, h, :], exps[1], ALU.mult)
                    dve.scalar_tensor_tensor(gq[:, h, :], gq[:, h, :], G_DK ** -0.5, exps[0], ALU.mult,
                                             ALU.mult).then_inc(GL["dec_done"], 1)
                dve.wait_ge(GL["dec_done"], G_HEADS)
                step(dve.memset(att[0], 0.0))
                step(dve.memset(att[1], 0.0))
                mask = gmask.bitcast(U32).unsqueeze(1).broadcast_to([P, TT, P])
                for h in range(G_HEADS):
                    dve.wait_ge(GL["att_done"], h + 1)
                    dve.copy_predicated(att[h % 2].rearrange("p (t n) -> p t n", t=TT), mask,
                                        banks[:, 0, :].rearrange("p (t n) -> p t n", t=TT))\
                       .then_inc(GL["att_ready"], 1)
                    dve.wait_ge(GL["kv_done"], h + 1)
                    for c in range(NCH - 1):
                        if c >= 4:
                            dve.wait_ge(GL["o_done"], h * TT + (c - 3) // 2 + 1)
                        elif h:
                            dve.wait_ge(GL["o_done"], h * TT)
                        old = states[:, c % 4, :]
                        b, half = 2 + 2 * (c % 2) + (c // 2) // 2, (c // 2) % 2
                        new_product = banks[:, b, half * 256:(half + 1) * 256]
                        if c == 0:
                            ins = dve.tensor_copy(states[:, 1, :], new_product)
                        else:
                            ins = dve.scalar_tensor_tensor(states[:, (c + 1) % 4, :], old,
                                                           decay[:, h, c:c + 1], new_product, ALU.mult, ALU.add)
                        ins.then_inc(GL["state_ready"], 1)
                        if c < NCH - 2:
                            dve.wait_ge(GL["state_ready"], h * (NCH - 1) + c + 1)
                    dve.wait_ge(GL["o_rstd"], h + 1)
                    for tt in range(TT):
                        if h or tt >= 2:
                            dve.wait_ge(GL["o_turned"], h * TT + tt - 1)
                        dve.tensor_scalar(o_nat[:, tt % 2, :], banks[:, 6 + tt // 2, 256 * (tt % 2):256 * (tt % 2) + 256],
                                          small[:, 4 * (h % 2) + tt:4 * (h % 2) + tt + 1], None, ALU.mult)\
                           .then_inc(GL["o_scaled"], 1)
                    dve.wait_ge(GL["o_turned"], (h + 1) * TT)
                    for j in range(2):
                        c = 2 * h + j
                        dve.scalar_tensor_tensor(gr[:, c, :], banks[:, j, :], head_gain(c), gr[:, c, :],
                                                 ALU.mult, ALU.mult).then_inc(GL["y_ready"], 1)
                    for j in range(2):
                        c = 2 * h + j
                        dve.wait_ge(GL["out_high"], c + 1)
                        dve.tensor_tensor(operand_low[:, c, :], gr[:, c, :],
                                          operand_high[:, c, :].bitcast(F32), ALU.subtract)\
                           .then_inc(GL["out_low"], 1)
                for v in range(12, 16):
                    split_low(ph.unit + v + AHEAD)

            def cross(ph):
                base = 4 * ph.nth
                for v in range(4):
                    split_low(ph.unit + v + AHEAD)
                for tt in range(TT + 1):
                    if tt < TT:
                        b = tt % 2
                        neg_max = small[:, 8 * b:8 * b + 4]
                        dve.wait_ge(XA["scores"], base + tt + 1)
                        step(dve.tensor_reduce(neg_max, token_banks(tt).rearrange("p (h n) -> p h n", h=X_HEADS),
                                               AX.X, ALU.max))
                        dve.tensor_scalar(neg_max, neg_max, -((D // X_HEADS) ** -0.5), None, ALU.mult)\
                           .then_inc(XA["maxed"], 1)
                    if tt:
                        b = (tt - 1) % 2
                        total = small[:, 8 * b + 4:8 * b + 8]
                        dve.wait_ge(XA["exped"], base + tt)
                        step(dve.reciprocal(total, total))
                        for h in range(X_HEADS):
                            last = dve.tensor_scalar(xp[b][:, h, :], xp[b][:, h, :], total[:, h:h + 1], None,
                                                     ALU.mult)
                        last.then_inc(XA["normed"], 1)
                for j in range(KT):
                    dve.wait_ge(XA["out_high"], 8 * ph.nth + j + 1)
                    dve.tensor_tensor(operand_low[:, j, :], banks[:, j, :],
                                      operand_high[:, j, :].bitcast(F32), ALU.subtract)\
                       .then_inc(XA["out_low"], 1)
                for v in range(4, 8):
                    split_low(ph.unit + v + AHEAD)

            for ph in phases:
                {"ffn": ffn, "ab": window, "gla": gated, "xattn": cross}[ph.name](ph)
                boundary(ph)

        @block.tensor
        def _(pe):
            def three(out_, w_high, w_low, a_high, a_low, start, stop):
                pe.matmul(out_, w_high, a_high, start=start, stop=False)
                pe.matmul(out_, w_high, a_low, start=False, stop=False)
                return pe.matmul(out_, w_low, a_high, start=False, stop=stop)

            def column_chunk(u, pick, out_, cols):
                for kt in range(KT):
                    last = three(out_, pick(high_weights[:, u % RING, :], kt),
                                 pick(low_weights[:, u % RING, :], kt),
                                 operand_high[:, kt, cols], operand_low[:, kt, cols],
                                 kt == 0, kt == KT - 1)
                return last

            def natural(u, out_, tokens, c0, n):
                for kt in range(KT):
                    w = slice(kt * 256 + c0, kt * 256 + c0 + n)
                    last = three(out_, operand_high[:, kt, tokens], operand_low[:, kt, tokens],
                                 high_weights[:, u % RING, w], low_weights[:, u % RING, w],
                                 kt == 0, kt == KT - 1)
                return last

            def block_of(half):
                return lambda slot, kt: slot[:, kt * 256 + half * P:kt * 256 + half * P + P]

            def turn_x(ph, tt, frees_unit=False):
                pe.wait_ge(x_scaled, ph.tile + tt + 1)
                for kt in range(KT):
                    last = pe.transpose(token_banks(tt)[:, kt * P:(kt + 1) * P],
                                        scaled[:, tt, kt * P:(kt + 1) * P], identity[:])
                    if kt == 0 and frees_unit:
                        last.then_inc(unit_used, 1)
                last.then_inc(x_turned, 1)

            def output_unit(u, tt, k, chunk, start, stop):
                rows, slot = slice(tt * P, (tt + 1) * P), u % RING
                for nh in range(2):
                    w = slice(k * D + nh * T, k * D + (nh + 1) * T)
                    last = three(banks[:, 2 * tt + nh, :], operand_high[:, chunk, rows],
                                 operand_low[:, chunk, rows], high_weights[:, slot, w],
                                 low_weights[:, slot, w], start, stop)
                return last

            def last_units(ph, u, first_chunk):
                nxt = phases[ph.index + 1] if ph.index < LAST else None
                pe.wait_ge(low_done, u + 2)
                for tt in range(TT):
                    for j in range(4):
                        last = output_unit(u + j // 2, tt, j % 2, first_chunk + j, False, j == 3)
                        if j == 1 and tt == TT - 1:
                            last.then_inc(unit_used, 1)
                    last.then_inc(y_done, 1)
                    if nxt and tt >= 2:
                        turn_x(nxt, tt - 2, frees_unit=tt == TT - 1)
                if nxt:
                    turn_x(nxt, TT - 2)
                    turn_x(nxt, TT - 1)

            def output_projection(ph, u):
                for v in range(2):
                    pe.wait_ge(low_done, u + v + 1)
                    for k in range(2):
                        for tt in range(TT):
                            last = output_unit(u + v, tt, k, 2 * v + k, v + k == 0, False)
                    last.then_inc(unit_used, 1)
                last_units(ph, u + 2, 4)

            pe.wait_ge(table_loaded, 16 * 5)
            pe.transpose(banks[:, 7, 0:P], gain_rows[:, 0, :], identity[:])
            pe.transpose(banks[:, 7, P:GAIN_ROWS], gain_rows[0:GAIN_ROWS - P, 1, :],
                         identity[0:GAIN_ROWS - P, 0:GAIN_ROWS - P]).then_inc(gains_turned, 1)
            for mt in range(MT):
                pe.wait_ge(mem_scaled_done, mt + 1)
                for kt in range(KT):
                    last = pe.transpose(token_banks(mt)[:, kt * P:(kt + 1) * P],
                                        mem_scaled[:, mt, kt * P:(kt + 1) * P], identity[:])
                last.then_inc(mem_turned, 1)
            pe.wait_ge(mem_low, MT)
            for u in range(8 * LAYERS):
                i, layer, bank = u // 4, u // 8, banks[:, u % 4, :]
                pe.wait_ge(low_done, u + 1)
                if u >= 4:
                    pe.wait_ge(mem_evac, u - 3)
                for half in range(2):
                    if i % 2 == 0:
                        last = column_chunk(u, block_of(half), bank[:, half * MEM:(half + 1) * MEM],
                                            slice(layer * MEM, (layer + 1) * MEM))
                    else:
                        m = layer * MEM + half * P
                        last = natural(u, bank[:, half * 256:(half + 1) * 256], slice(m, m + P), 0, 256)
                last.then_inc(unit_used, 1)
            pe.wait_ge(mem_evac, 8 * LAYERS)
            for tt in range(TT):
                turn_x(phases[0], tt)

            def ffn(ph):
                n0, u = ph.nth * FC, ph.unit
                pe.wait_ge(x_low, ph.tile + TT)
                all_tokens = slice(0, T)
                gate = lambda slot, kt: slot[:, kt * P:(kt + 1) * P]
                up = lambda slot, kt: slot[:, (KT + kt) * P:(KT + kt + 1) * P]
                with pe.Fori(0, FC // RING) as it:
                    for k in range(RING):
                        pe.wait_ge(low_done, u + k + 1 + it * RING)
                        pe.wait_ge(silu_done, CREDIT + n0 + k - RING + 1 + it * RING)
                        column_chunk(u + k, gate, banks[:, 2 * k, :], all_tokens).then_inc(gate_done, 1)
                        pe.wait_ge(hidden_done, CREDIT + n0 + k - RING + 1 + it * RING)
                        column_chunk(u + k, up, banks[:, 2 * k + 1, :], all_tokens).then_inc(unit_used, 1)
                u += FC
                a0 = ph.nth * (FC // 2)
                pe.wait_ge(hidden_done, CREDIT + n0 + FC)

                def whole(v, more=0, start=False):
                    pe.wait_ge(low_done, u + v + 1 + more)
                    pe.wait_ge(act_low, a0 + v + 1 + more)
                    for k in range(2):
                        for tt in range(TT):
                            last = output_unit(u + v, tt, k, 2 * (v % 4) + k, start and k == 0, False)
                    last.then_inc(unit_used, 1)
                for v in range(2):
                    whole(v, start=v == 0)
                with pe.Fori(0, FC // 2 // RING - 1) as it:
                    for k in range(RING):
                        whole(2 + k, it * RING)
                pe.wait_ge(act_low, a0 + FC // 2)
                last_units(ph, u + FC // 2 - 2, 4)

            def window(ph):
                u = ph.unit
                pe.wait_ge(x_low, ph.tile + TT)
                for v in range(7):
                    pe.wait_ge(low_done, u + v + 1)
                    if v >= 3:
                        pe.wait_ge(AB["in_evac"], min(v - 2, 3))
                    for half in range(2):
                        if v < 2:
                            last = column_chunk(u + v, block_of(half), banks[:, 2 * v + half, :], slice(0, T))
                        elif v == 2 and half == 0:
                            column_chunk(u + v, block_of(0), banks[:, 4, :], slice(0, T))
                        elif v == 2:
                            for i in range(7):
                                start = i * P if i < 4 else (i - 4) * P + CHUNK
                                last = natural(u + v, banks[:, 5 + i // 4, (i % 4) * P:(i % 4 + 1) * P],
                                               slice(start, start + P), P, P)
                        elif v < 5:
                            last = column_chunk(u + v, block_of(half), banks[:, 2 * (v - 3) + half, :], slice(0, T))
                        else:
                            for tt in range(2 * half, 2 * half + 2):
                                last = natural(u + v, banks[:, 2 * (v - 3) + half, (tt % 2) * 256:(tt % 2 + 1) * 256],
                                               slice(tt * P, (tt + 1) * P), 0, 256)
                    last.then_inc(unit_used, 1)
                pe.wait_ge(AB["tables"], AB_TABLES)
                pe.wait_ge(AB["in_evac"], 7)

                def scores(c):
                    b, k0 = c % 2, max(c - 1, 0) * CHUNK
                    if c >= 2:
                        pe.wait_ge(AB["shifted"], c - 1)
                    for kv in range(2):
                        rows = slice(kv * 64, kv * 64 + 64)
                        for pair in range(2):
                            last = pe.matmul(banks[:, 2 * b + kv, pair * P:(pair + 1) * P],
                                             qT[rows, c // 2, (c % 2) * 256 + pair * P:(c % 2) * 256 + (pair + 1) * P],
                                             kT[rows, k0:k0 + P], start=True, stop=True)
                    last.then_inc(AB["scores"], 1)

                scores(0)
                scores(1)
                for g in range(SGU_GROUPS):
                    last = pe.transpose(banks[:, 6, g * P:(g + 1) * P], sgu_raw[:, g, :], identity[:])
                last.then_inc(AB["sguT_psum"], 1)
                pe.wait_ge(AB["masked"], 1)
                pe.wait_ge(AB["ln_done"], TT)
                for g in range(SGU_GROUPS):
                    for tt in range(TT):
                        last = pe.matmul(banks[:, 4 + g, tt * P:(tt + 1) * P], vg[:, tt, g * P:(g + 1) * P],
                                         sguT[:, g, :], start=True, stop=True)
                    last.then_inc(AB["mixed"], 1)
                pe.wait_ge(AB["yb_done"], SGU_GROUPS)
                for c in range(NCH):
                    b = c % 2
                    pe.wait_ge(AB["normed"], c + 1)
                    if c >= 2:
                        pe.wait_ge(AB["p_evac"], c - 1)
                    for g in range(4):
                        last = pe.transpose(banks[:, 4 + b, g * P:(g + 1) * P], probs[b][:, g, :], identity[:])
                    last.then_inc(AB["p_turned"], 1)
                    if c + 2 < NCH:
                        scores(c + 2)
                    pe.wait_ge(AB["p_evac"], c + 1)
                    if c >= 2:
                        pe.wait_ge(AB["out_low"], SGU_GROUPS + c - 1)
                    tile = max(c - 1, 0)
                    window_of = v_win[:, tile // 2 if tile % 2 == 0 else 4 + tile // 2, :]
                    pe.matmul(banks[:, 6 + b, :], window_of, probsT[b], start=True, stop=True)\
                      .then_inc(AB["attended"], 1)
                pe.wait_ge(AB["out_low"], SGU_GROUPS + NCH)
                output_projection(ph, u + 7)

            def gated(ph):
                u = ph.unit
                pe.wait_ge(x_low, ph.tile + TT)
                for v in range(12):
                    pe.wait_ge(low_done, u + v + 1)
                    if v >= 4:
                        pe.wait_ge(GL["in_evac"], v - 3)
                    for half in range(2):
                        bank = banks[:, 2 * (v % 4) + half, :]
                        if 4 <= v < 8:
                            for tt in range(2 * half, 2 * half + 2):
                                last = natural(u + v, bank[:, (tt % 2) * 256:(tt % 2 + 1) * 256],
                                               slice(tt * P, (tt + 1) * P), 0, 256)
                        else:
                            last = column_chunk(u + v, block_of(half), bank, slice(0, T))
                    last.then_inc(unit_used, 1)
                pe.wait_ge(GL["tables"], 16 * 6)
                pe.wait_ge(GL["in_evac"], 9)
                for tt in range(TT):
                    for kt in range(KT):
                        for k, operand in enumerate((operand_high, operand_low)):
                            last = pe.matmul(banks[:, 0, tt * G_RANK:(tt + 1) * G_RANK],
                                             operand[:, kt, tt * P:(tt + 1) * P].bitcast(F32),
                                             gate_raw[:, kt, :], start=kt + k == 0, stop=kt == KT - 1 and k == 1)
                last.then_inc(GL["g_done"], 1)
                pe.wait_ge(GL["g_copied"], 1)
                for tt in range(TT):
                    last = pe.transpose(banks[:, 1, tt * P:(tt + 1) * P], g_nat[:, tt, :], identity[:])
                last.then_inc(GL["g_turned"], 1)
                pe.wait_ge(GL["gT_ready"], 1)
                pe.wait_ge(GL["in_evac"], 12)
                for tt in range(TT):
                    pe.matmul(banks[:, 2 + tt, :], gT[0:G_RANK + 1, tt * P:(tt + 1) * P],
                              gate_w[0:G_RANK + 1, :], start=True, stop=True).then_inc(GL["z_done"], 1)
                pe.wait_ge(GL["log_ready"], TT)
                for h in range(G_HEADS):
                    if h:
                        pe.wait_ge(GL["exp_done"], h)
                    for bank, table in ((0, gcum), (1, gend)):
                        for tt in range(TT):
                            last = pe.matmul(banks[:, bank, tt * P:(tt + 1) * P],
                                             loga[:, tt, h * P:(h + 1) * P], table, start=True, stop=True)
                    last.then_inc(GL["cum_done"], 1)
                    pe.wait_ge(GL["kend_made"], h + 1)
                    if h:
                        pe.wait_ge(GL["kend_ready"], h)
                    for tt in range(TT):
                        last = pe.transpose(banks[:, 2, tt * P:(tt + 1) * P], exps[2][:, tt * P:(tt + 1) * P],
                                            identity[:])
                    last.then_inc(GL["kend_turned"], 1)
                pe.wait_ge(GL["dec_done"], G_HEADS)
                pe.wait_ge(GL["kend_ready"], G_HEADS)
                for h in range(G_HEADS):
                    if h:
                        pe.wait_ge(GL["y_ready"], 2 * h)
                    for tt in range(TT):
                        s = slice(tt * P, (tt + 1) * P)
                        last = pe.matmul(banks[:, 0, s], gk[:, h, s], gq[:, h, s], start=True, stop=True)
                    last.then_inc(GL["att_done"], 1)
                    if h:
                        pe.wait_ge(GL["state_ready"], h * (NCH - 1))
                    for c in range(NCH - 1):
                        rows, bank, half = slice((c % 2) * 64, (c % 2) * 64 + 64), 2 + 2 * (c % 2) + (c // 2) // 2, (c // 2) % 2
                        last = pe.matmul(banks[:, bank, half * 256:(half + 1) * 256],
                                         loga[rows, c // 2, h * P:(h + 1) * P],
                                         gv[rows, c // 2, h * G_DV:(h + 1) * G_DV], start=True, stop=True)
                    last.then_inc(GL["kv_done"], 1)
                    pe.wait_ge(GL["att_ready"], h + 1)
                    if h:
                        pe.wait_ge(GL["o_scaled"], h * TT)
                    for tt in range(TT):
                        o = banks[:, 6 + tt // 2, (tt % 2) * 256:(tt % 2 + 1) * 256]
                        values = gv[:, tt, h * G_DV:(h + 1) * G_DV]
                        if tt == 0:
                            pe.matmul(o[0:64, :], att[h % 2][:, 0:64], values, start=True, stop=True)
                            pe.matmul(o[64:P, :], att[h % 2][:, 64:P], values, start=True, stop=False)
                        else:
                            pe.matmul(o, att[h % 2][:, tt * P:(tt + 1) * P], values, start=True, stop=False)
                        for c in (2 * tt, 2 * tt + 1):
                            if c == 0:
                                continue
                            pe.wait_ge(GL["state_ready"], h * (NCH - 1) + c)
                            r = slice((c % 2) * 64, (c % 2) * 64 + 64)
                            last = pe.matmul(o[r, :], gq[:, h, c * CHUNK:(c + 1) * CHUNK], states[:, c % 4, :],
                                             start=False, stop=True)
                        last.then_inc(GL["o_done"], 1)
                    for tt in range(TT):
                        pe.wait_ge(GL["o_scaled"], h * TT + tt + 1)
                        for j in range(2):
                            last = pe.transpose(banks[:, j, tt * P:(tt + 1) * P],
                                                o_nat[:, tt % 2, j * P:(j + 1) * P], identity[:])
                        last.then_inc(GL["o_turned"], 1)
                pe.wait_ge(GL["out_low"], KT)
                output_projection(ph, u + 12)

            def cross(ph):
                u, base = ph.unit, 4 * ph.nth
                pe.wait_ge(x_low, ph.tile + TT)
                for v in range(4):
                    pe.wait_ge(low_done, u + v + 1)
                    for half in range(2):
                        last = column_chunk(u + v, block_of(half), banks[:, 2 * v + half, :], slice(0, T))
                    last.then_inc(unit_used, 1)
                pe.wait_ge(XA["in_evac"], base + 4)
                pe.wait_ge(XA["kv_loaded"], 32 * (ph.nth + 1))
                for tt in range(TT):
                    for h in range(X_HEADS):
                        for dc in range(2):
                            last = pe.matmul(token_banks(tt)[:, h * MEM:(h + 1) * MEM],
                                             xq[:, 2 * h + dc, tt * P:(tt + 1) * P], xk[:, 2 * h + dc, :],
                                             start=dc == 0, stop=dc == 1)
                    last.then_inc(XA["scores"], 1)
                for tt in range(TT):
                    pe.wait_ge(XA["normed"], base + tt + 1)
                    for h in range(X_HEADS):
                        for mc in range(2):
                            i = 2 * h + mc
                            last = pe.transpose(token_banks(tt)[:, i * P:(i + 1) * P],
                                                xp[tt % 2][:, h, mc * P:(mc + 1) * P], identity[:])
                    last.then_inc(XA["p_turned"], 1)
                pe.wait_ge(XA["p_evac"], base + 4)
                for j in range(KT):
                    for mc in range(MT):
                        last = pe.matmul(banks[:, j, :], xv[:, mc, j * P:(j + 1) * P], xpT[:, 2 * (j // 2) + mc, :],
                                         start=mc == 0, stop=mc == MT - 1)
                    last.then_inc(XA["attended"], 1)
                pe.wait_ge(XA["out_low"], 8 * (ph.nth + 1))
                output_projection(ph, u + 4)

            for ph in phases:
                {"ffn": ffn, "ab": window, "gla": gated, "xattn": cross}[ph.name](ph)


_INS = ["x", "mem", "norm_g", "ffn1_w_in", "ffn1_w_out", "ffn2_w_in", "ffn2_w_out", "xattn_w_q",
        "xattn_w_kv", "xattn_w_o", "ab_w_in", "ab_sink", "ab_sgu_w", "ab_sgu_b", "ab_sgu_norm_g",
        "ab_w_out", "c_w_in", "c_gate_w", "c_gate_b", "c_head_norm_g", "c_w_out"]


def build(nc, shapes, stop=None):
    args = [nc.dram_tensor(f"in_{name}_dram", shape, F32, kind="ExternalInput").ap()
            for name, shape in shapes]
    result = nc.dram_tensor("out_0_dram", (1, T, D), F32, kind="ExternalOutput").ap()
    trunk_kernel(nc, *args, result, stop=stop)


def kernel(**inputs):
    import concourse.bacc as bacc
    from concourse.bass_utils import run_bass_kernel_spmd

    arrays = {f"in_{name}_dram": np.ascontiguousarray(inputs[name]) for name in _INS}
    arrays["in_constants_dram"] = constant_table()
    nc = bacc.Bacc("TRN2", target_bir_lowering=False, num_devices=1)
    build(nc, [(n[3:-5], a.shape) for n, a in arrays.items()])
    return run_bass_kernel_spmd(nc, [arrays], core_ids=[0]).results[0]["out_0_dram"]
```

```python
from contextlib import ExitStack

import numpy as np

import concourse.bass as bass
from concourse import mybir

F32 = mybir.dt.float32
F32R = mybir.dt.float32r
BF16 = mybir.dt.bfloat16
U32 = mybir.dt.uint32
ALU = mybir.AluOpType
ACT = mybir.ActivationFunctionType
AX = mybir.AxisListType

P = 128
D = 1024
KT = D // P
T = 512
TT = T // P
MEM = 256
MT = MEM // P
FF = 4 * D
FC = FF // P
LAYERS = 2
NORMS = 9
EPS = 1e-6
CHUNK = 64
NCH = T // CHUNK
UNIT = 2048
RING = 4
RAW = 2
AHEAD = 2
A_HEADS, A_DIM = 8, 64
AB_WIDTH = 512
SGU_GROUPS = 4
G_HEADS, G_DK, G_DV = 4, 128, 256
G_RANK = 16
X_HEADS = 4
NEG = -1e30
CREDIT = RING
GAIN_ROWS = LAYERS * NORMS * KT + SGU_GROUPS + KT

C_ID, C_CUM, C_END, C_MASK, C_BIAS0, C_BIAS = 0, 128, 256, 384, 512, 1024
C_ALL = 1536


def constant_table():
    c = np.zeros((P, C_ALL), np.float32)
    row, col = np.arange(P)[:, None], np.arange(P)[None, :]
    same = row // CHUNK == col // CHUNK
    c[:, C_ID:C_ID + P] = row == col
    c[:, C_CUM:C_CUM + P] = (same & (row <= col)) / 16.0
    c[:, C_END:C_END + P] = (same & (row > col)) / 16.0
    c[:, C_MASK:C_MASK + P] = same & (row <= col)
    slopes = (2.0 ** (-8.0 * np.arange(1, A_HEADS + 1) / A_HEADS)).astype(np.float32)
    q = np.arange(P) % CHUNK
    for kv in range(2):
        for pair in range(2):
            group = 2 * kv + pair
            head = 4 * kv + 2 * pair + np.arange(P) // CHUNK
            dist = np.abs(q[:, None] + CHUNK - np.arange(P)[None, :]).astype(np.float32)
            c[:, C_BIAS + group * P:C_BIAS + (group + 1) * P] = -slopes[head][:, None] * dist
            first = np.abs(q[:, None] - np.arange(P)[None, :]).astype(np.float32)
            bias = np.where(np.arange(P)[None, :] < CHUNK, -slopes[head][:, None] * first, NEG)
            c[:, C_BIAS0 + group * P:C_BIAS0 + (group + 1) * P] = bias
    return c


class Phase:

    def __init__(self, name, unit, norm_in, norm_out, layer, index, nth):
        self.name, self.unit, self.norm_in, self.norm_out = name, unit, norm_in, norm_out
        self.layer, self.index = layer, index
        self.tile = TT * index
        self.nth = nth


def trunk_kernel(nc, x_in, mem_in, norm_g, f1_in, f1_out, f2_in, f2_out, xq_w, xkv_w, xo_w,
                 ab_in, ab_sink, sgu_w, sgu_b, sgu_g, ab_out, c_in, c_gate_w, c_gate_b,
                 c_head_g, c_out, constants, out, stop=None):
    phases = []
    unit = LAYERS * 8
    for layer in range(LAYERS):
        mixer = ("ab", 7 + 4) if layer % 2 == 0 else ("gla", 12 + 4)
        for name, n, pre, post in (("ffn", 48, 0, 1), (*mixer, 2, 3), ("xattn", 8, 5, 6),
                                   ("ffn", 48, 7, 8)):
            nth = sum(ph.name == name for ph in phases)
            phases.append(Phase(name, unit, pre, post, layer, len(phases), nth))
            unit += n
    phases = phases[:stop]
    if stop is not None and stop < 8:
        unit = phases[-1].unit + {"ffn": 48, "ab": 11, "gla": 16, "xattn": 8}[phases[-1].name]
    UNITS = unit
    LAST = len(phases) - 1

    with ExitStack() as ctx:
        def sb(name, shape, dt=F32):
            return ctx.enter_context(nc.sbuf_tensor(name, shape, dt))

        def sem(name):
            return ctx.enter_context(nc.semaphore(name))

        x_res = sb("x_res", [P, TT, D])
        operand_high = sb("operand_high", [P, KT, T], F32R)
        operand_low = sb("operand_low", [P, KT, T], F32R)
        hidden = sb("hidden", [P, FC, T])
        raw_weights = sb("raw_weights", [P, RAW, UNIT])
        high_weights = sb("high_weights", [P, RING, UNIT], F32R)
        low_weights = sb("low_weights", [P, RING, UNIT], F32R)
        post_gain = sb("post_gain", [P, D])
        silu_buf = sb("silu_buf", [P, D])
        square_junk = sb("square_junk", [P, D], BF16)
        identity = sb("identity", [P, P])
        gain_cols = sb("gain_cols", [P, GAIN_ROWS])
        stats = sb("stats", [P, 128])
        ss_y, ss_x = stats[:, 0:4], stats[:, 4:8]
        rstd_y, rstd_x, neg_half = stats[:, 12:16], stats[:, 16:20], stats[:, 20:24]
        credit = sb("credit", [P, 2 * CREDIT])
        small = stats[:, 24:128]
        banks = ctx.enter_context(nc.psum_tensor("banks", [P, 8, T], F32))
        silu = silu_buf[:].rearrange("p (b n) -> p b n", b=2)

        flat = hidden[:].rearrange("p c n -> p (c n)")
        scaled = flat[:, 0:TT * D].rearrange("p (t n) -> p t n", t=TT)

        def parts(start, *sizes):
            found = []
            for size in sizes:
                n = size if isinstance(size, int) else size[0] * size[1]
                a = flat[:, start:start + n]
                found.append(a if isinstance(size, int) else a.rearrange("p (a b) -> p a b", a=size[0]))
                start += n
            assert start <= FC * T, start
            return found

        mem_nat, mem_scaled = parts(0, (MT, D), (MT, D))
        gain_rows, *mem_kv = parts(2 * MT * D, (2, P), *[KT * MEM] * (2 * LAYERS))
        (qT, uT, vg, kT, v_win, probs0, probs1, probsT0, probsT1, bias_tab, sgu_raw, sguT, sgu_bias,
         yb, sink) = parts(0, (4, T), (4, T), (TT, T), T, (7, P), (4, P), (4, P), T, T, (2, T),
                           (4, P), (4, P), (4, P), (4, T), 4)
        probs, probsT = (probs0, probs1), (probsT0, probsT1)
        (gq, gk, gr, gv, loga, exp0, exp1, exp2, gmask, gcum, gend, decay) = parts(
            0, (G_HEADS, T), (G_HEADS, T), (KT, T), (TT, D), (TT, T), T, T, T, P, P, P,
            (G_HEADS, NCH))
        exps = (exp0, exp1, exp2)
        gate_raw = silu_buf[:, 0:KT * G_RANK].rearrange("p (k n) -> p k n", k=KT)
        gate_w = silu_buf[:, P:P + T]
        g_nat, gT, z_tmp = exp1.rearrange("p (t n) -> p t n", t=TT), exp0, (exp2, exp1)
        states = silu_buf[:].rearrange("p (s n) -> p s n", s=4)
        att = exp0
        o_nat = parts(TT * D + 2 * TT * D + TT * T + T, (TT, G_DV))[0]
        xq, xk, xv, xp0, xp1, xpT = parts(0, (KT, T), (KT, MEM), (MT, D), (X_HEADS, MEM),
                                          (X_HEADS, MEM), (KT, T))
        xp = (xp0, xp1)

        key_store = nc.dram_tensor("key_store", (LAYERS, P, KT * MEM), F32, kind="Internal").ap()
        value_store = nc.dram_tensor("value_store", (LAYERS, P, MT * D), F32, kind="Internal").ap()

        raw_landed = [sem(f"raw_landed{i}") for i in range(RAW)]
        high_done, low_done, unit_used = sem("high_done"), sem("low_done"), sem("unit_used")
        x_loaded, mem_loaded, table_loaded, out_stored = (
            sem("x_loaded"), sem("mem_loaded"), sem("table_loaded"), sem("out_stored"))
        half_set = sem("half_set")
        gains_turned, gains_ready = sem("gains_turned"), sem("gains_ready")
        mem_sq, mem_rstd, mem_scaled_done, mem_turned = (
            sem("mem_sq"), sem("mem_rstd"), sem("mem_scaled_done"), sem("mem_turned"))
        mem_high, mem_low, mem_evac, kv_stored = (
            sem("mem_high"), sem("mem_low"), sem("mem_evac"), sem("kv_stored"))
        pool_step, dve_step, act_step = sem("pool_step"), sem("dve_step"), sem("act_step")
        steps = {"pool": 0, "dve": 0, "act": 0}
        y_done, y_sq, y_rstd, x_new, gain_loaded = (
            sem("y_done"), sem("y_sq"), sem("y_rstd"), sem("x_new"), sem("gain_loaded"))
        x_sq, x_rstd, x_scaled, x_turned, x_high, x_low = (
            sem("x_sq"), sem("x_rstd"), sem("x_scaled"), sem("x_turned"), sem("x_high"), sem("x_low"))
        gate_done, chunks_read, silu_done, hidden_done, act_high, act_low = (
            sem("gate_done"), sem("chunks_read"), sem("silu_done"), sem("hidden_done"), sem("act_high"),
            sem("act_low"))
        AB = {n: sem("ab_" + n) for n in (
            "in_evac", "tables", "masked", "stat_done", "ln_rstd", "ln_done", "sguT_psum",
            "sguT_ready", "mixed", "yb_done", "yb_high", "scores", "shifted", "exped",
            "normed", "p_turned", "p_evac", "attended", "out_high", "out_low")}
        GL = {n: sem("gla_" + n) for n in (
            "in_evac", "tables", "cleared", "g_done", "g_copied", "g_turned", "gT_ready",
            "z_done", "z_copied", "r_done", "z_abs", "z_log", "log_ready", "cum_done", "exp_done", "dec_done",
            "kend_made", "kend_turned", "kend_ready", "att_done", "att_ready", "kv_done", "state_ready", "o_done",
            "o_sq", "o_rstd", "o_scaled", "o_turned", "y_ready", "out_high", "out_low")}
        XA = {n: sem("x_att_" + n) for n in (
            "kv_loaded", "in_evac", "scores", "maxed", "exped", "normed", "p_turned",
            "p_evac", "attended", "out_high", "out_low")}
        block = ctx.enter_context(nc.Block())

        in_pieces = {ph.unit + i for ph in phases if ph.name == "ab" for i in (0, 1, 7, 8)}

        def landed(u):
            return sum(64 if v in in_pieces else 32 for v in range(u % RAW, u + 1, RAW))

        AB_TABLES = 16 * (2 + 1 + SGU_GROUPS + A_HEADS)

        def gain_col(layer, norm, kt):
            c = (layer * NORMS + norm) * KT + kt
            return gain_cols[:, c:c + 1]

        def sgu_gain(g):
            c = LAYERS * NORMS * KT + g
            return gain_cols[:, c:c + 1]

        def head_gain(c):
            c += LAYERS * NORMS * KT + SGU_GROUPS
            return gain_cols[:, c:c + 1]

        def token_banks(tt):
            return banks[:, 2 * tt:2 * tt + 2, :].rearrange("p b n -> p (b n)")

        @block.sync
        def _(sp):
            sp.dma_start(mem_nat, mem_in[0].rearrange("(t p) n -> p t n", p=P)).then_inc(mem_loaded, 16)
            sp.dma_start(identity[:], constants[:, C_ID:C_ID + P]).then_inc(table_loaded, 16)
            rows = norm_g.rearrange("l k (c p) -> (l k c) p", p=P)
            n = LAYERS * NORMS * KT
            sp.dma_start(gain_rows[:, 0, :], rows[0:P, :]).then_inc(table_loaded, 16)
            sp.dma_start(gain_rows[0:n - P, 1, :], rows[P:n, :]).then_inc(table_loaded, 16)
            sp.dma_start(gain_rows[n - P:n - P + SGU_GROUPS, 1, :],
                         sgu_g[0].rearrange("(g p) -> g p", p=P)).then_inc(table_loaded, 16)
            sp.dma_start(gain_rows[n - P + SGU_GROUPS:GAIN_ROWS - P, 1, :],
                         c_head_g[0].rearrange("(g p) -> g p", p=P)).then_inc(table_loaded, 16)

            def load(u, first, second, more=0):
                if u >= RAW:
                    sp.wait_ge(low_done, u - RAW + 1 + more)
                slot = raw_weights[:, u % RAW, :]
                for (dst, src) in (first(slot), second(slot)):
                    sp.dma_start(dst, src).then_inc(raw_landed[u % RAW], 16)

            def columns(u, w, c0):
                src = w.rearrange("(k p) n -> p k n", p=P)[:, :, c0:c0 + 2 * P]
                h = KT // 2
                grid = lambda slot: slot.rearrange("p (k n) -> p k n", k=KT)
                load(u, lambda s: (grid(s)[:, 0:h, :], src[:, 0:h, :]),
                     lambda s: (grid(s)[:, h:KT, :], src[:, h:KT, :]))

            def rows_of(u, w, r0, more=0, step=0):
                def half(k):
                    start = r0 + k * P + step
                    src = w[start:start + P, :] if isinstance(start, int) else w[bass.ds(start, P), :]
                    return lambda s: (s[:, k * D:(k + 1) * D], src)
                load(u, half(0), half(1), more)

            for layer in range(LAYERS):
                for i in range(8):
                    columns(8 * layer + i, xkv_w[layer], 256 * i)
                    if layer == 0 and i == 1:
                        sp.dma_start(x_res[:], x_in[0].rearrange("(t p) n -> p t n", p=P))\
                          .then_inc(x_loaded, 16)
            for ph in phases:
                u = ph.unit
                if ph.name == "ffn":
                    w_in, w_out = ((f1_in, f1_out), (f2_in, f2_out))[ph.nth % 2]
                    src = w_in[ph.layer].rearrange("(k p) (two n) -> p k two n", p=P, two=2)
                    grid = lambda slot, h: slot.rearrange("p (h k n) -> p h k n", h=2, k=KT)[:, h]
                    with sp.Fori(0, FC // RING) as it:
                        for k in range(RING):
                            c = it * (RING * P) + k * P
                            load(u + k, lambda s: (grid(s, 0), src[:, :, 0, bass.ds(c, P)]),
                                 lambda s: (grid(s, 1), src[:, :, 1, bass.ds(c, P)]), it * RING)
                    u += FC
                    with sp.Fori(0, FC // 2 // RING) as it:
                        for k in range(RING):
                            rows_of(u + k, w_out[ph.layer], 2 * P * k, it * RING, it * (RING * 2 * P))
                elif ph.name == "ab":
                    w = ab_in[0].rearrange("(k p) n -> p k n", p=P)
                    for i in range(2):
                        sp.wait_ge(low_done, u + i - RAW + 1)
                        slot = raw_weights[:, (u + i) % RAW, :].rearrange("p (k h n) -> p k h n", k=KT, h=4)
                        for h in range(2):
                            for kv in range(2):
                                c = (4 * kv + 2 * i + h) * A_DIM
                                sp.dma_start(slot[:, :, 2 * h + kv, :], w[:, :, c:c + A_DIM])\
                                  .then_inc(raw_landed[(u + i) % RAW], 16)
                    for i in range(2, 7):
                        columns(u + i, ab_in[0], 256 * i)
                    for i in range(2):
                        v = u + 7 + i
                        sp.wait_ge(low_done, v - RAW + 1)
                        for k in range(2):
                            for kv in range(2):
                                r = (4 * kv + 2 * i + k) * A_DIM
                                sp.dma_start(raw_weights[kv * A_DIM:(kv + 1) * A_DIM, v % RAW, k * D:(k + 1) * D],
                                             ab_out[0][r:r + A_DIM, :]).then_inc(raw_landed[v % RAW], 16)
                    for i in range(2, 4):
                        rows_of(u + 7 + i, ab_out[0], 256 * i)
                elif ph.name == "gla":
                    for i in range(12):
                        columns(u + i, c_in[0], 256 * i)
                    for i in range(4):
                        rows_of(u + 12 + i, c_out[0], 256 * i)
                else:
                    for i in range(4):
                        columns(u + i, xq_w[ph.layer], 256 * i)
                    for i in range(4):
                        rows_of(u + 4 + i, xo_w[ph.layer], 256 * i)
            for tt in range(TT):
                sp.wait_ge(x_new, phases[-1].tile + tt + 1)
                sp.dma_start(out[0, tt * P:(tt + 1) * P, :], x_res[:, tt, :]).then_inc(out_stored, 16)
            sp.wait_ge(out_stored, 16 * TT)

        @block.gpsimd
        def _(pool):
            def rsqrt(rstd, ss, count, done, quarter=1.0):
                pool.tensor_scalar(rstd, ss, quarter / count, quarter * EPS,
                                   ALU.mult, ALU.add).then_inc(pool_step, 1)
                steps["pool"] += 1
                pool.wait_ge(pool_step, steps["pool"])
                pool.tensor_tensor(rstd, rstd, neg_half[:, 0:rstd.shape[1]],
                                   ALU.pow).then_inc(done, 1)

            pool.memset(neg_half, -0.5).then_inc(half_set, 1)
            pool.wait_ge(half_set, 1)

            pool.wait_ge(mem_sq, MT)
            rsqrt(small[:, 0:MT], ss_y[:, 0:MT], D, mem_rstd)

            def x_norm(base):
                for tt in range(TT):
                    pool.wait_ge(x_sq, base + tt + 1)
                    rsqrt(rstd_x[:, tt:tt + 1], ss_x[:, tt:tt + 1], D, x_rstd)

            x_norm(0)
            for i in range(2 * LAYERS):
                pool.wait_ge(mem_evac, 4 * (i + 1))
                store = (key_store, value_store)[i % 2]
                pool.dma_start(store[i // 2], mem_kv[i]).then_inc(kv_stored, 16)

            for ph in phases:
                if ph.index:
                    pool.wait_ge(x_new, ph.tile)
                row = norm_g[ph.layer, ph.norm_out:ph.norm_out + 1, :]
                pool.dma_start(post_gain[:], row.broadcast_to([P, D])).then_inc(gain_loaded, 16)
                if ph.name == "ab":
                    for t, c in ((0, C_BIAS0), (1, C_BIAS)):
                        pool.dma_start(bias_tab[:, t, :], constants[:, c:c + T]).then_inc(AB["tables"], 16)
                    pool.dma_start(sgu_raw, sgu_w[0].rearrange("g i j -> i g j")).then_inc(AB["tables"], 16)
                    for g in range(SGU_GROUPS):
                        pool.dma_start(sgu_bias[:, g, :], sgu_b[0, g:g + 1, :].broadcast_to([P, P]))\
                            .then_inc(AB["tables"], 16)
                    for kv in range(2):
                        for pair in range(2):
                            for e in range(2):
                                head = 4 * kv + 2 * pair + e
                                pool.dma_start(sink[e * 64:(e + 1) * 64, 2 * kv + pair:2 * kv + pair + 1],
                                               ab_sink[0:1, head:head + 1].broadcast_to([64, 1]))\
                                    .then_inc(AB["tables"], 16)
                    pool.wait_ge(AB["stat_done"], 1)
                    rsqrt(small[:, 12:16], small[:, 8:12], 1.0, AB["ln_rstd"])
                elif ph.name == "gla":
                    for dst, c in ((gmask, C_MASK), (gcum, C_CUM), (gend, C_END)):
                        pool.dma_start(dst, constants[:, c:c + P]).then_inc(GL["tables"], 16)
                    pool.dma_start(gate_raw, c_in[0].rearrange("(k p) n -> p k n", p=P)
                                   [:, :, 3072:3072 + G_RANK]).then_inc(GL["tables"], 16)
                    pool.dma_start(gate_w[0:G_RANK, :], c_gate_w[0]).then_inc(GL["tables"], 16)
                    pool.dma_start(gate_w[G_RANK:G_RANK + 1, :], c_gate_b[0:1, :]).then_inc(GL["tables"], 16)
                    for h in range(G_HEADS):
                        pool.wait_ge(GL["o_sq"], TT * (h + 1))
                        rsqrt(small[:, 4 * (h % 2):4 * (h % 2) + 4], small[:, 8 + 4 * (h % 2):12 + 4 * (h % 2)],
                              G_DV, GL["o_rstd"])
                elif ph.name == "xattn":
                    if ph.nth == 0:
                        pool.wait_ge(kv_stored, 16 * 2 * LAYERS)
                    pool.dma_start(xk.rearrange("p a b -> p (a b)"), key_store[ph.layer]).then_inc(XA["kv_loaded"], 16)
                    pool.dma_start(xv.rearrange("p a b -> p (a b)"), value_store[ph.layer]).then_inc(XA["kv_loaded"], 16)
                for tt in range(TT):
                    pool.wait_ge(y_sq, ph.tile + tt + 1)
                    rsqrt(rstd_y[:, tt:tt + 1], ss_y[:, tt:tt + 1], D, y_rstd,
                          4.0 if ph.name == "ffn" else 1.0)
                    if ph.index < LAST:
                        pool.wait_ge(x_sq, ph.tile + TT + tt + 1)
                        rsqrt(rstd_x[:, tt:tt + 1], ss_x[:, tt:tt + 1], D, x_rstd)

        @block.scalar
        def _(act):
            def split_high(u, more=0):
                if isinstance(more, int) and u >= UNITS:
                    return
                act.wait_ge(raw_landed[u % RAW], landed(u) + 16 * more)
                if u >= RING:
                    act.wait_ge(unit_used, u - RING + 1 + more)
                act.activation(high_weights[:, u % RING, :], raw_weights[:, u % RAW, :], ACT.Copy)\
                   .then_inc(high_done, 1)

            def square_x(base, tt):
                act.activation(square_junk[:], x_res[:, tt, :], ACT.Square,
                               accum_out=ss_x[:, tt:tt + 1]).then_inc(x_sq, 1)

            def operand_high_of(ph, tt):
                act.wait_ge(x_turned, ph.tile + tt + 1)
                for kt in range(KT):
                    last = act.activation(operand_high[:, kt, tt * P:(tt + 1) * P],
                                          token_banks(tt)[:, kt * P:(kt + 1) * P], ACT.Copy,
                                          scale=gain_col(ph.layer, ph.norm_in, kt))
                last.then_inc(x_high, 1)

            def boundary(ph):
                nxt = phases[ph.index + 1] if ph.index < LAST else None
                for tt in range(TT):
                    if nxt and tt == TT - 1:
                        split_high(nxt.unit + 1)
                    act.wait_ge(y_done, ph.tile + tt + 1)
                    if nxt and tt:
                        act.wait_ge(x_sq, nxt.tile + tt)
                    elif tt:
                        act.wait_ge(y_sq, ph.tile + tt)
                    act.activation(square_junk[:], token_banks(tt), ACT.Square,
                                   accum_out=ss_y[:, tt:tt + 1]).then_inc(y_sq, 1)
                    if nxt:
                        if tt:
                            operand_high_of(nxt, tt - 1)
                        act.wait_ge(x_new, ph.tile + tt + 1)
                        square_x(nxt.tile, tt)
                if nxt:
                    operand_high_of(nxt, TT - 1)

            act.wait_ge(table_loaded, 80)
            for k in range(CREDIT):
                act.activation(credit[:, k:k + 1], identity[:, k:k + 1], ACT.Copy).then_inc(silu_done, 1)
            act.wait_ge(mem_loaded, 16)
            for mt in range(MT):
                if mt:
                    act.wait_ge(mem_sq, mt)
                act.activation(square_junk[:], mem_nat[:, mt, :], ACT.Square,
                               accum_out=ss_y[:, mt:mt + 1]).then_inc(mem_sq, 1)
            act.wait_ge(gains_turned, 1)
            act.activation(gain_cols[:], banks[:, 7, 0:GAIN_ROWS], ACT.Copy).then_inc(gains_ready, 1)
            act.wait_ge(gains_ready, 1)
            for mt in range(MT):
                act.wait_ge(mem_turned, mt + 1)
                for layer in range(LAYERS):
                    for kt in range(KT):
                        c = layer * MEM + mt * P
                        last = act.activation(operand_high[:, kt, c:c + P],
                                              token_banks(mt)[:, kt * P:(kt + 1) * P], ACT.Copy,
                                              scale=gain_col(layer, 4, kt))
                last.then_inc(mem_high, 1)
            for u in range(AHEAD):
                split_high(u)
            act.wait_ge(x_loaded, 16)
            act.wait_ge(mem_sq, MT)
            for tt in range(TT):
                if tt:
                    act.wait_ge(x_sq, tt)
                square_x(0, tt)
            for u in range(8 * LAYERS):
                split_high(u + AHEAD)
                act.wait_ge(unit_used, u + 1)
                i, half = divmod(u, 4)
                src = banks[:, u % 4 + 4 * (u // 8), :].rearrange("p (a n) -> p a n", a=2)
                if i % 2 == 0:
                    dst = mem_kv[i].rearrange("p (a n) -> p a n", a=KT)[:, 2 * half:2 * half + 2, :]
                else:
                    dst = mem_kv[i].rearrange("p (a n) -> p a n", a=MT)[:, :, half * MEM:(half + 1) * MEM]
                act.activation(dst, src, ACT.Copy).then_inc(mem_evac, 1)
                if u in (8, 9):
                    operand_high_of(phases[0], u - 8)
            operand_high_of(phases[0], 2)
            operand_high_of(phases[0], 3)

            def ffn(ph):
                n0, u = ph.nth * FC, ph.unit
                with act.Fori(0, FC // RING) as it:
                    for k in range(RING):
                        split_high(u + k + AHEAD, it * RING)
                        act.wait_ge(gate_done, n0 + k + 1 + it * RING)
                        act.wait_ge(hidden_done, CREDIT + n0 + k - 1 + it * RING)
                        act.activation(silu[:, k % 2, :], banks[:, 2 * k, :], ACT.Silu)\
                           .then_inc(silu_done, 1)
                u += FC
                def pair(k, more=0):
                    if isinstance(more, int):
                        src = hidden[:, 2 * (k + more):2 * (k + more) + 2, :]
                    else:
                        src = hidden[:, bass.ds(more * 2 + 2 * k, 2), :]
                    act.activation(operand_high[:, 2 * (k % 4):2 * (k % 4) + 2, :], src, ACT.Copy)\
                       .then_inc(act_high, 1)
                for k in range(AHEAD):
                    act.wait_ge(chunks_read, 2 * (n0 + FC - 1) + k + 1)
                    pair(k)
                act.wait_ge(unit_used, u)
                act.wait_ge(hidden_done, CREDIT + n0 + FC)
                with act.Fori(0, FC // 2 // RING - 1) as it:
                    for k in range(RING):
                        split_high(u + k + AHEAD, it * RING)
                        act.wait_ge(unit_used, u + k + AHEAD - RING + 1 + it * RING)
                        pair(k + AHEAD, it * RING)
                for v in range(FC // 2 - RING, FC // 2 - 1):
                    split_high(u + v + AHEAD)
                    if v + AHEAD < FC // 2:
                        act.wait_ge(unit_used, u + v + AHEAD - RING + 1)
                        pair(v + AHEAD)

            def inputs(ph, count, evac, evacuate):
                for v in range(count):
                    split_high(ph.unit + v + AHEAD)
                    act.wait_ge(unit_used, ph.unit + v + 1)
                    evacuate(v, evac)

            def outputs(ph, start):
                for v in range(start, start + 3):
                    split_high(ph.unit + v + AHEAD)

            def pair_of_banks(b):
                return banks[:, 2 * b:2 * b + 2, :]

            def window(ph):
                def evacuate(v, evac):
                    if v < 2:
                        act.activation(qT.rearrange("p a b -> p (a b)").rearrange(
                                           "p (c j n) -> p j c n", c=NCH, j=4)[:, 2 * v:2 * v + 2, :, :],
                                       pair_of_banks(v).rearrange("p j (c n) -> p j c n", c=NCH),
                                       ACT.Copy).then_inc(evac, 1)
                    elif v == 2:
                        act.activation(kT, banks[:, 4, :], ACT.Copy)
                        act.activation(v_win.rearrange("p a b -> p (a b)")[:, 0:T], banks[:, 5, :], ACT.Copy)
                        act.activation(v_win.rearrange("p a b -> p (a b)")[:, T:7 * P],
                                       banks[:, 6, 0:3 * P], ACT.Copy).then_inc(evac, 1)
                    elif v < 5:
                        act.activation(uT[:, 2 * v - 6:2 * v - 4, :], pair_of_banks(v - 3), ACT.Copy).then_inc(evac, 1)
                    else:
                        act.activation(vg[:, :, (v - 5) * 256:(v - 4) * 256],
                                       pair_of_banks(v - 3).rearrange("p b (t n) -> p (b t) n", n=256),
                                       ACT.Copy).then_inc(evac, 1)
                inputs(ph, 7, AB["in_evac"], evacuate)
                act.wait_ge(AB["sguT_psum"], 1)
                act.activation(sguT.rearrange("p a b -> p (a b)"), banks[:, 6, :], ACT.Copy)\
                   .then_inc(AB["sguT_ready"], 1)
                for g in range(SGU_GROUPS):
                    act.wait_ge(AB["yb_done"], g + 1)
                    act.activation(operand_high[:, 4 + g, :], yb[:, g, :], ACT.Copy).then_inc(AB["yb_high"], 1)
                for c in range(NCH):
                    b = c % 2
                    act.wait_ge(AB["shifted"], c + 1)
                    neg_max, sink_gap, total, sink_exp = (
                        small[:, 32 + 16 * b + 4 * i:36 + 16 * b + 4 * i] for i in range(4))
                    act.activation(sink_exp, sink_gap, ACT.Exp)
                    for g in range(4):
                        last = act.activation(probs[b][:, g, :], probs[b][:, g, :], ACT.Exp,
                                              bias=neg_max[:, g:g + 1], accum_out=total[:, g:g + 1])
                    last.then_inc(AB["exped"], 1)
                    act.wait_ge(AB["p_turned"], c + 1)
                    act.activation(probsT[b], banks[:, 4 + b, :], ACT.Copy).then_inc(AB["p_evac"], 1)
                    if c:
                        attended(c - 1)
                attended(NCH - 1)
                outputs(ph, 7)

            def attended(c):
                    b = c % 2
                    act.wait_ge(AB["attended"], c + 1)
                    for kv in range(2):
                        rows = slice(kv * 64, kv * 64 + 64)
                        last = act.activation(
                            operand_high[rows, 0:4, c * CHUNK:(c + 1) * CHUNK],
                            banks[rows, 6 + b, kv * 256:(kv + 1) * 256].rearrange("p (j q) -> p j q", j=4),
                            ACT.Copy)
                    last.then_inc(AB["out_high"], 1)

            def gated(ph):
                u = ph.unit

                def squares(h, tiles):
                    for tt in tiles:
                        act.wait_ge(GL["o_done"], h * TT + tiles[-1] + 1)
                        if h + tt:
                            act.wait_ge(GL["o_sq"], h * TT + tt)
                        ss = small[:, 8 + 4 * (h % 2) + tt:9 + 4 * (h % 2) + tt]
                        act.activation(square_junk[:, 0:G_DV],
                                       banks[:, 5 + tt // 2, 256 * (tt % 2):256 * (tt % 2) + 256],
                                       ACT.Square, accum_out=ss).then_inc(GL["o_sq"], 1)

                def z_copy(tt):
                    act.wait_ge(GL["z_done"], tt + 1)
                    act.activation(loga[:, tt, :], banks[:, 6 + tt % 2, :], ACT.Copy).then_inc(GL["z_copied"], 1)

                act.wait_ge(GL["g_done"], 1)
                act.wait_ge(GL["cleared"], 1)
                act.activation(g_nat[:, :, 0:G_RANK],
                               banks[:, 6, 0:TT * G_RANK].rearrange("p (t n) -> p t n", t=TT), ACT.Copy)\
                   .then_inc(GL["g_copied"], 1)
                for v in range(8):
                    split_high(u + v + AHEAD)
                    if v >= 4:
                        h = v - 4
                        act.wait_ge(GL["cum_done"], h + 1)
                        if h:
                            act.wait_ge(GL["kend_turned"], h)
                            act.wait_ge(GL["dec_done"], h)
                        act.activation(exps[0], banks[:, 6, :], ACT.Exp)
                        act.activation(exps[1], banks[:, 6, :], ACT.Exp, scale=-1.0)
                        act.activation(exps[2], banks[:, 7, :], ACT.Exp).then_inc(GL["exp_done"], 1)
                    if v == 2:
                        act.wait_ge(GL["g_turned"], 1)
                        act.activation(gT, banks[:, 7, :], ACT.Copy).then_inc(GL["gT_ready"], 1)
                    if v == 3:
                        z_copy(0)
                        z_copy(1)
                    act.wait_ge(unit_used, u + v + 1)
                    if v < 2:
                        act.wait_ge(unit_used, u + 2)
                    src = pair_of_banks(v % 3)
                    if v < 4:
                        act.activation((gq, gk)[v // 2][:, 2 * (v % 2):2 * (v % 2) + 2, :], src, ACT.Copy)\
                           .then_inc(GL["in_evac"], 1)
                    else:
                        act.activation(gv[:, :, (v - 4) * 256:(v - 3) * 256],
                                       src.rearrange("p b (t n) -> p (b t) n", n=256), ACT.Copy)\
                           .then_inc(GL["in_evac"], 1)
                    if v == 3:
                        z_copy(2)
                        z_copy(3)
                        for tt in range(TT):
                            act.wait_ge(GL["z_abs"], tt + 1)
                            act.activation(z_tmp[tt % 2], z_tmp[tt % 2], ACT.Exp, scale=-1.0).then_inc(act_step, 1)
                            steps["act"] += 1
                            act.wait_ge(act_step, steps["act"])
                            act.activation(z_tmp[tt % 2], z_tmp[tt % 2], ACT.Ln, bias=1.0).then_inc(GL["z_log"], 1)
                    if v >= 4:
                        act.wait_ge(GL["kend_turned"], h + 1)
                        act.activation(loga[:, :, h * P:(h + 1) * P],
                                       banks[:, 6, :].rearrange("p (t n) -> p t n", t=TT), ACT.Copy)\
                           .then_inc(GL["kend_ready"], 1)
                for h in range(G_HEADS):
                    v = 8 + h
                    split_high(u + v + AHEAD)
                    act.wait_ge(GL["r_done"], h + 1)
                    act.activation(gr[:, 2 * h, :], banks[:, 0, :], ACT.Silu).then_inc(GL["in_evac"], 1)
                    if h:
                        squares(h - 1, (2, 3))
                    act.wait_ge(unit_used, u + v + 1)
                    act.activation(gr[:, 2 * h + 1, :], banks[:, 1, :], ACT.Silu).then_inc(GL["in_evac"], 1)
                    squares(h, (0, 1))
                squares(G_HEADS - 1, (2, 3))
                for c in range(KT):
                    act.wait_ge(GL["y_ready"], c + 1)
                    act.activation(operand_high[:, c, :], gr[:, c, :], ACT.Copy).then_inc(GL["out_high"], 1)
                outputs(ph, 12)

            def cross(ph):
                base = 4 * ph.nth
                def evacuate(v, evac):
                    act.activation(xq[:, 2 * v:2 * v + 2, :], pair_of_banks(v), ACT.Copy).then_inc(evac, 1)
                for v in range(4):
                    split_high(ph.unit + v + AHEAD)
                    act.wait_ge(unit_used, ph.unit + v + 1)
                    evacuate(v, XA["in_evac"])
                for tt in range(TT):
                    b = tt % 2
                    neg_max, total = small[:, 8 * b:8 * b + 4], small[:, 8 * b + 4:8 * b + 8]
                    act.wait_ge(XA["maxed"], base + tt + 1)
                    if base + tt >= 2:
                        act.wait_ge(XA["p_turned"], base + tt - 1)
                    for h in range(X_HEADS):
                        last = act.activation(xp[b][:, h, :], token_banks(tt)[:, h * MEM:(h + 1) * MEM], ACT.Exp,
                                              bias=neg_max[:, h:h + 1], scale=(D // X_HEADS) ** -0.5,
                                              accum_out=total[:, h:h + 1])
                    last.then_inc(XA["exped"], 1)
                    if tt:
                        cross_turned(base, tt - 1)
                cross_turned(base, TT - 1)
                for j in range(KT):
                    act.wait_ge(XA["attended"], 8 * ph.nth + j + 1)
                    act.activation(operand_high[:, j, :], banks[:, j, :], ACT.Copy).then_inc(XA["out_high"], 1)
                outputs(ph, 4)

            def cross_turned(base, tt):
                act.wait_ge(XA["p_turned"], base + tt + 1)
                act.activation(xpT[:, :, tt * P:(tt + 1) * P],
                               token_banks(tt).rearrange("p (a n) -> p a n", a=KT), ACT.Copy)\
                   .then_inc(XA["p_evac"], 1)

            for ph in phases:
                {"ffn": ffn, "ab": window, "gla": gated, "xattn": cross}[ph.name](ph)
                boundary(ph)

        @block.vector
        def _(dve):
            def step(instruction):
                instruction.then_inc(dve_step, 1)
                steps["dve"] += 1
                dve.wait_ge(dve_step, steps["dve"])

            def split_low(u, more=0):
                if isinstance(more, int) and u >= UNITS:
                    return
                dve.wait_ge(high_done, u + 1 + more)
                dve.tensor_tensor(low_weights[:, u % RING, :], raw_weights[:, u % RAW, :],
                                  high_weights[:, u % RING, :].bitcast(F32), ALU.subtract)\
                   .then_inc(low_done, 1)

            def scale_x(ph, tt):
                dve.wait_ge(x_rstd, ph.tile + tt + 1)
                dve.tensor_scalar(scaled[:, tt, :], x_res[:, tt, :], rstd_x[:, tt:tt + 1], None,
                                  ALU.mult).then_inc(x_scaled, 1)

            def operand_low_of(ph, tt):
                dve.wait_ge(x_high, ph.tile + tt + 1)
                for kt in range(KT):
                    cols = slice(tt * P, (tt + 1) * P)
                    last = dve.scalar_tensor_tensor(
                        operand_low[:, kt, cols], token_banks(tt)[:, kt * P:(kt + 1) * P],
                        gain_col(ph.layer, ph.norm_in, kt), operand_high[:, kt, cols].bitcast(F32),
                        ALU.mult, ALU.subtract)
                last.then_inc(x_low, 1)

            def boundary(ph):
                nxt = phases[ph.index + 1] if ph.index < LAST else None
                dve.wait_ge(gain_loaded, 16 * (ph.index + 1))
                for tt in range(TT):
                    if nxt and tt == TT - 1:
                        split_low(nxt.unit + 1)
                    dve.wait_ge(y_rstd, ph.tile + tt + 1)
                    step(dve.scalar_tensor_tensor(token_banks(tt), token_banks(tt), rstd_y[:, tt:tt + 1],
                                                  post_gain[:], ALU.mult, ALU.mult))
                    dve.tensor_tensor(x_res[:, tt, :], token_banks(tt), x_res[:, tt, :], ALU.add)\
                       .then_inc(x_new, 1)
                    if nxt:
                        if tt:
                            operand_low_of(nxt, tt - 1)
                        scale_x(nxt, tt)
                if nxt:
                    operand_low_of(nxt, TT - 1)

            for k in range(CREDIT):
                dve.memset(credit[:, CREDIT + k:CREDIT + k + 1], 0.0).then_inc(hidden_done, 1)
            for mt in range(MT):
                dve.wait_ge(mem_rstd, 1)
                dve.tensor_scalar(mem_scaled[:, mt, :], mem_nat[:, mt, :], small[:, mt:mt + 1], None,
                                  ALU.mult).then_inc(mem_scaled_done, 1)
            for mt in range(MT):
                dve.wait_ge(mem_high, mt + 1)
                for layer in range(LAYERS):
                    for kt in range(KT):
                        c = slice(layer * MEM + mt * P, layer * MEM + (mt + 1) * P)
                        last = dve.scalar_tensor_tensor(
                            operand_low[:, kt, c], token_banks(mt)[:, kt * P:(kt + 1) * P],
                            gain_col(layer, 4, kt), operand_high[:, kt, c].bitcast(F32),
                            ALU.mult, ALU.subtract)
                last.then_inc(mem_low, 1)
            for u in range(AHEAD):
                split_low(u)
            dve.wait_ge(mem_turned, MT)
            for tt in range(TT):
                scale_x(phases[0], tt)
            for u in range(8 * LAYERS):
                split_low(u + AHEAD)
                if u in (8, 9):
                    operand_low_of(phases[0], u - 8)
            operand_low_of(phases[0], 2)
            operand_low_of(phases[0], 3)
            dve.wait_ge(kv_stored, 16 * 2 * LAYERS)

            def ffn(ph):
                n0, u = ph.nth * FC, ph.unit
                a0 = ph.nth * (FC // 2)

                def hidden_chunk(k, more=0):
                    dve.wait_ge(silu_done, CREDIT + n0 + k + 1 + more)
                    dve.wait_ge(unit_used, ph.unit + k + 1 + more)
                    f = k + more if isinstance(more, int) else bass.ds(more + k, 1)
                    f = slice(f, f + 1) if isinstance(f, int) else f
                    dve.tensor_tensor(hidden[:, f, :], silu[:, k % 2:k % 2 + 1, :],
                                      banks[:, 2 * (k % 4) + 1:2 * (k % 4) + 2, :],
                                      ALU.mult).then_inc(hidden_done, 1)
                with dve.Fori(0, FC // RING - 1) as it:
                    for k in range(RING):
                        split_low(u + k + AHEAD, it * RING)
                        hidden_chunk(k, it * RING)
                for k in range(FC - RING, FC):
                    split_low(u + k + AHEAD)
                    if k < FC - 1:
                        hidden_chunk(k)
                u += FC
                def pair(k, more=0):
                    dve.wait_ge(act_high, a0 + k + 1 + more)
                    if isinstance(more, int):
                        src = hidden[:, 2 * (k + more):2 * (k + more) + 2, :]
                    else:
                        src = hidden[:, bass.ds(more * 2 + 2 * k, 2), :]
                    part_of = slice(2 * (k % 4), 2 * (k % 4) + 2)
                    dve.tensor_tensor(operand_low[:, part_of, :], src,
                                      operand_high[:, part_of, :].bitcast(F32), ALU.subtract)\
                       .then_inc(act_low, 1)
                for k in range(AHEAD):
                    pair(k)
                hidden_chunk(FC - 1)
                with dve.Fori(0, FC // 2 // RING - 1) as it:
                    for k in range(RING):
                        split_low(u + k + AHEAD, it * RING)
                        pair(k + AHEAD, it * RING)
                for v in range(FC // 2 - RING, FC // 2 - 1):
                    split_low(u + v + AHEAD)
                    if v + AHEAD < FC // 2:
                        pair(v + AHEAD)

            def window(ph):
                for v in range(7):
                    split_low(ph.unit + v + AHEAD)
                dve.wait_ge(AB["in_evac"], 7)
                raw_stats, mean_var = small[:, 20:26], small[:, 26:28]
                for tt in range(TT):
                    step(dve.bn_stats(raw_stats, vg[:, tt, :]))
                    step(dve.bn_aggr(mean_var, raw_stats))
                    step(dve.tensor_copy(small[:, 16 + tt:17 + tt], mean_var[:, 0:1]))
                    step(dve.tensor_copy(small[:, 8 + tt:9 + tt], mean_var[:, 1:2]))
                dve.memset(small[:, 28:29], 0.0).then_inc(AB["stat_done"], 1)
                dve.wait_ge(AB["sguT_ready"], 1)
                dve.memset(sguT[64:P, :, 0:64], 0.0).then_inc(AB["masked"], 1)
                dve.wait_ge(AB["ln_rstd"], 1)
                for tt in range(TT):
                    dve.tensor_scalar(vg[:, tt, :], vg[:, tt, :], small[:, 16 + tt:17 + tt],
                                      small[:, 12 + tt:13 + tt], ALU.subtract, ALU.mult)\
                       .then_inc(AB["ln_done"], 1)
                dve.wait_ge(AB["tables"], AB_TABLES)
                for c in range(2):
                    biased(c)
                for g in range(SGU_GROUPS):
                    dve.wait_ge(AB["mixed"], g + 1)
                    step(dve.scalar_tensor_tensor(
                        yb[:, g, :].rearrange("p (t n) -> p t n", t=TT),
                        banks[:, 4 + g, :].rearrange("p (t n) -> p t n", t=TT), sgu_gain(g),
                        sgu_bias[:, g:g + 1, :].broadcast_to([P, TT, P]), ALU.mult, ALU.add))
                    dve.tensor_tensor(yb[:, g, :], yb[:, g, :], uT[:, g, :], ALU.mult).then_inc(AB["yb_done"], 1)
                for g in range(SGU_GROUPS):
                    dve.wait_ge(AB["yb_high"], g + 1)
                    dve.tensor_tensor(operand_low[:, 4 + g, :], yb[:, g, :],
                                      operand_high[:, 4 + g, :].bitcast(F32), ALU.subtract)\
                       .then_inc(AB["out_low"], 1)
                for c in range(NCH):
                    b = c % 2
                    dve.wait_ge(AB["exped"], c + 1)
                    neg_max, sink_gap, total, sink_exp = (
                        small[:, 32 + 16 * b + 4 * i:36 + 16 * b + 4 * i] for i in range(4))
                    step(dve.tensor_tensor(total, total, sink_exp, ALU.add))
                    step(dve.reciprocal(total, total))
                    for g in range(4):
                        last = dve.tensor_scalar(probs[b][:, g, :], probs[b][:, g, :], total[:, g:g + 1],
                                                 None, ALU.mult)
                    last.then_inc(AB["normed"], 1)
                    if c + 2 < NCH:
                        dve.wait_ge(AB["p_turned"], c + 1)
                        biased(c + 2)
                    if c:
                        attended_low(c - 1)
                attended_low(NCH - 1)
                for v in range(7, 10):
                    split_low(ph.unit + v + AHEAD)

            def attended_low(c):
                    b = c % 2
                    dve.wait_ge(AB["out_high"], c + 1)
                    for kv in range(2):
                        rows, cols = slice(kv * 64, kv * 64 + 64), slice(c * CHUNK, (c + 1) * CHUNK)
                        last = dve.tensor_tensor(
                            operand_low[rows, 0:4, cols],
                            banks[rows, 6 + b, kv * 256:(kv + 1) * 256].rearrange("p (j q) -> p j q", j=4),
                            operand_high[rows, 0:4, cols].bitcast(F32), ALU.subtract)
                    last.then_inc(AB["out_low"], 1)

            def biased(c):
                b = c % 2
                neg_max, sink_gap, total, sink_exp = (
                    small[:, 32 + 16 * b + 4 * i:36 + 16 * b + 4 * i] for i in range(4))
                dve.wait_ge(AB["scores"], c + 1)
                step(dve.scalar_tensor_tensor(
                    probs[b].rearrange("p (k n) q -> p k (n q)", k=2), banks[:, 2 * b:2 * b + 2, 0:256],
                    A_DIM ** -0.5, bias_tab[:, min(c, 1), :].rearrange("p (k n) -> p k n", k=2),
                    ALU.mult, ALU.add))
                step(dve.tensor_reduce(neg_max, probs[b], AX.X, ALU.max))
                step(dve.tensor_tensor(neg_max, neg_max, sink, ALU.max))
                step(dve.tensor_tensor(sink_gap, sink, neg_max, ALU.subtract))
                dve.tensor_scalar(neg_max, neg_max, -1.0, None, ALU.mult).then_inc(AB["shifted"], 1)

            def gated(ph):
                step(dve.memset(exp1, 0.0))
                dve.memset(g_nat[:, :, G_RANK:G_RANK + 1], 1.0).then_inc(GL["cleared"], 1)

                def absolute(tt):
                    dve.wait_ge(GL["z_copied"], tt + 1)
                    if tt >= 2:
                        dve.wait_ge(GL["log_ready"], tt - 1)
                    dve.scalar_tensor_tensor(z_tmp[tt % 2], loga[:, tt, :], -1.0, loga[:, tt, :],
                                             ALU.mult, ALU.max).then_inc(GL["z_abs"], 1)

                def decays(h):
                    dve.wait_ge(GL["exp_done"], h + 1)
                    dve.wait_ge(GL["in_evac"], 4)
                    dve.tensor_copy(decay[:, h, :], exps[0].rearrange("p (c n) -> p c n", c=NCH)[:, :, CHUNK - 1])
                    dve.tensor_tensor(exps[2], exps[2], gk[:, h, :], ALU.mult).then_inc(GL["kend_made"], 1)
                    dve.tensor_tensor(gk[:, h, :], gk[:, h, :], exps[1], ALU.mult)
                    dve.scalar_tensor_tensor(gq[:, h, :], gq[:, h, :], G_DK ** -0.5, exps[0], ALU.mult,
                                             ALU.mult).then_inc(GL["dec_done"], 1)

                def mask_scores(h):
                    dve.wait_ge(GL["att_done"], h + 1)
                    dve.copy_predicated(att.rearrange("p (t n) -> p t n", t=TT), mask,
                                        banks[:, 2, :].rearrange("p (t n) -> p t n", t=TT))\
                       .then_inc(GL["att_ready"], 1)

                def make_states(h, chunks):
                    for c in chunks:
                        dve.wait_ge(GL["kv_done"], 2 * h + (1 if c < 4 else 2))
                        if c >= 4:
                            dve.wait_ge(GL["o_done"], h * TT + (c - 3) // 2 + 1)
                        elif h:
                            dve.wait_ge(GL["o_done"], h * TT)
                        half = (c // 2) % 2
                        product = banks[:, 3 + c % 2, half * 256:(half + 1) * 256]
                        if c == 0:
                            dve.tensor_copy(states[:, 1, :], product).then_inc(GL["state_ready"], 1)
                        else:
                            dve.wait_ge(GL["state_ready"], h * (NCH - 1) + c)
                            dve.scalar_tensor_tensor(states[:, (c + 1) % 4, :], states[:, c % 4, :],
                                                     decay[:, h, c:c + 1], product, ALU.mult, ALU.add)\
                               .then_inc(GL["state_ready"], 1)

                def scale_outputs(h):
                    dve.wait_ge(GL["o_rstd"], h + 1)
                    if h:
                        dve.wait_ge(GL["o_turned"], h * TT)
                    for tt in range(TT):
                        dve.tensor_scalar(o_nat[:, tt, :], banks[:, 5 + tt // 2, 256 * (tt % 2):256 * (tt % 2) + 256],
                                          small[:, 4 * (h % 2) + tt:4 * (h % 2) + tt + 1], None, ALU.mult)\
                           .then_inc(GL["o_scaled"], 1)

                def gate_outputs(h):
                    dve.wait_ge(GL["o_turned"], (h + 1) * TT)
                    dve.wait_ge(GL["in_evac"], 8 + 2 * (h + 1))
                    for j, bank in ((0, 7), (1, 2)):
                        c = 2 * h + j
                        dve.scalar_tensor_tensor(gr[:, c, :], banks[:, bank, :], head_gain(c), gr[:, c, :],
                                                 ALU.mult, ALU.mult).then_inc(GL["y_ready"], 1)

                for v in range(8):
                    split_low(ph.unit + v + AHEAD)
                    if v == 3:
                        absolute(0)
                        absolute(1)
                        for tt in range(TT):
                            dve.wait_ge(GL["z_log"], tt + 1)
                            dve.scalar_tensor_tensor(loga[:, tt, :], loga[:, tt, :], 0.0, z_tmp[tt % 2],
                                                     ALU.min, ALU.subtract).then_inc(GL["log_ready"], 1)
                            if tt + 2 < TT:
                                absolute(tt + 2)
                    if v >= 4:
                        decays(v - 4)
                dve.wait_ge(GL["dec_done"], G_HEADS)
                step(dve.memset(att, 0.0))
                mask = gmask.bitcast(U32).unsqueeze(1).broadcast_to([P, TT, P])
                for h in range(G_HEADS):
                    split_low(ph.unit + 8 + h + AHEAD)
                    if h:
                        dve.wait_ge(GL["o_done"], h * TT)
                    mask_scores(h)
                    make_states(h, range(4))
                    if h:
                        scale_outputs(h - 1)
                        gate_outputs(h - 1)
                    make_states(h, range(4, NCH - 1))
                scale_outputs(G_HEADS - 1)
                gate_outputs(G_HEADS - 1)
                for c in range(KT):
                    dve.wait_ge(GL["out_high"], c + 1)
                    dve.tensor_tensor(operand_low[:, c, :], gr[:, c, :],
                                      operand_high[:, c, :].bitcast(F32), ALU.subtract)\
                       .then_inc(GL["out_low"], 1)
                for v in range(12, 15):
                    split_low(ph.unit + v + AHEAD)

            def cross(ph):
                base = 4 * ph.nth
                for v in range(4):
                    split_low(ph.unit + v + AHEAD)
                for tt in range(TT + 1):
                    if tt < TT:
                        b = tt % 2
                        neg_max = small[:, 8 * b:8 * b + 4]
                        dve.wait_ge(XA["scores"], base + tt + 1)
                        step(dve.tensor_reduce(neg_max, token_banks(tt).rearrange("p (h n) -> p h n", h=X_HEADS),
                                               AX.X, ALU.max))
                        dve.tensor_scalar(neg_max, neg_max, -((D // X_HEADS) ** -0.5), None, ALU.mult)\
                           .then_inc(XA["maxed"], 1)
                    if tt:
                        b = (tt - 1) % 2
                        total = small[:, 8 * b + 4:8 * b + 8]
                        dve.wait_ge(XA["exped"], base + tt)
                        step(dve.reciprocal(total, total))
                        for h in range(X_HEADS):
                            last = dve.tensor_scalar(xp[b][:, h, :], xp[b][:, h, :], total[:, h:h + 1], None,
                                                     ALU.mult)
                        last.then_inc(XA["normed"], 1)
                for j in range(KT):
                    dve.wait_ge(XA["out_high"], 8 * ph.nth + j + 1)
                    dve.tensor_tensor(operand_low[:, j, :], banks[:, j, :],
                                      operand_high[:, j, :].bitcast(F32), ALU.subtract)\
                       .then_inc(XA["out_low"], 1)
                for v in range(4, 7):
                    split_low(ph.unit + v + AHEAD)

            for ph in phases:
                {"ffn": ffn, "ab": window, "gla": gated, "xattn": cross}[ph.name](ph)
                boundary(ph)

        @block.tensor
        def _(pe):
            def three(out_, w_high, w_low, a_high, a_low, start, stop):
                pe.matmul(out_, w_high, a_high, start=start, stop=False)
                pe.matmul(out_, w_high, a_low, start=False, stop=False)
                return pe.matmul(out_, w_low, a_high, start=False, stop=stop)

            def column_chunk(u, pick, out_, cols, read=None):
                for kt in range(KT):
                    last = three(out_, pick(high_weights[:, u % RING, :], kt),
                                 pick(low_weights[:, u % RING, :], kt),
                                 operand_high[:, kt, cols], operand_low[:, kt, cols],
                                 kt == 0, kt == KT - 1)
                    if read is not None and kt in (1, 3):
                        last.then_inc(read, 1)
                return last

            def natural(u, out_, tokens, c0, n):
                for kt in range(KT):
                    w = slice(kt * 256 + c0, kt * 256 + c0 + n)
                    last = three(out_, operand_high[:, kt, tokens], operand_low[:, kt, tokens],
                                 high_weights[:, u % RING, w], low_weights[:, u % RING, w],
                                 kt == 0, kt == KT - 1)
                return last

            def block_of(half):
                return lambda slot, kt: slot[:, kt * 256 + half * P:kt * 256 + half * P + P]

            def turn_x(ph, tt, frees_unit=False):
                pe.wait_ge(x_scaled, ph.tile + tt + 1)
                for kt in range(KT):
                    last = pe.transpose(token_banks(tt)[:, kt * P:(kt + 1) * P],
                                        scaled[:, tt, kt * P:(kt + 1) * P], identity[:])
                    if kt == 0 and frees_unit:
                        last.then_inc(unit_used, 1)
                last.then_inc(x_turned, 1)

            def output_unit(u, tt, k, chunk, start, stop):
                rows, slot = slice(tt * P, (tt + 1) * P), u % RING
                halves = [(banks[:, 2 * tt + nh, :], slice(k * D + nh * T, k * D + (nh + 1) * T))
                          for nh in range(2)]
                for bank, w in halves:
                    pe.matmul(bank, operand_high[:, chunk, rows], high_weights[:, slot, w],
                              start=start, stop=False)
                    pe.matmul(bank, operand_high[:, chunk, rows], low_weights[:, slot, w],
                              start=False, stop=False)
                for bank, w in halves:
                    last = pe.matmul(bank, operand_low[:, chunk, rows], high_weights[:, slot, w],
                                     start=False, stop=stop)
                return last

            def last_units(ph, u, chunks, ready=None, base=0):
                nxt = phases[ph.index + 1] if ph.index < LAST else None
                for tt in range(TT):
                    for j, chunk in enumerate(chunks):
                        if tt == 0 and j % 2 == 0:
                            pe.wait_ge(low_done, u + j // 2 + 1)
                        if tt == 0 and ready is not None:
                            pe.wait_ge(ready, base + chunk + 1)
                        last = output_unit(u + j // 2, tt, j % 2, chunk, False, j == 5)
                        if tt == TT - 1 and j in (1, 3):
                            last.then_inc(unit_used, 1)
                    last.then_inc(y_done, 1)
                    if nxt and tt:
                        turn_x(nxt, tt - 1, frees_unit=tt == TT - 1)
                if nxt:
                    first_units(nxt)

            def first_units(ph):
                picks = (block_of(0), block_of(1)) if ph.name != "ffn" else (ffn_gate, ffn_up)
                early, late = slice(0, T // 2), slice(T // 2, T)
                pe.wait_ge(x_low, ph.tile + 2)
                for k in range(2):
                    pe.wait_ge(low_done, ph.unit + k + 1)
                    for half in range(2):
                        column_chunk(ph.unit + k, picks[half], banks[:, 2 * k + half, early], early)
                        if (k, half) == (1, 0):
                            turn_x(ph, TT - 1)
                pe.wait_ge(x_low, ph.tile + TT)
                for k in range(2):
                    for half in range(2):
                        last = column_chunk(ph.unit + k, picks[half], banks[:, 2 * k + half, late], late,
                                            chunks_read if ph.name == "ffn" and half else None)
                        if half:
                            last.then_inc(unit_used, 1)
                        elif ph.name == "ffn":
                            last.then_inc(gate_done, 1)

            def ffn_gate(slot, kt):
                return slot[:, kt * P:(kt + 1) * P]

            def ffn_up(slot, kt):
                return slot[:, (KT + kt) * P:(KT + kt + 1) * P]

            def output_projection(ph, u, ready, base):
                pe.wait_ge(low_done, u + 1)
                for k in range(2):
                    pe.wait_ge(ready, base + k + 1)
                    for tt in range(TT):
                        last = output_unit(u, tt, k, k, k == 0, False)
                last.then_inc(unit_used, 1)
                last_units(ph, u + 1, range(2, 8), ready, base)

            pe.wait_ge(table_loaded, 16 * 5)
            pe.transpose(banks[:, 7, 0:P], gain_rows[:, 0, :], identity[:])
            pe.transpose(banks[:, 7, P:GAIN_ROWS], gain_rows[0:GAIN_ROWS - P, 1, :],
                         identity[0:GAIN_ROWS - P, 0:GAIN_ROWS - P]).then_inc(gains_turned, 1)
            for mt in range(MT):
                pe.wait_ge(mem_scaled_done, mt + 1)
                for kt in range(KT):
                    last = pe.transpose(token_banks(mt)[:, kt * P:(kt + 1) * P],
                                        mem_scaled[:, mt, kt * P:(kt + 1) * P], identity[:])
                last.then_inc(mem_turned, 1)
            pe.wait_ge(mem_low, MT)
            for u in range(8 * LAYERS):
                i, layer, bank = u // 4, u // 8, banks[:, u % 4 + 4 * (u // 8), :]
                pe.wait_ge(low_done, u + 1)
                if u == 8:
                    pe.wait_ge(mem_evac, 8)
                    turn_x(phases[0], 0)
                    turn_x(phases[0], 1)
                if u % 8 >= 4:
                    pe.wait_ge(mem_evac, u - 3)
                for half in range(2):
                    if i % 2 == 0:
                        last = column_chunk(u, block_of(half), bank[:, half * MEM:(half + 1) * MEM],
                                            slice(layer * MEM, (layer + 1) * MEM))
                    else:
                        m = layer * MEM + half * P
                        last = natural(u, bank[:, half * 256:(half + 1) * 256], slice(m, m + P), 0, 256)
                last.then_inc(unit_used, 1)
            pe.wait_ge(mem_evac, 8 * LAYERS)
            turn_x(phases[0], 2)
            first_units(phases[0])

            def ffn(ph):
                n0, u = ph.nth * FC, ph.unit
                all_tokens = slice(0, T)

                def gate_and_up(k, more=0):
                    pe.wait_ge(low_done, u + k + 1 + more)
                    pe.wait_ge(silu_done, CREDIT + n0 + k - RING + 1 + more)
                    column_chunk(u + k, ffn_gate, banks[:, 2 * (k % 4), :], all_tokens).then_inc(gate_done, 1)
                    pe.wait_ge(hidden_done, CREDIT + n0 + k - RING + 1 + more)
                    column_chunk(u + k, ffn_up, banks[:, 2 * (k % 4) + 1, :], all_tokens,
                                 chunks_read).then_inc(unit_used, 1)
                with pe.Fori(0, FC // RING - 1) as it:
                    for k in range(RING):
                        gate_and_up(2 + k, it * RING)
                gate_and_up(FC - 2)
                gate_and_up(FC - 1)
                u += FC
                a0 = ph.nth * (FC // 2)

                def whole(v, more=0, start=False):
                    pe.wait_ge(low_done, u + v + 1 + more)
                    pe.wait_ge(act_low, a0 + v + 1 + more)
                    for k in range(2):
                        for tt in range(TT):
                            if start and k == 0:
                                pe.wait_ge(hidden_done, CREDIT + n0 + FC - TT + tt + 1)
                            last = output_unit(u + v, tt, k, 2 * (v % 4) + k, start and k == 0, False)
                    last.then_inc(unit_used, 1)
                whole(0, start=True)
                with pe.Fori(0, FC // 2 // RING - 1) as it:
                    for k in range(RING):
                        whole(1 + k, it * RING)
                pe.wait_ge(act_low, a0 + FC // 2)
                last_units(ph, u + FC // 2 - 3, range(2, 8))

            def window(ph):
                u = ph.unit
                for v in range(2, 7):
                    pe.wait_ge(low_done, u + v + 1)
                    if v >= 3:
                        pe.wait_ge(AB["in_evac"], min(v - 2, 3))
                    for half in range(2):
                        if v == 2 and half == 0:
                            column_chunk(u + v, block_of(0), banks[:, 4, :], slice(0, T))
                        elif v == 2:
                            for i in range(7):
                                start = i * P if i < 4 else (i - 4) * P + CHUNK
                                last = natural(u + v, banks[:, 5 + i // 4, (i % 4) * P:(i % 4 + 1) * P],
                                               slice(start, start + P), P, P)
                        elif v < 5:
                            last = column_chunk(u + v, block_of(half), banks[:, 2 * (v - 3) + half, :], slice(0, T))
                        else:
                            for tt in range(2 * half, 2 * half + 2):
                                last = natural(u + v, banks[:, 2 * (v - 3) + half, (tt % 2) * 256:(tt % 2 + 1) * 256],
                                               slice(tt * P, (tt + 1) * P), 0, 256)
                    last.then_inc(unit_used, 1)
                pe.wait_ge(AB["tables"], AB_TABLES)
                pe.wait_ge(AB["in_evac"], 7)

                def scores(c):
                    b, k0 = c % 2, max(c - 1, 0) * CHUNK
                    if c >= 2:
                        pe.wait_ge(AB["shifted"], c - 1)
                    for kv in range(2):
                        rows = slice(kv * 64, kv * 64 + 64)
                        for pair in range(2):
                            last = pe.matmul(banks[:, 2 * b + kv, pair * P:(pair + 1) * P],
                                             qT[rows, c // 2, (c % 2) * 256 + pair * P:(c % 2) * 256 + (pair + 1) * P],
                                             kT[rows, k0:k0 + P], start=True, stop=True)
                    last.then_inc(AB["scores"], 1)

                scores(0)
                scores(1)
                for g in range(SGU_GROUPS):
                    last = pe.transpose(banks[:, 6, g * P:(g + 1) * P], sgu_raw[:, g, :], identity[:])
                last.then_inc(AB["sguT_psum"], 1)
                pe.wait_ge(AB["masked"], 1)
                pe.wait_ge(AB["ln_done"], TT)
                for g in range(SGU_GROUPS):
                    for tt in range(TT):
                        last = pe.matmul(banks[:, 4 + g, tt * P:(tt + 1) * P], vg[:, tt, g * P:(g + 1) * P],
                                         sguT[:, g, :], start=True, stop=True)
                    last.then_inc(AB["mixed"], 1)
                pe.wait_ge(AB["yb_done"], SGU_GROUPS)
                for c in range(NCH):
                    b = c % 2
                    pe.wait_ge(AB["normed"], c + 1)
                    if c >= 2:
                        pe.wait_ge(AB["p_evac"], c - 1)
                    for g in range(4):
                        last = pe.transpose(banks[:, 4 + b, g * P:(g + 1) * P], probs[b][:, g, :], identity[:])
                    last.then_inc(AB["p_turned"], 1)
                    if c + 2 < NCH:
                        scores(c + 2)
                    pe.wait_ge(AB["p_evac"], c + 1)
                    if c >= 2:
                        pe.wait_ge(AB["out_low"], SGU_GROUPS + c - 1)
                    tile = max(c - 1, 0)
                    window_of = v_win[:, tile // 2 if tile % 2 == 0 else 4 + tile // 2, :]
                    pe.matmul(banks[:, 6 + b, :], window_of, probsT[b], start=True, stop=True)\
                      .then_inc(AB["attended"], 1)
                pe.wait_ge(AB["out_low"], SGU_GROUPS + NCH)
                output_projection(ph, u + 7, AB["out_low"], 4)

            def gated(ph):
                u = ph.unit

                def gate_inner():
                    pe.wait_ge(GL["tables"], 16 * 6)
                    for tt in range(TT):
                        for kt in range(KT):
                            for k, operand in enumerate((operand_high, operand_low)):
                                last = pe.matmul(banks[:, 6, tt * G_RANK:(tt + 1) * G_RANK],
                                                 operand[:, kt, tt * P:(tt + 1) * P].bitcast(F32),
                                                 gate_raw[:, kt, :], start=kt + k == 0, stop=kt == KT - 1 and k == 1)
                    last.then_inc(GL["g_done"], 1)

                def gate_turn():
                    pe.wait_ge(GL["g_copied"], 1)
                    for tt in range(TT):
                        last = pe.transpose(banks[:, 7, tt * P:(tt + 1) * P], g_nat[:, tt, :], identity[:])
                    last.then_inc(GL["g_turned"], 1)

                def gate_z(tt):
                    pe.wait_ge(GL["gT_ready"], 1)
                    if tt >= 2:
                        pe.wait_ge(GL["z_copied"], tt - 1)
                    pe.matmul(banks[:, 6 + tt % 2, :], gT[0:G_RANK + 1, tt * P:(tt + 1) * P],
                              gate_w[0:G_RANK + 1, :], start=True, stop=True).then_inc(GL["z_done"], 1)

                def sums(h):
                    pe.wait_ge(GL["log_ready"], TT)
                    if h:
                        pe.wait_ge(GL["kend_ready"], h)
                    for bank, table in ((6, gcum), (7, gend)):
                        for tt in range(TT):
                            last = pe.matmul(banks[:, bank, tt * P:(tt + 1) * P],
                                             loga[:, tt, h * P:(h + 1) * P], table, start=True, stop=True)
                    last.then_inc(GL["cum_done"], 1)

                def turn_keys(h):
                    pe.wait_ge(GL["kend_made"], h + 1)
                    for tt in range(TT):
                        last = pe.transpose(banks[:, 6, tt * P:(tt + 1) * P], exps[2][:, tt * P:(tt + 1) * P],
                                            identity[:])
                    last.then_inc(GL["kend_turned"], 1)

                def key_values(h, chunks):
                    for c in chunks:
                        rows, half = slice((c % 2) * 64, (c % 2) * 64 + 64), (c // 2) % 2
                        last = pe.matmul(banks[:, 3 + c % 2, half * 256:(half + 1) * 256],
                                         loga[rows, c // 2, h * P:(h + 1) * P],
                                         gv[rows, c // 2, h * G_DV:(h + 1) * G_DV], start=True, stop=True)
                    last.then_inc(GL["kv_done"], 1)

                def scores(h):
                    pe.wait_ge(GL["dec_done"], h + 1)
                    if h >= 2:
                        pe.wait_ge(GL["y_ready"], 2 * (h - 1))
                    for tt in range(TT):
                        s = slice(tt * P, (tt + 1) * P)
                        last = pe.matmul(banks[:, 2, s], gk[:, h, s], gq[:, h, s], start=True, stop=True)
                    last.then_inc(GL["att_done"], 1)
                    if h:
                        pe.wait_ge(GL["state_ready"], h * (NCH - 1))
                    key_values(h, range(4))

                def outputs_of(h, tiles):
                    pe.wait_ge(GL["att_ready"], h + 1)
                    if h:
                        pe.wait_ge(GL["o_scaled"], h * TT)
                    for tt in tiles:
                        o = banks[:, 5 + tt // 2, (tt % 2) * 256:(tt % 2 + 1) * 256]
                        values = gv[:, tt, h * G_DV:(h + 1) * G_DV]
                        if tt == 0:
                            pe.matmul(o[0:64, :], att[:, 0:64], values, start=True, stop=True)
                            pe.matmul(o[64:P, :], att[:, 64:P], values, start=True, stop=False)
                        else:
                            pe.matmul(o, att[:, tt * P:(tt + 1) * P], values, start=True, stop=False)
                        for c in (2 * tt, 2 * tt + 1):
                            if c == 0:
                                continue
                            pe.wait_ge(GL["state_ready"], h * (NCH - 1) + c)
                            r = slice((c % 2) * 64, (c % 2) * 64 + 64)
                            last = pe.matmul(o[r, :], gq[:, h, c * CHUNK:(c + 1) * CHUNK], states[:, c % 4, :],
                                             start=False, stop=True)
                        last.then_inc(GL["o_done"], 1)

                def turn_outputs(h):
                    pe.wait_ge(GL["o_scaled"], (h + 1) * TT)
                    if h:
                        pe.wait_ge(GL["y_ready"], 2 * h)
                    pe.wait_ge(GL["att_ready"], min(h + 2, G_HEADS))
                    for tt in range(TT):
                        for j, bank in ((0, 7), (1, 2)):
                            last = pe.transpose(banks[:, bank, tt * P:(tt + 1) * P],
                                                o_nat[:, tt, j * P:(j + 1) * P], identity[:])
                        last.then_inc(GL["o_turned"], 1)

                gate_inner()
                after = {
                    (2, 0): lambda: gate_turn(),
                    (2, 1): lambda: (gate_z(0), gate_z(1)),
                    (3, 0): lambda: (gate_z(2), gate_z(3)),
                }
                for h in range(G_HEADS):
                    after[4 + h, 0] = lambda h=h: sums(h)
                    after[4 + h, 1] = lambda h=h: turn_keys(h)
                for v in range(2, 8):
                    pe.wait_ge(low_done, u + v + 1)
                    if v >= 3:
                        pe.wait_ge(GL["in_evac"], v - 2)
                    for half in range(2):
                        bank = banks[:, 2 * (v % 3) + half, :]
                        if v >= 4:
                            for tt in range(2 * half, 2 * half + 2):
                                last = natural(u + v, bank[:, (tt % 2) * 256:(tt % 2 + 1) * 256],
                                               slice(tt * P, (tt + 1) * P), 0, 256)
                        else:
                            last = column_chunk(u + v, block_of(half), bank, slice(0, T))
                        if half:
                            last.then_inc(unit_used, 1)
                        after[v, half]() if (v, half) in after else None
                for h in range(G_HEADS):
                    v = 8 + h
                    pe.wait_ge(low_done, u + v + 1)
                    pe.wait_ge(GL["in_evac"], 7 if h == 0 else 2 * h + 7)
                    column_chunk(u + v, block_of(0), banks[:, 0, :], slice(0, T)).then_inc(GL["r_done"], 1)
                    if h:
                        outputs_of(h - 1, (2, 3))
                    else:
                        pe.wait_ge(GL["in_evac"], 8)
                        pe.wait_ge(GL["kend_ready"], G_HEADS)
                    scores(h)
                    pe.wait_ge(GL["in_evac"], 8 if h == 0 else 2 * h + 8)
                    column_chunk(u + v, block_of(1), banks[:, 1, :], slice(0, T)).then_inc(unit_used, 1)
                    if h:
                        turn_outputs(h - 1)
                    outputs_of(h, (0, 1))
                    pe.wait_ge(GL["state_ready"], h * (NCH - 1) + 4)
                    key_values(h, range(4, NCH - 1))
                outputs_of(G_HEADS - 1, (2, 3))
                turn_outputs(G_HEADS - 1)
                pe.wait_ge(GL["y_ready"], KT)
                output_projection(ph, u + 12, GL["out_low"], 0)

            def cross(ph):
                u, base = ph.unit, 4 * ph.nth
                for v in range(2, 4):
                    pe.wait_ge(low_done, u + v + 1)
                    for half in range(2):
                        last = column_chunk(u + v, block_of(half), banks[:, 2 * v + half, :], slice(0, T))
                    last.then_inc(unit_used, 1)
                pe.wait_ge(XA["in_evac"], base + 4)
                pe.wait_ge(XA["kv_loaded"], 32 * (ph.nth + 1))
                for tt in range(TT):
                    for h in range(X_HEADS):
                        for dc in range(2):
                            last = pe.matmul(token_banks(tt)[:, h * MEM:(h + 1) * MEM],
                                             xq[:, 2 * h + dc, tt * P:(tt + 1) * P], xk[:, 2 * h + dc, :],
                                             start=dc == 0, stop=dc == 1)
                    last.then_inc(XA["scores"], 1)
                for tt in range(TT):
                    pe.wait_ge(XA["normed"], base + tt + 1)
                    for h in range(X_HEADS):
                        for mc in range(2):
                            i = 2 * h + mc
                            last = pe.transpose(token_banks(tt)[:, i * P:(i + 1) * P],
                                                xp[tt % 2][:, h, mc * P:(mc + 1) * P], identity[:])
                    last.then_inc(XA["p_turned"], 1)
                pe.wait_ge(XA["p_evac"], base + 4)
                for j in range(KT):
                    for mc in range(MT):
                        last = pe.matmul(banks[:, j, :], xv[:, mc, j * P:(j + 1) * P], xpT[:, 2 * (j // 2) + mc, :],
                                         start=mc == 0, stop=mc == MT - 1)
                    last.then_inc(XA["attended"], 1)
                pe.wait_ge(XA["out_low"], 8 * (ph.nth + 1))
                output_projection(ph, u + 4, XA["out_low"], 8 * ph.nth)

            for ph in phases:
                {"ffn": ffn, "ab": window, "gla": gated, "xattn": cross}[ph.name](ph)


_INS = ["x", "mem", "norm_g", "ffn1_w_in", "ffn1_w_out", "ffn2_w_in", "ffn2_w_out", "xattn_w_q",
        "xattn_w_kv", "xattn_w_o", "ab_w_in", "ab_sink", "ab_sgu_w", "ab_sgu_b", "ab_sgu_norm_g",
        "ab_w_out", "c_w_in", "c_gate_w", "c_gate_b", "c_head_norm_g", "c_w_out"]


def build(nc, shapes, stop=None):
    args = [nc.dram_tensor(f"in_{name}_dram", shape, F32, kind="ExternalInput").ap()
            for name, shape in shapes]
    result = nc.dram_tensor("out_0_dram", (1, T, D), F32, kind="ExternalOutput").ap()
    trunk_kernel(nc, *args, result, stop=stop)


def kernel(**inputs):
    import concourse.bacc as bacc
    from concourse.bass_utils import run_bass_kernel_spmd

    arrays = {f"in_{name}_dram": np.ascontiguousarray(inputs[name]) for name in _INS}
    arrays["in_constants_dram"] = constant_table()
    nc = bacc.Bacc("TRN2", target_bir_lowering=False, num_devices=1)
    build(nc, [(n[3:-5], a.shape) for n, a in arrays.items()])
    return run_bass_kernel_spmd(nc, [arrays], core_ids=[0]).results[0]["out_0_dram"]
```

```python
from contextlib import ExitStack

import numpy as np

import concourse.bass as bass
from concourse import mybir

F32 = mybir.dt.float32
F32R = mybir.dt.float32r
BF16 = mybir.dt.bfloat16
U32 = mybir.dt.uint32
ALU = mybir.AluOpType
ACT = mybir.ActivationFunctionType
AX = mybir.AxisListType

P = 128
D = 1024
KT = D // P
T = 512
TT = T // P
MEM = 256
MT = MEM // P
FF = 4 * D
FC = FF // P
LAYERS = 2
NORMS = 9
EPS = 1e-6
CHUNK = 64
NCH = T // CHUNK
UNIT = 2048
RING = 4
RAW = 2
AHEAD = 2
A_HEADS, A_DIM = 8, 64
SGU_GROUPS = 4
G_HEADS, G_DK, G_DV = 4, 128, 256
G_RANK = 16
X_HEADS = 4
NEG = -1e30
CREDIT = RING
GAIN_ROWS = LAYERS * NORMS * KT + SGU_GROUPS + KT

C_ID, C_CUM, C_END, C_MASK, C_BIAS0, C_BIAS = 0, 128, 256, 384, 512, 1024
C_ALL = 1536


def constant_table():
    c = np.zeros((P, C_ALL), np.float32)
    row, col = np.arange(P)[:, None], np.arange(P)[None, :]
    same = row // CHUNK == col // CHUNK
    c[:, C_ID:C_ID + P] = row == col
    c[:, C_CUM:C_CUM + P] = (same & (row <= col)) / 16.0
    c[:, C_END:C_END + P] = (same & (row > col)) / 16.0
    c[:, C_MASK:C_MASK + P] = same & (row <= col)
    slopes = (2.0 ** (-8.0 * np.arange(1, A_HEADS + 1) / A_HEADS)).astype(np.float32)
    q = np.arange(P) % CHUNK
    for kv in range(2):
        for pair in range(2):
            group = 2 * kv + pair
            head = 4 * kv + 2 * pair + np.arange(P) // CHUNK
            dist = np.abs(q[:, None] + CHUNK - np.arange(P)[None, :]).astype(np.float32)
            c[:, C_BIAS + group * P:C_BIAS + (group + 1) * P] = -slopes[head][:, None] * dist
            first = np.abs(q[:, None] - np.arange(P)[None, :]).astype(np.float32)
            bias = np.where(np.arange(P)[None, :] < CHUNK, -slopes[head][:, None] * first, NEG)
            c[:, C_BIAS0 + group * P:C_BIAS0 + (group + 1) * P] = bias
    return c


class Phase:

    def __init__(self, name, unit, norm_in, norm_out, layer, index, nth):
        self.name, self.unit, self.norm_in, self.norm_out = name, unit, norm_in, norm_out
        self.layer, self.index = layer, index
        self.tile = TT * index
        self.nth = nth


def trunk_kernel(nc, x_in, mem_in, norm_g, f1_in, f1_out, f2_in, f2_out, xq_w, xkv_w, xo_w,
                 ab_in, ab_sink, sgu_w, sgu_b, sgu_g, ab_out, c_in, c_gate_w, c_gate_b,
                 c_head_g, c_out, constants, out):
    phases = []
    unit = LAYERS * 8
    for layer in range(LAYERS):
        mixer = ("ab", 7 + 4) if layer % 2 == 0 else ("gla", 12 + 4)
        for name, n, pre, post in (("ffn", 48, 0, 1), (*mixer, 2, 3), ("xattn", 8, 5, 6),
                                   ("ffn", 48, 7, 8)):
            nth = sum(ph.name == name for ph in phases)
            phases.append(Phase(name, unit, pre, post, layer, len(phases), nth))
            unit += n
    UNITS = unit
    LAST = len(phases) - 1

    with ExitStack() as ctx:
        def sb(name, shape, dt=F32):
            return ctx.enter_context(nc.sbuf_tensor(name, shape, dt))

        def sem(name):
            return ctx.enter_context(nc.semaphore(name))

        x_res = sb("x_res", [P, TT, D])
        operand_high = sb("operand_high", [P, KT, T], F32R)
        operand_low = sb("operand_low", [P, KT, T], F32R)
        hidden = sb("hidden", [P, FC, T])
        raw_weights = sb("raw_weights", [P, RAW, UNIT])
        high_weights = sb("high_weights", [P, RING, UNIT], F32R)
        low_weights = sb("low_weights", [P, RING, UNIT], F32R)
        post_gain = sb("post_gain", [P, D])
        silu_buf = sb("silu_buf", [P, D])
        square_junk = sb("square_junk", [P, D], BF16)
        identity = sb("identity", [P, P])
        gain_cols = sb("gain_cols", [P, GAIN_ROWS])
        stats = sb("stats", [P, 128])
        gate_parts = sb("gate_parts", [P, 2, KT, G_RANK], F32R)
        ss_y, ss_x = stats[:, 0:4], stats[:, 4:8]
        rstd_y, rstd_x, neg_half = stats[:, 12:16], stats[:, 16:20], stats[:, 20:24]
        credit = sb("credit", [P, 2 * CREDIT])
        small = stats[:, 24:128]
        banks = ctx.enter_context(nc.psum_tensor("banks", [P, 8, T], F32))
        silu = silu_buf[:].rearrange("p (b n) -> p b n", b=2)

        flat = hidden[:].rearrange("p c n -> p (c n)")
        scaled = flat[:, 0:TT * D].rearrange("p (t n) -> p t n", t=TT)

        def parts(start, *sizes):
            found = []
            for size in sizes:
                n = size if isinstance(size, int) else size[0] * size[1]
                a = flat[:, start:start + n]
                found.append(a if isinstance(size, int) else a.rearrange("p (a b) -> p a b", a=size[0]))
                start += n
            assert start <= FC * T, start
            return found

        mem_nat, mem_scaled = parts(0, (MT, D), (MT, D))
        gain_rows, *mem_kv = parts(2 * MT * D, (2, P), *[KT * MEM] * (2 * LAYERS))
        (qT, uT, vg, kT, v_win, probs0, probs1, probsT0, probsT1, bias_tab, sgu_raw, sguT, sgu_bias,
         yb, kept, sink) = parts(0, (4, T), (4, T), (TT, T), T, (7, P), (4, P), (4, P), T, T, (2, T),
                                 (4, P), (4, P), (4, P), (4, T), (4, T), 4)
        probs, probsT = (probs0, probs1), (probsT0, probsT1)
        vT = yb[:, 0, :]
        (gq, gk, gr, gv, loga, exp0, exp1, exp2, gmask, gcum, gend, decay) = parts(
            0, (G_HEADS, T), (G_HEADS, T), (KT, T), (TT, D), (TT, T), T, T, T, P, P, P,
            (G_HEADS, NCH))
        exps = (exp0, exp1, exp2)
        gate_raw = silu_buf[:, 0:KT * G_RANK].rearrange("p (k n) -> p k n", k=KT)
        gate_w = silu_buf[:, P:P + T]
        gate_high, gate_low = gate_parts[:, 0], gate_parts[:, 1]
        gT, z_tmp = exp0, gr[:, 0:TT, :]
        states = silu_buf[:].rearrange("p (s n) -> p s n", s=4)
        att = exp0
        o_nat = parts(TT * D + 2 * TT * D + TT * T + T, (TT, G_DV))[0]
        xq, xk, xv, xp0, xp1, xpT = parts(0, (KT, T), (KT, MEM), (MT, D), (TT, MEM),
                                          (TT, MEM), (KT, T))
        xp = (xp0, xp1)

        key_store = nc.dram_tensor("key_store", (LAYERS, P, KT * MEM), F32, kind="Internal").ap()
        value_store = nc.dram_tensor("value_store", (LAYERS, P, MT * D), F32, kind="Internal").ap()

        raw_landed = [sem(f"raw_landed{i}") for i in range(RAW)]
        high_done, low_done, unit_used = sem("high_done"), sem("low_done"), sem("unit_used")
        x_loaded, mem_loaded, mem_loaded_too, table_loaded, out_stored = (
            sem("x_loaded"), sem("mem_loaded"), sem("mem_loaded_too"), sem("table_loaded"), sem("out_stored"))
        half_set = sem("half_set")
        gains_turned, gains_ready = sem("gains_turned"), sem("gains_ready")
        mem_sq, mem_rstd, mem_scaled_done, mem_turned = (
            sem("mem_sq"), sem("mem_rstd"), sem("mem_scaled_done"), sem("mem_turned"))
        mem_high, mem_low, mem_evac, kv_stored = (
            sem("mem_high"), sem("mem_low"), sem("mem_evac"), sem("kv_stored"))
        pool_step, dve_step, act_step = sem("pool_step"), sem("dve_step"), sem("act_step")
        steps = {"pool": 0, "dve": 0, "act": 0}
        y_done, y_sq, y_rstd, x_new, gain_loaded = (
            sem("y_done"), sem("y_sq"), sem("y_rstd"), sem("x_new"), sem("gain_loaded"))
        x_sq, x_rstd, x_scaled, x_turned, x_high, x_low = (
            sem("x_sq"), sem("x_rstd"), sem("x_scaled"), sem("x_turned"), sem("x_high"), sem("x_low"))
        gate_done, chunks_read, silu_done, hidden_done, act_high, act_low = (
            sem("gate_done"), sem("chunks_read"), sem("silu_done"), sem("hidden_done"), sem("act_high"),
            sem("act_low"))
        AB = {n: sem("ab_" + n) for n in (
            "in_evac", "tables", "v_turned", "v_ready", "masked", "stat_done", "ln_rstd", "ln_done", "sguT_psum",
            "sguT_ready", "mixed", "yb_done", "scores", "shifted", "exped",
            "normed", "p_turned", "p_evac", "attended", "kept", "out_high", "out_low")}
        GL = {n: sem("gla_" + n) for n in (
            "in_evac", "tables", "cleared", "gate_high", "gate_low", "g_done", "gT_ready",
            "z_done", "z_copied", "r_done", "z_abs", "z_log", "log_ready", "cum_done", "exp_done", "dec_done",
            "kend_made", "kend_turned", "kend_ready", "att_done", "att_ready", "kv_done", "state_ready", "o_done",
            "o_sq", "o_rstd", "o_scaled", "o_turned", "y_ready", "out_high", "out_low")}
        XA = {n: sem("x_att_" + n) for n in (
            "kv_loaded", "in_evac", "scores", "maxed", "exped", "normed", "p_turned",
            "p_evac", "attended", "out_high", "out_low")}
        block = ctx.enter_context(nc.Block())

        in_pieces = {ph.unit + i for ph in phases if ph.name == "ab" for i in (0, 1, 9, 10)}

        def landed(u):
            return sum(64 if v in in_pieces else 32 for v in range(u % RAW, u + 1, RAW))

        AB_TABLES = 16 * (2 + 1 + SGU_GROUPS + A_HEADS)

        def gain_col(layer, norm, kt):
            c = (layer * NORMS + norm) * KT + kt
            return gain_cols[:, c:c + 1]

        def sgu_gain(g):
            c = LAYERS * NORMS * KT + g
            return gain_cols[:, c:c + 1]

        def head_gain(c):
            c += LAYERS * NORMS * KT + SGU_GROUPS
            return gain_cols[:, c:c + 1]

        def head_banks(h):
            b = (0, 2, 6, 4)[h]
            return banks[:, b:b + 2, :].rearrange("p b n -> p (b n)")

        def token_banks(tt):
            return banks[:, 2 * tt:2 * tt + 2, :].rearrange("p b n -> p (b n)")

        @block.sync
        def _(sp):
            sp.dma_start(mem_nat[:, 0, :], mem_in[0, 0:P, :]).then_inc(mem_loaded, 16)
            sp.dma_start(identity[:], constants[:, C_ID:C_ID + P]).then_inc(table_loaded, 16)
            rows = norm_g.rearrange("l k (c p) -> (l k c) p", p=P)
            n = LAYERS * NORMS * KT
            sp.dma_start(gain_rows[:, 0, :], rows[0:P, :]).then_inc(table_loaded, 16)
            sp.dma_start(gain_rows[0:n - P, 1, :], rows[P:n, :]).then_inc(table_loaded, 16)
            sp.dma_start(gain_rows[n - P:n - P + SGU_GROUPS, 1, :],
                         sgu_g[0].rearrange("(g p) -> g p", p=P)).then_inc(table_loaded, 16)
            sp.dma_start(gain_rows[n - P + SGU_GROUPS:GAIN_ROWS - P, 1, :],
                         c_head_g[0].rearrange("(g p) -> g p", p=P)).then_inc(table_loaded, 16)
            sp.dma_start(mem_nat[:, 1, :], mem_in[0, P:2 * P, :]).then_inc(mem_loaded_too, 16)

            def load(u, first, second, more=0):
                if u >= RAW:
                    sp.wait_ge(low_done, u - RAW + 1 + more)
                slot = raw_weights[:, u % RAW, :]
                for (dst, src) in (first(slot), second(slot)):
                    sp.dma_start(dst, src).then_inc(raw_landed[u % RAW], 16)

            def columns(u, w, c0):
                src = w.rearrange("(k p) n -> p k n", p=P)[:, :, c0:c0 + 2 * P]
                h = KT // 2
                grid = lambda slot: slot.rearrange("p (k n) -> p k n", k=KT)
                load(u, lambda s: (grid(s)[:, 0:h, :], src[:, 0:h, :]),
                     lambda s: (grid(s)[:, h:KT, :], src[:, h:KT, :]))

            def rows_of(u, w, r0, more=0, step=0):
                def half(k):
                    start = r0 + k * P + step
                    src = w[start:start + P, :] if isinstance(start, int) else w[bass.ds(start, P), :]
                    return lambda s: (s[:, k * D:(k + 1) * D], src)
                load(u, half(0), half(1), more)

            for layer in range(LAYERS):
                for i in range(8):
                    columns(8 * layer + i, xkv_w[layer], 256 * i)
                    if layer == 0 and i == 1:
                        sp.dma_start(x_res[:], x_in[0].rearrange("(t p) n -> p t n", p=P))\
                          .then_inc(x_loaded, 16)
            for ph in phases:
                u = ph.unit
                if ph.name == "ffn":
                    w_in, w_out = ((f1_in, f1_out), (f2_in, f2_out))[ph.nth % 2]
                    src = w_in[ph.layer].rearrange("(k p) (two n) -> p k two n", p=P, two=2)
                    grid = lambda slot, h: slot.rearrange("p (h k n) -> p h k n", h=2, k=KT)[:, h]
                    with sp.Fori(0, FC // RING) as it:
                        for k in range(RING):
                            c = it * (RING * P) + k * P
                            load(u + k, lambda s: (grid(s, 0), src[:, :, 0, bass.ds(c, P)]),
                                 lambda s: (grid(s, 1), src[:, :, 1, bass.ds(c, P)]), it * RING)
                    u += FC
                    with sp.Fori(0, FC // 2 // RING) as it:
                        for k in range(RING):
                            rows_of(u + k, w_out[ph.layer], 2 * P * k, it * RING, it * (RING * 2 * P))
                elif ph.name == "ab":
                    w = ab_in[0].rearrange("(k p) n -> p k n", p=P)
                    for i in range(2):
                        sp.wait_ge(low_done, u + i - RAW + 1)
                        slot = raw_weights[:, (u + i) % RAW, :].rearrange("p (k h n) -> p k h n", k=KT, h=4)
                        for h in range(2):
                            for kv in range(2):
                                c = (4 * kv + 2 * i + h) * A_DIM
                                sp.dma_start(slot[:, :, 2 * h + kv, :], w[:, :, c:c + A_DIM])\
                                  .then_inc(raw_landed[(u + i) % RAW], 16)
                    for i, first in zip(range(2, 7), (2, 5, 6, 3, 4)):
                        columns(u + i, ab_in[0], 256 * first)
                    for i in range(2):
                        rows_of(u + 7 + i, ab_out[0], 256 * (2 + i))
                    for i in range(2):
                        v = u + 9 + i
                        sp.wait_ge(low_done, v - RAW + 1)
                        for k in range(2):
                            for kv in range(2):
                                r = (4 * kv + 2 * i + k) * A_DIM
                                sp.dma_start(raw_weights[kv * A_DIM:(kv + 1) * A_DIM, v % RAW, k * D:(k + 1) * D],
                                             ab_out[0][r:r + A_DIM, :]).then_inc(raw_landed[v % RAW], 16)
                elif ph.name == "gla":
                    for i in range(12):
                        columns(u + i, c_in[0], 256 * i)
                    for i in range(4):
                        rows_of(u + 12 + i, c_out[0], 256 * i)
                else:
                    for i in range(4):
                        columns(u + i, xq_w[ph.layer], 256 * i)
                    for i in range(4):
                        rows_of(u + 4 + i, xo_w[ph.layer], 256 * i)
            for tt in range(TT):
                sp.wait_ge(x_new, phases[-1].tile + tt + 1)
                sp.dma_start(out[0, tt * P:(tt + 1) * P, :], x_res[:, tt, :]).then_inc(out_stored, 16)
            sp.wait_ge(out_stored, 16 * TT)

        @block.gpsimd
        def _(pool):
            def rsqrt(rstd, ss, count, done, quarter=1.0):
                pool.tensor_scalar(rstd, ss, quarter / count, quarter * EPS,
                                   ALU.mult, ALU.add).then_inc(pool_step, 1)
                steps["pool"] += 1
                pool.wait_ge(pool_step, steps["pool"])
                pool.tensor_tensor(rstd, rstd, neg_half[:, 0:rstd.shape[1]],
                                   ALU.pow).then_inc(done, 1)

            pool.memset(neg_half, -0.5).then_inc(half_set, 1)
            pool.wait_ge(half_set, 1)

            for mt in range(MT):
                pool.wait_ge(mem_sq, mt + 1)
                rsqrt(small[:, mt:mt + 1], ss_y[:, mt:mt + 1], D, mem_rstd)

            def x_norm(base):
                for tt in range(TT):
                    pool.wait_ge(x_sq, base + tt + 1)
                    rsqrt(rstd_x[:, tt:tt + 1], ss_x[:, tt:tt + 1], D, x_rstd)

            x_norm(0)
            for i in range(2 * LAYERS):
                pool.wait_ge(mem_evac, 4 * (i + 1))
                store = (key_store, value_store)[i % 2]
                pool.dma_start(store[i // 2], mem_kv[i]).then_inc(kv_stored, 16)

            for ph in phases:
                if ph.index:
                    pool.wait_ge(x_new, ph.tile)
                row = norm_g[ph.layer, ph.norm_out:ph.norm_out + 1, :]
                pool.dma_start(post_gain[:], row.broadcast_to([P, D])).then_inc(gain_loaded, 16)
                if ph.name == "ab":
                    for t, c in ((0, C_BIAS0), (1, C_BIAS)):
                        pool.dma_start(bias_tab[:, t, :], constants[:, c:c + T]).then_inc(AB["tables"], 16)
                    pool.dma_start(sgu_raw, sgu_w[0].rearrange("g i j -> i g j")).then_inc(AB["tables"], 16)
                    for g in range(SGU_GROUPS):
                        pool.dma_start(sgu_bias[:, g, :], sgu_b[0, g:g + 1, :].broadcast_to([P, P]))\
                            .then_inc(AB["tables"], 16)
                    for kv in range(2):
                        for pair in range(2):
                            for e in range(2):
                                head = 4 * kv + 2 * pair + e
                                pool.dma_start(sink[e * 64:(e + 1) * 64, 2 * kv + pair:2 * kv + pair + 1],
                                               ab_sink[0:1, head:head + 1].broadcast_to([64, 1]))\
                                    .then_inc(AB["tables"], 16)
                    pool.wait_ge(AB["stat_done"], 1)
                    rsqrt(small[:, 12:16], small[:, 8:12], 1.0, AB["ln_rstd"])
                elif ph.name == "gla":
                    for dst, c in ((gmask, C_MASK), (gcum, C_CUM), (gend, C_END)):
                        pool.dma_start(dst, constants[:, c:c + P]).then_inc(GL["tables"], 16)
                    pool.dma_start(gate_raw, c_in[0].rearrange("(k p) n -> p k n", p=P)
                                   [:, :, 3072:3072 + G_RANK]).then_inc(GL["tables"], 16)
                    pool.dma_start(gate_w[0:G_RANK, :], c_gate_w[0]).then_inc(GL["tables"], 16)
                    pool.dma_start(gate_w[G_RANK:G_RANK + 1, :], c_gate_b[0:1, :]).then_inc(GL["tables"], 16)
                    for h in range(G_HEADS):
                        pool.wait_ge(GL["o_sq"], TT * (h + 1))
                        rsqrt(small[:, 4 * (h % 2):4 * (h % 2) + 4], small[:, 8 + 4 * (h % 2):12 + 4 * (h % 2)],
                              G_DV, GL["o_rstd"])
                elif ph.name == "xattn":
                    if ph.nth == 0:
                        pool.wait_ge(kv_stored, 16 * 2 * LAYERS)
                    pool.dma_start(xk.rearrange("p a b -> p (a b)"), key_store[ph.layer]).then_inc(XA["kv_loaded"], 16)
                    pool.dma_start(xv.rearrange("p a b -> p (a b)"), value_store[ph.layer]).then_inc(XA["kv_loaded"], 16)
                for tt in range(TT):
                    pool.wait_ge(y_sq, ph.tile + tt + 1)
                    rsqrt(rstd_y[:, tt:tt + 1], ss_y[:, tt:tt + 1], D, y_rstd,
                          4.0 if ph.name == "ffn" else 1.0)
                    if ph.index < LAST:
                        pool.wait_ge(x_sq, ph.tile + TT + tt + 1)
                        rsqrt(rstd_x[:, tt:tt + 1], ss_x[:, tt:tt + 1], D, x_rstd)

        @block.scalar
        def _(act):
            def split_high(u, more=0):
                if isinstance(more, int) and u >= UNITS:
                    return
                act.wait_ge(raw_landed[u % RAW], landed(u) + 16 * more)
                if u >= RING:
                    act.wait_ge(unit_used, u - RING + 1 + more)
                act.activation(high_weights[:, u % RING, :], raw_weights[:, u % RAW, :], ACT.Copy)\
                   .then_inc(high_done, 1)

            def square_x(base, tt):
                act.activation(square_junk[:], x_res[:, tt, :], ACT.Square,
                               accum_out=ss_x[:, tt:tt + 1]).then_inc(x_sq, 1)

            def operand_high_of(ph, tt):
                act.wait_ge(x_turned, ph.tile + tt + 1)
                for kt in range(KT):
                    last = act.activation(operand_high[:, kt, tt * P:(tt + 1) * P],
                                          token_banks(tt)[:, kt * P:(kt + 1) * P], ACT.Copy,
                                          scale=gain_col(ph.layer, ph.norm_in, kt))
                    if kt % (KT // 2) == KT // 2 - 1:
                        last.then_inc(x_high, 1)

            def boundary(ph):
                nxt = phases[ph.index + 1] if ph.index < LAST else None
                for tt in range(TT):
                    if nxt and tt == TT - 1:
                        split_high(nxt.unit + 1)
                    act.wait_ge(y_done, ph.tile + tt + 1)
                    if nxt and tt:
                        act.wait_ge(x_sq, nxt.tile + tt)
                    elif tt:
                        act.wait_ge(y_sq, ph.tile + tt)
                    act.activation(square_junk[:], token_banks(tt), ACT.Square,
                                   accum_out=ss_y[:, tt:tt + 1]).then_inc(y_sq, 1)
                    if nxt:
                        if tt:
                            operand_high_of(nxt, tt - 1)
                        act.wait_ge(x_new, ph.tile + tt + 1)
                        square_x(nxt.tile, tt)
                if nxt:
                    operand_high_of(nxt, TT - 1)

            act.wait_ge(mem_loaded, 16)
            for mt in range(MT):
                if mt:
                    act.wait_ge(mem_sq, mt)
                    act.wait_ge(mem_loaded_too, 16)
                act.activation(square_junk[:], mem_nat[:, mt, :], ACT.Square,
                               accum_out=ss_y[:, mt:mt + 1]).then_inc(mem_sq, 1)
                if mt == 0:
                    act.wait_ge(gains_turned, 1)
                    act.activation(gain_cols[:], banks[:, 7, 0:GAIN_ROWS], ACT.Copy).then_inc(gains_ready, 1)
            act.wait_ge(table_loaded, 80)
            for k in range(CREDIT):
                act.activation(credit[:, k:k + 1], identity[:, k:k + 1], ACT.Copy).then_inc(silu_done, 1)
            act.wait_ge(gains_ready, 1)

            def memory_high(layer, mt):
                act.wait_ge(mem_turned, mt + 1)
                for kt in range(KT):
                    c = layer * MEM + mt * P
                    last = act.activation(operand_high[:, kt, c:c + P],
                                          token_banks(2 + mt)[:, kt * P:(kt + 1) * P], ACT.Copy,
                                          scale=gain_col(layer, 4, kt))
                    if kt % (KT // 2) == KT // 2 - 1:
                        last.then_inc(mem_high, 1)

            memory_high(0, 0)
            split_high(0)
            memory_high(0, 1)
            split_high(1)
            act.wait_ge(x_loaded, 16)
            act.wait_ge(mem_sq, MT)
            for tt in range(TT):
                if tt:
                    act.wait_ge(x_sq, tt)
                square_x(0, tt)
            for u in range(8 * LAYERS):
                split_high(u + AHEAD)
                act.wait_ge(unit_used, u + 1)
                i, half = divmod(u, 4)
                src = banks[:, u % 4 + 4 * (u // 8), :].rearrange("p (a n) -> p a n", a=2)
                if i % 2 == 0:
                    dst = mem_kv[i].rearrange("p (a n) -> p a n", a=KT)[:, 2 * half:2 * half + 2, :]
                else:
                    dst = mem_kv[i].rearrange("p (a n) -> p a n", a=MT)[:, :, half * MEM:(half + 1) * MEM]
                act.activation(dst, src, ACT.Copy).then_inc(mem_evac, 1)
                if u == 1:
                    memory_high(1, 0)
                    memory_high(1, 1)
                if u in (8, 9):
                    operand_high_of(phases[0], u - 8)
            operand_high_of(phases[0], 2)
            operand_high_of(phases[0], 3)

            def ffn(ph):
                n0, u = ph.nth * FC, ph.unit
                with act.Fori(0, FC // RING) as it:
                    for k in range(RING):
                        split_high(u + k + AHEAD, it * RING)
                        act.wait_ge(gate_done, n0 + k + 1 + it * RING)
                        act.wait_ge(hidden_done, CREDIT + n0 + k - 1 + it * RING)
                        act.activation(silu[:, k % 2, :], banks[:, 2 * k, :], ACT.Silu)\
                           .then_inc(silu_done, 1)
                u += FC
                def pair(k, more=0):
                    if isinstance(more, int):
                        src = hidden[:, 2 * (k + more):2 * (k + more) + 2, :]
                    else:
                        src = hidden[:, bass.ds(more * 2 + 2 * k, 2), :]
                    act.activation(operand_high[:, 2 * (k % 4):2 * (k % 4) + 2, :], src, ACT.Copy)\
                       .then_inc(act_high, 1)
                for k in range(AHEAD):
                    act.wait_ge(chunks_read, 2 * (n0 + FC - 1) + k + 1)
                    pair(k)
                act.wait_ge(unit_used, u)
                act.wait_ge(hidden_done, CREDIT + n0 + FC)
                with act.Fori(0, FC // 2 // RING - 1) as it:
                    for k in range(RING):
                        split_high(u + k + AHEAD, it * RING)
                        act.wait_ge(unit_used, u + k + AHEAD - RING + 1 + it * RING)
                        pair(k + AHEAD, it * RING)
                for v in range(FC // 2 - RING, FC // 2 - 1):
                    split_high(u + v + AHEAD)
                    if v + AHEAD < FC // 2:
                        act.wait_ge(unit_used, u + v + AHEAD - RING + 1)
                        pair(v + AHEAD)

            def outputs(ph, start):
                for v in range(start, start + 3):
                    split_high(ph.unit + v + AHEAD)

            def pair_of_banks(b):
                return banks[:, 2 * b:2 * b + 2, :]

            def window(ph):
                u = ph.unit

                def evacuate(v):
                    act.wait_ge(unit_used, u + v + 1)
                    if v < 2:
                        last = act.activation(qT.rearrange("p a b -> p (a b)").rearrange(
                                                  "p (c j n) -> p j c n", c=NCH, j=4)[:, 2 * v:2 * v + 2, :, :],
                                              pair_of_banks(v).rearrange("p j (c n) -> p j c n", c=NCH), ACT.Copy)
                    elif v == 2:
                        act.activation(kT, banks[:, 4, :], ACT.Copy)
                        last = act.activation(vT, banks[:, 5, :], ACT.Copy)
                    elif v < 5:
                        last = act.activation(vg[:, :, (v - 3) * 256:(v - 2) * 256],
                                              pair_of_banks(v - 3).rearrange("p b (t n) -> p (b t) n", n=256),
                                              ACT.Copy)
                    else:
                        last = act.activation(uT[:, 2 * v - 10:2 * v - 8, :], pair_of_banks(0), ACT.Copy)
                    last.then_inc(AB["in_evac"], 1)

                def exponentials(c):
                    b = c % 2
                    act.wait_ge(AB["shifted"], c + 1)
                    neg_max, sink_gap, total, sink_exp = (
                        small[:, 32 + 16 * b + 4 * i:36 + 16 * b + 4 * i] for i in range(4))
                    act.activation(sink_exp, sink_gap, ACT.Exp)
                    for g in range(4):
                        last = act.activation(probs[b][:, g, :], probs[b][:, g, :], ACT.Exp,
                                              bias=neg_max[:, g:g + 1], accum_out=total[:, g:g + 1])
                    last.then_inc(AB["exped"], 1)

                def keep_turned(c):
                    act.wait_ge(AB["p_turned"], c + 1)
                    act.activation(probsT[c % 2], banks[:, 6, :], ACT.Copy).then_inc(AB["p_evac"], 1)

                def keep_attended(c):
                    act.wait_ge(AB["attended"], c + 1)
                    for kv in range(2):
                        rows = slice(kv * 64, kv * 64 + 64)
                        last = act.activation(
                            kept[rows, :, c * CHUNK:(c + 1) * CHUNK],
                            banks[rows, 7, kv * 256:(kv + 1) * 256].rearrange("p (j q) -> p j q", j=4),
                            ACT.Copy)
                    last.then_inc(AB["kept"], 1)

                def gating_high(g):
                    act.wait_ge(AB["yb_done"], g + 1)
                    act.activation(operand_high[:, 4 + g, :], yb[:, g, :], ACT.Copy).then_inc(AB["out_high"], 1)

                for v in range(3):
                    split_high(u + v + AHEAD)
                    evacuate(v)
                for s in range(NCH):
                    if s == 0:
                        act.wait_ge(AB["v_turned"], 1)
                        act.activation(v_win.rearrange("p a b -> p (a b)")[:, 0:T], banks[:, 6, :], ACT.Copy)
                        act.activation(v_win.rearrange("p a b -> p (a b)")[:, T:7 * P],
                                       banks[:, 7, 0:3 * P], ACT.Copy).then_inc(AB["v_ready"], 1)
                    if s % 2:
                        evacuate(3 + s // 2)
                    if s >= 2:
                        keep_attended(s - 2)
                    if s:
                        keep_turned(s - 1)
                    if s == 1:
                        act.wait_ge(AB["sguT_psum"], 1)
                        act.activation(sguT.rearrange("p a b -> p (a b)"), banks[:, 7, :], ACT.Copy)\
                           .then_inc(AB["sguT_ready"], 1)
                    if s == NCH - 1:
                        gating_high(0)
                        gating_high(1)
                    exponentials(s)
                    if s % 2 == 0:
                        split_high(u + 3 + s // 2 + AHEAD)
                keep_attended(NCH - 2)
                gating_high(2)
                gating_high(3)
                split_high(u + 7 + AHEAD)
                keep_turned(NCH - 1)
                keep_attended(NCH - 1)
                act.wait_ge(AB["kept"], NCH)
                for j in range(4):
                    act.activation(operand_high[:, j, :], kept[:, j, :], ACT.Copy).then_inc(AB["out_high"], 1)
                split_high(u + 8 + AHEAD)
                split_high(u + 9 + AHEAD)

            def gated(ph):
                u = ph.unit

                def squares(h, tiles):
                    for tt in tiles:
                        act.wait_ge(GL["o_done"], h * TT + tiles[-1] + 1)
                        if h + tt:
                            act.wait_ge(GL["o_sq"], h * TT + tt)
                        ss = small[:, 8 + 4 * (h % 2) + tt:9 + 4 * (h % 2) + tt]
                        act.activation(square_junk[:, 0:G_DV],
                                       banks[:, 5 + tt // 2, 256 * (tt % 2):256 * (tt % 2) + 256],
                                       ACT.Square, accum_out=ss).then_inc(GL["o_sq"], 1)

                def z_copy(tt):
                    act.wait_ge(GL["z_done"], tt + 1)
                    act.activation(loga[:, tt, :], banks[:, 6 + tt % 2, :], ACT.Copy).then_inc(GL["z_copied"], 1)

                act.wait_ge(GL["tables"], 16 * 6)
                act.activation(gate_high, gate_raw, ACT.Copy).then_inc(GL["gate_high"], 1)
                for v in range(8):
                    split_high(u + v + AHEAD)
                    if v >= 4:
                        h = v - 4
                        act.wait_ge(GL["cum_done"], h + 1)
                        if h:
                            act.wait_ge(GL["kend_turned"], h)
                            act.wait_ge(GL["dec_done"], h)
                        act.activation(exps[0], banks[:, 6, :], ACT.Exp)
                        act.activation(exps[1], banks[:, 6, :], ACT.Exp, scale=-1.0)
                        act.activation(exps[2], banks[:, 7, :], ACT.Exp).then_inc(GL["exp_done"], 1)
                    if v == 2:
                        act.wait_ge(GL["g_done"], 1)
                        act.wait_ge(GL["cleared"], 1)
                        act.activation(gT[0:G_RANK, :], banks[0:G_RANK, 6, :], ACT.Copy)\
                           .then_inc(GL["gT_ready"], 1)
                        z_copy(0)
                        z_copy(1)
                    act.wait_ge(unit_used, u + v + 1)
                    if v < 2:
                        act.wait_ge(unit_used, u + 2)
                    src = pair_of_banks(v % 3)
                    if v < 4:
                        act.activation((gq, gk)[v // 2][:, 2 * (v % 2):2 * (v % 2) + 2, :], src, ACT.Copy)\
                           .then_inc(GL["in_evac"], 1)
                    else:
                        act.activation(gv[:, :, (v - 4) * 256:(v - 3) * 256],
                                       src.rearrange("p b (t n) -> p (b t) n", n=256), ACT.Copy)\
                           .then_inc(GL["in_evac"], 1)
                    if v == 2:
                        z_copy(2)
                        z_copy(3)
                        for tt in range(TT):
                            act.wait_ge(GL["z_abs"], tt + 1)
                            act.activation(z_tmp[:, tt, :], z_tmp[:, tt, :], ACT.Exp, scale=-1.0)\
                               .then_inc(act_step, 1)
                        steps["act"] += TT
                        act.wait_ge(act_step, steps["act"])
                        for tt in range(TT):
                            act.activation(z_tmp[:, tt, :], z_tmp[:, tt, :], ACT.Ln, bias=1.0)\
                               .then_inc(GL["z_log"], 1)
                    if v >= 4:
                        act.wait_ge(GL["kend_turned"], h + 1)
                        act.activation(loga[:, :, h * P:(h + 1) * P],
                                       banks[:, 6, :].rearrange("p (t n) -> p t n", t=TT), ACT.Copy)\
                           .then_inc(GL["kend_ready"], 1)
                def out_high(c):
                    act.wait_ge(GL["y_ready"], c + 1)
                    act.activation(operand_high[:, c, :], gr[:, c, :], ACT.Copy).then_inc(GL["out_high"], 1)

                for h in range(G_HEADS):
                    v = 8 + h
                    split_high(u + v + AHEAD)
                    act.wait_ge(GL["r_done"], h + 1)
                    act.activation(gr[:, 2 * h, :], banks[:, 0, :], ACT.Silu).then_inc(GL["in_evac"], 1)
                    if h:
                        squares(h - 1, (2, 3))
                    act.wait_ge(unit_used, u + v + 1)
                    act.activation(gr[:, 2 * h + 1, :], banks[:, 1, :], ACT.Silu).then_inc(GL["in_evac"], 1)
                    if h == G_HEADS - 1:
                        out_high(0)
                        out_high(1)
                    squares(h, (0, 1))
                squares(G_HEADS - 1, (2, 3))
                for c in range(2, KT):
                    out_high(c)
                outputs(ph, 12)

            def cross(ph):
                u, base = ph.unit, 4 * ph.nth

                def evacuate(h, bank):
                    act.wait_ge(unit_used, u + max(h, 1) + 1)
                    act.activation(xq[:, 2 * h:2 * h + 2, :], banks[:, bank:bank + 2, :], ACT.Copy)\
                       .then_inc(XA["in_evac"], 1)

                def exponentials(h):
                    b = h % 2
                    neg_max, total = small[:, 8 * b:8 * b + 4], small[:, 8 * b + 4:8 * b + 8]
                    act.wait_ge(XA["maxed"], base + h + 1)
                    if base + h >= 2:
                        act.wait_ge(XA["p_turned"], base + h - 1)
                    for tt in range(TT):
                        last = act.activation(xp[b][:, tt, :], head_banks(h)[:, tt * MEM:(tt + 1) * MEM], ACT.Exp,
                                              bias=neg_max[:, tt:tt + 1], scale=(D // X_HEADS) ** -0.5,
                                              accum_out=total[:, tt:tt + 1])
                    last.then_inc(XA["exped"], 1)

                def keep_turned(h):
                    act.wait_ge(XA["p_turned"], base + h + 1)
                    act.activation(xpT[:, 2 * h:2 * h + 2, :].rearrange("p a n -> p (a n)"), head_banks(h),
                                   ACT.Copy).then_inc(XA["p_evac"], 1)

                def out_high(h):
                    for half in range(2):
                        j = 2 * h + half
                        act.wait_ge(XA["attended"], 8 * ph.nth + j + 1)
                        act.activation(operand_high[:, j, :], head_banks(h)[:, half * T:(half + 1) * T], ACT.Copy)\
                           .then_inc(XA["out_high"], 1)

                split_high(u + 2)
                split_high(u + 3)
                evacuate(0, 0)
                evacuate(1, 2)
                exponentials(0)
                evacuate(2, 6)
                split_high(u + 4)
                exponentials(1)
                keep_turned(0)
                exponentials(2)
                evacuate(3, 4)
                keep_turned(1)
                exponentials(3)
                split_high(u + 5)
                keep_turned(2)
                out_high(0)
                out_high(1)
                keep_turned(3)
                out_high(2)
                out_high(3)
                outputs(ph, 4)

            for ph in phases:
                {"ffn": ffn, "ab": window, "gla": gated, "xattn": cross}[ph.name](ph)
                boundary(ph)

        @block.vector
        def _(dve):
            def step(instruction):
                instruction.then_inc(dve_step, 1)
                steps["dve"] += 1
                dve.wait_ge(dve_step, steps["dve"])

            def split_low(u, more=0):
                if isinstance(more, int) and u >= UNITS:
                    return
                dve.wait_ge(high_done, u + 1 + more)
                dve.tensor_tensor(low_weights[:, u % RING, :], raw_weights[:, u % RAW, :],
                                  high_weights[:, u % RING, :].bitcast(F32), ALU.subtract)\
                   .then_inc(low_done, 1)

            def scale_x(ph, tt):
                dve.wait_ge(x_rstd, ph.tile + tt + 1)
                dve.tensor_scalar(scaled[:, tt, :], x_res[:, tt, :], rstd_x[:, tt:tt + 1], None,
                                  ALU.mult).then_inc(x_scaled, 1)

            def operand_low_of(ph, tt):
                for kt in range(KT):
                    dve.wait_ge(x_high, 2 * (ph.tile + tt) + (1 if kt < KT // 2 else 2))
                    cols = slice(tt * P, (tt + 1) * P)
                    last = dve.scalar_tensor_tensor(
                        operand_low[:, kt, cols], token_banks(tt)[:, kt * P:(kt + 1) * P],
                        gain_col(ph.layer, ph.norm_in, kt), operand_high[:, kt, cols].bitcast(F32),
                        ALU.mult, ALU.subtract)
                    if kt % (KT // 2) == KT // 2 - 1:
                        last.then_inc(x_low, 1)

            def boundary(ph):
                nxt = phases[ph.index + 1] if ph.index < LAST else None
                dve.wait_ge(gain_loaded, 16 * (ph.index + 1))
                for tt in range(TT):
                    if nxt and tt == TT - 1:
                        split_low(nxt.unit + 1)
                    dve.wait_ge(y_rstd, ph.tile + tt + 1)
                    step(dve.scalar_tensor_tensor(token_banks(tt), token_banks(tt), rstd_y[:, tt:tt + 1],
                                                  post_gain[:], ALU.mult, ALU.mult))
                    dve.tensor_tensor(x_res[:, tt, :], token_banks(tt), x_res[:, tt, :], ALU.add)\
                       .then_inc(x_new, 1)
                    if nxt:
                        if tt:
                            operand_low_of(nxt, tt - 1)
                        scale_x(nxt, tt)
                if nxt:
                    operand_low_of(nxt, TT - 1)

            for k in range(CREDIT):
                dve.memset(credit[:, CREDIT + k:CREDIT + k + 1], 0.0).then_inc(hidden_done, 1)
            for mt in range(MT):
                dve.wait_ge(mem_rstd, mt + 1)
                dve.tensor_scalar(mem_scaled[:, mt, :], mem_nat[:, mt, :], small[:, mt:mt + 1], None,
                                  ALU.mult).then_inc(mem_scaled_done, 1)

            def memory_low(layer, mt):
                for kt in range(KT):
                    dve.wait_ge(mem_high, 2 * (MT * layer + mt) + (1 if kt < KT // 2 else 2))
                    c = slice(layer * MEM + mt * P, layer * MEM + (mt + 1) * P)
                    last = dve.scalar_tensor_tensor(
                        operand_low[:, kt, c], token_banks(2 + mt)[:, kt * P:(kt + 1) * P],
                        gain_col(layer, 4, kt), operand_high[:, kt, c].bitcast(F32),
                        ALU.mult, ALU.subtract)
                last.then_inc(mem_low, 1)

            memory_low(0, 0)
            split_low(0)
            memory_low(0, 1)
            split_low(1)
            dve.wait_ge(mem_turned, MT)
            for tt in range(TT):
                scale_x(phases[0], tt)
            for u in range(8 * LAYERS):
                split_low(u + AHEAD)
                if u == 1:
                    memory_low(1, 0)
                    memory_low(1, 1)
                if u in (8, 9):
                    operand_low_of(phases[0], u - 8)
            operand_low_of(phases[0], 2)
            operand_low_of(phases[0], 3)
            dve.wait_ge(kv_stored, 16 * 2 * LAYERS)

            def ffn(ph):
                n0, u = ph.nth * FC, ph.unit
                a0 = ph.nth * (FC // 2)

                def hidden_chunk(k, more=0):
                    dve.wait_ge(silu_done, CREDIT + n0 + k + 1 + more)
                    dve.wait_ge(unit_used, ph.unit + k + 1 + more)
                    f = k + more if isinstance(more, int) else bass.ds(more + k, 1)
                    f = slice(f, f + 1) if isinstance(f, int) else f
                    dve.tensor_tensor(hidden[:, f, :], silu[:, k % 2:k % 2 + 1, :],
                                      banks[:, 2 * (k % 4) + 1:2 * (k % 4) + 2, :],
                                      ALU.mult).then_inc(hidden_done, 1)
                with dve.Fori(0, FC // RING - 1) as it:
                    for k in range(RING):
                        split_low(u + k + AHEAD, it * RING)
                        hidden_chunk(k, it * RING)
                for k in range(FC - RING, FC):
                    split_low(u + k + AHEAD)
                    if k < FC - 1:
                        hidden_chunk(k)
                u += FC
                def pair(k, more=0):
                    dve.wait_ge(act_high, a0 + k + 1 + more)
                    if isinstance(more, int):
                        src = hidden[:, 2 * (k + more):2 * (k + more) + 2, :]
                    else:
                        src = hidden[:, bass.ds(more * 2 + 2 * k, 2), :]
                    part_of = slice(2 * (k % 4), 2 * (k % 4) + 2)
                    dve.tensor_tensor(operand_low[:, part_of, :], src,
                                      operand_high[:, part_of, :].bitcast(F32), ALU.subtract)\
                       .then_inc(act_low, 1)
                for k in range(AHEAD):
                    pair(k)
                hidden_chunk(FC - 1)
                with dve.Fori(0, FC // 2 // RING - 1) as it:
                    for k in range(RING):
                        split_low(u + k + AHEAD, it * RING)
                        pair(k + AHEAD, it * RING)
                for v in range(FC // 2 - RING, FC // 2 - 1):
                    split_low(u + v + AHEAD)
                    if v + AHEAD < FC // 2:
                        pair(v + AHEAD)

            def window(ph):
                u = ph.unit

                def biased(c):
                    b = c % 2
                    neg_max, sink_gap, total, sink_exp = (
                        small[:, 32 + 16 * b + 4 * i:36 + 16 * b + 4 * i] for i in range(4))
                    dve.wait_ge(AB["scores"], c + 1)
                    if c >= 2:
                        dve.wait_ge(AB["p_turned"], c - 1)
                    step(dve.scalar_tensor_tensor(
                        probs[b].rearrange("p (k n) q -> p k (n q)", k=2), banks[:, 4:6, 0:256],
                        A_DIM ** -0.5, bias_tab[:, min(c, 1), :].rearrange("p (k n) -> p k n", k=2),
                        ALU.mult, ALU.add))
                    step(dve.tensor_reduce(neg_max, probs[b], AX.X, ALU.max))
                    step(dve.tensor_tensor(neg_max, neg_max, sink, ALU.max))
                    step(dve.tensor_tensor(sink_gap, sink, neg_max, ALU.subtract))
                    dve.tensor_scalar(neg_max, neg_max, -1.0, None, ALU.mult).then_inc(AB["shifted"], 1)

                def normed(c):
                    b = c % 2
                    dve.wait_ge(AB["exped"], c + 1)
                    neg_max, sink_gap, total, sink_exp = (
                        small[:, 32 + 16 * b + 4 * i:36 + 16 * b + 4 * i] for i in range(4))
                    step(dve.tensor_tensor(total, total, sink_exp, ALU.add))
                    step(dve.reciprocal(total, total))
                    for g in range(4):
                        last = dve.tensor_scalar(probs[b][:, g, :], probs[b][:, g, :], total[:, g:g + 1],
                                                 None, ALU.mult)
                    last.then_inc(AB["normed"], 1)

                def gating_statistics():
                    dve.wait_ge(AB["in_evac"], 5)
                    raw_stats = small[:, 64:88].rearrange("p (t n) -> p t n", t=TT)
                    mean_var = small[:, 88:96].rearrange("p (t n) -> p t n", t=TT)
                    for tt in range(TT):
                        last = dve.bn_stats(raw_stats[:, tt, :], vg[:, tt, :])
                    step(last)
                    for tt in range(TT):
                        last = dve.bn_aggr(mean_var[:, tt, :], raw_stats[:, tt, :])
                    step(last)
                    dve.tensor_copy(small[:, 16:20], mean_var[:, :, 0])
                    dve.tensor_copy(small[:, 8:12], mean_var[:, :, 1]).then_inc(AB["stat_done"], 1)

                def gating_norm():
                    dve.wait_ge(AB["ln_rstd"], 1)
                    for tt in range(TT):
                        last = dve.tensor_scalar(vg[:, tt, :], vg[:, tt, :], small[:, 16 + tt:17 + tt],
                                                 small[:, 12 + tt:13 + tt], ALU.subtract, ALU.mult)
                    last.then_inc(AB["ln_done"], 1)

                def gate_u(g):
                    dve.wait_ge(AB["mixed"], g + 1)
                    step(dve.scalar_tensor_tensor(
                        yb[:, g, :].rearrange("p (t n) -> p t n", t=TT),
                        banks[:, 2 + g % 2, :].rearrange("p (t n) -> p t n", t=TT), sgu_gain(g),
                        sgu_bias[:, g:g + 1, :].broadcast_to([P, TT, P]), ALU.mult, ALU.add))
                    dve.wait_ge(AB["in_evac"], 6 + g // 2)
                    dve.tensor_tensor(yb[:, g, :], yb[:, g, :], uT[:, g, :], ALU.mult).then_inc(AB["yb_done"], 1)

                def out_low(i):
                    dve.wait_ge(AB["out_high"], i + 1)
                    chunk = (4 + i) % KT
                    src = yb[:, i, :] if i < 4 else kept[:, i - 4, :]
                    dve.tensor_tensor(operand_low[:, chunk, :], src,
                                      operand_high[:, chunk, :].bitcast(F32), ALU.subtract)\
                       .then_inc(AB["out_low"], 1)

                for v in range(3):
                    split_low(u + v + AHEAD)
                for s in range(NCH):
                    biased(s)
                    if s == 1:
                        dve.wait_ge(AB["sguT_ready"], 1)
                        dve.memset(sguT[64:P, :, 0:64], 0.0).then_inc(AB["masked"], 1)
                    if s == NCH - 1:
                        out_low(0)
                        out_low(1)
                        gate_u(2)
                        gate_u(3)
                    if s == 5:
                        gating_norm()
                    if s == 6:
                        gate_u(0)
                        gate_u(1)
                    normed(s)
                    if s % 2 == 0:
                        split_low(u + 3 + s // 2 + AHEAD)
                    if s == 3:
                        gating_statistics()
                out_low(2)
                out_low(3)
                split_low(u + 7 + AHEAD)
                for j in range(4):
                    out_low(4 + j)
                split_low(u + 8 + AHEAD)
                split_low(u + 9 + AHEAD)

            def gated(ph):
                dve.memset(gT[0:32, :], 1.0).then_inc(GL["cleared"], 1)
                dve.wait_ge(GL["gate_high"], 1)
                dve.tensor_tensor(gate_low, gate_raw, gate_high.bitcast(F32), ALU.subtract)\
                   .then_inc(GL["gate_low"], 1)

                def decays(h):
                    dve.wait_ge(GL["exp_done"], h + 1)
                    dve.wait_ge(GL["in_evac"], 4)
                    dve.tensor_copy(decay[:, h, :], exps[0].rearrange("p (c n) -> p c n", c=NCH)[:, :, CHUNK - 1])
                    dve.tensor_tensor(exps[2], exps[2], gk[:, h, :], ALU.mult).then_inc(GL["kend_made"], 1)
                    dve.tensor_tensor(gk[:, h, :], gk[:, h, :], exps[1], ALU.mult)
                    dve.scalar_tensor_tensor(gq[:, h, :], gq[:, h, :], G_DK ** -0.5, exps[0], ALU.mult,
                                             ALU.mult).then_inc(GL["dec_done"], 1)

                def mask_scores(h):
                    dve.wait_ge(GL["att_done"], h + 1)
                    dve.copy_predicated(att.rearrange("p (t n) -> p t n", t=TT), mask,
                                        banks[:, 2, :].rearrange("p (t n) -> p t n", t=TT))\
                       .then_inc(GL["att_ready"], 1)

                def make_states(h, chunks):
                    for c in chunks:
                        dve.wait_ge(GL["kv_done"], 2 * h + (1 if c < 4 else 2))
                        if c >= 4:
                            dve.wait_ge(GL["o_done"], h * TT + (c - 3) // 2 + 1)
                        elif h:
                            dve.wait_ge(GL["o_done"], h * TT)
                        half = (c // 2) % 2
                        product = banks[:, 3 + c % 2, half * 256:(half + 1) * 256]
                        if c == 0:
                            dve.tensor_copy(states[:, 1, :], product).then_inc(GL["state_ready"], 1)
                        else:
                            dve.wait_ge(GL["state_ready"], h * (NCH - 1) + c)
                            dve.scalar_tensor_tensor(states[:, (c + 1) % 4, :], states[:, c % 4, :],
                                                     decay[:, h, c:c + 1], product, ALU.mult, ALU.add)\
                               .then_inc(GL["state_ready"], 1)

                def scale_outputs(h):
                    dve.wait_ge(GL["o_rstd"], h + 1)
                    if h:
                        dve.wait_ge(GL["o_turned"], h * TT)
                    for tt in range(TT):
                        dve.tensor_scalar(o_nat[:, tt, :], banks[:, 5 + tt // 2, 256 * (tt % 2):256 * (tt % 2) + 256],
                                          small[:, 4 * (h % 2) + tt:4 * (h % 2) + tt + 1], None, ALU.mult)\
                           .then_inc(GL["o_scaled"], 1)

                def gate_outputs(h):
                    dve.wait_ge(GL["o_turned"], (h + 1) * TT)
                    dve.wait_ge(GL["in_evac"], 8 + 2 * (h + 1))
                    for j, bank in ((0, 7), (1, 2)):
                        c = 2 * h + j
                        dve.scalar_tensor_tensor(gr[:, c, :], banks[:, bank, :], head_gain(c), gr[:, c, :],
                                                 ALU.mult, ALU.mult).then_inc(GL["y_ready"], 1)

                for v in range(8):
                    split_low(ph.unit + v + AHEAD)
                    if v == 2:
                        for tt in range(TT):
                            dve.wait_ge(GL["z_copied"], tt + 1)
                            dve.scalar_tensor_tensor(z_tmp[:, tt, :], loga[:, tt, :], -1.0, loga[:, tt, :],
                                                     ALU.mult, ALU.max).then_inc(GL["z_abs"], 1)
                        for tt in range(TT):
                            dve.wait_ge(GL["z_log"], tt + 1)
                            dve.scalar_tensor_tensor(loga[:, tt, :], loga[:, tt, :], 0.0, z_tmp[:, tt, :],
                                                     ALU.min, ALU.subtract).then_inc(GL["log_ready"], 1)
                    if v >= 4:
                        decays(v - 4)
                dve.wait_ge(GL["dec_done"], G_HEADS)
                step(dve.memset(att, 0.0))
                mask = gmask.bitcast(U32).unsqueeze(1).broadcast_to([P, TT, P])
                for h in range(G_HEADS):
                    split_low(ph.unit + 8 + h + AHEAD)
                    if h:
                        dve.wait_ge(GL["o_done"], h * TT)
                    mask_scores(h)
                    make_states(h, range(4))
                    if h:
                        scale_outputs(h - 1)
                        gate_outputs(h - 1)
                    make_states(h, range(4, NCH - 1))
                for c in range(KT):
                    if c == 2:
                        scale_outputs(G_HEADS - 1)
                    if c == 4:
                        gate_outputs(G_HEADS - 1)
                    dve.wait_ge(GL["out_high"], c + 1)
                    dve.tensor_tensor(operand_low[:, c, :], gr[:, c, :],
                                      operand_high[:, c, :].bitcast(F32), ALU.subtract)\
                       .then_inc(GL["out_low"], 1)
                for v in range(12, 15):
                    split_low(ph.unit + v + AHEAD)

            def cross(ph):
                u, base = ph.unit, 4 * ph.nth

                def maximum(h):
                    neg_max = small[:, 8 * (h % 2):8 * (h % 2) + 4]
                    dve.wait_ge(XA["scores"], base + h + 1)
                    step(dve.tensor_reduce(neg_max, head_banks(h).rearrange("p (t n) -> p t n", t=TT),
                                           AX.X, ALU.max))
                    dve.tensor_scalar(neg_max, neg_max, -((D // X_HEADS) ** -0.5), None, ALU.mult)\
                       .then_inc(XA["maxed"], 1)

                def normed(h):
                    b = h % 2
                    total = small[:, 8 * b + 4:8 * b + 8]
                    dve.wait_ge(XA["exped"], base + h + 1)
                    step(dve.reciprocal(total, total))
                    for tt in range(TT):
                        last = dve.tensor_scalar(xp[b][:, tt, :], xp[b][:, tt, :], total[:, tt:tt + 1], None,
                                                 ALU.mult)
                    last.then_inc(XA["normed"], 1)

                split_low(u + 2)
                split_low(u + 3)
                maximum(0)
                normed(0)
                maximum(1)
                split_low(u + 4)
                normed(1)
                maximum(2)
                normed(2)
                maximum(3)
                normed(3)
                split_low(u + 5)
                for j in range(KT):
                    dve.wait_ge(XA["out_high"], 8 * ph.nth + j + 1)
                    dve.tensor_tensor(operand_low[:, j, :], head_banks(j // 2)[:, (j % 2) * T:(j % 2 + 1) * T],
                                      operand_high[:, j, :].bitcast(F32), ALU.subtract)\
                       .then_inc(XA["out_low"], 1)
                for v in range(4, 7):
                    split_low(u + v + AHEAD)

            for ph in phases:
                {"ffn": ffn, "ab": window, "gla": gated, "xattn": cross}[ph.name](ph)
                boundary(ph)

        @block.tensor
        def _(pe):
            def three(out_, w_high, w_low, a_high, a_low, start, stop):
                pe.matmul(out_, w_high, a_high, start=start, stop=False)
                pe.matmul(out_, w_high, a_low, start=False, stop=False)
                return pe.matmul(out_, w_low, a_high, start=False, stop=stop)

            def column_chunk(u, pick, out_, cols, read=None, half_low=None):
                for kt in range(KT):
                    if half_low is not None and kt in (0, KT // 2):
                        pe.wait_ge(x_low, half_low + kt // (KT // 2))
                    last = three(out_, pick(high_weights[:, u % RING, :], kt),
                                 pick(low_weights[:, u % RING, :], kt),
                                 operand_high[:, kt, cols], operand_low[:, kt, cols],
                                 kt == 0, kt == KT - 1)
                    if read is not None and kt in (1, 3):
                        last.then_inc(read, 1)
                return last

            def natural(u, out_, tokens, c0, n):
                for kt in range(KT):
                    w = slice(kt * 256 + c0, kt * 256 + c0 + n)
                    last = three(out_, operand_high[:, kt, tokens], operand_low[:, kt, tokens],
                                 high_weights[:, u % RING, w], low_weights[:, u % RING, w],
                                 kt == 0, kt == KT - 1)
                return last

            def block_of(half):
                return lambda slot, kt: slot[:, kt * 256 + half * P:kt * 256 + half * P + P]

            def turn_x(ph, tt, frees_unit=False):
                pe.wait_ge(x_scaled, ph.tile + tt + 1)
                for kt in range(KT):
                    last = pe.transpose(token_banks(tt)[:, kt * P:(kt + 1) * P],
                                        scaled[:, tt, kt * P:(kt + 1) * P], identity[:])
                    if kt == 0 and frees_unit:
                        last.then_inc(unit_used, 1)
                last.then_inc(x_turned, 1)

            def output_unit(u, tt, k, chunk, start, stop):
                rows, slot = slice(tt * P, (tt + 1) * P), u % RING
                halves = [(banks[:, 2 * tt + nh, :], slice(k * D + nh * T, k * D + (nh + 1) * T))
                          for nh in range(2)]
                for bank, w in halves:
                    pe.matmul(bank, operand_high[:, chunk, rows], high_weights[:, slot, w],
                              start=start, stop=False)
                    pe.matmul(bank, operand_high[:, chunk, rows], low_weights[:, slot, w],
                              start=False, stop=False)
                for bank, w in halves:
                    last = pe.matmul(bank, operand_low[:, chunk, rows], high_weights[:, slot, w],
                                     start=False, stop=stop)
                return last

            def last_units(ph, u, chunks, ready=None, base=0):
                nxt = phases[ph.index + 1] if ph.index < LAST else None
                for tt in range(TT):
                    for j, chunk in enumerate(chunks):
                        if tt == 0 and j % 2 == 0:
                            pe.wait_ge(low_done, u + j // 2 + 1)
                        if tt == 0 and ready is not None:
                            pe.wait_ge(ready, base + j + 1)
                        last = output_unit(u + j // 2, tt, j % 2, chunk, False, j == 5)
                        if tt == TT - 1 and j in (1, 3):
                            last.then_inc(unit_used, 1)
                    last.then_inc(y_done, 1)
                    if nxt and tt:
                        turn_x(nxt, tt - 1, frees_unit=tt == TT - 1)
                if nxt:
                    first_units(nxt)

            def first_units(ph):
                picks = (block_of(0), block_of(1)) if ph.name != "ffn" else (ffn_gate, ffn_up)
                early, late = slice(0, T // 2), slice(T // 2, T)
                pe.wait_ge(x_low, 2 * (ph.tile + 2))
                for k in range(2):
                    pe.wait_ge(low_done, ph.unit + k + 1)
                    for half in range(2):
                        column_chunk(ph.unit + k, picks[half], banks[:, 2 * k + half, early], early)
                        if (k, half) == (1, 0):
                            turn_x(ph, TT - 1)
                for k in range(2):
                    for half in range(2):
                        last = column_chunk(ph.unit + k, picks[half], banks[:, 2 * k + half, late], late,
                                            chunks_read if ph.name == "ffn" and half else None,
                                            2 * (ph.tile + TT) - 1 if k + half == 0 else None)
                        if half:
                            last.then_inc(unit_used, 1)
                        elif ph.name == "ffn":
                            last.then_inc(gate_done, 1)

            def ffn_gate(slot, kt):
                return slot[:, kt * P:(kt + 1) * P]

            def ffn_up(slot, kt):
                return slot[:, (KT + kt) * P:(KT + kt + 1) * P]

            pe.wait_ge(table_loaded, 16 * 5)
            pe.transpose(banks[:, 7, 0:P], gain_rows[:, 0, :], identity[:])
            pe.transpose(banks[:, 7, P:GAIN_ROWS], gain_rows[0:GAIN_ROWS - P, 1, :],
                         identity[0:GAIN_ROWS - P, 0:GAIN_ROWS - P]).then_inc(gains_turned, 1)
            for mt in range(MT):
                pe.wait_ge(mem_scaled_done, mt + 1)
                if mt:
                    pe.wait_ge(gains_ready, 1)
                for kt in range(KT):
                    last = pe.transpose(token_banks(2 + mt)[:, kt * P:(kt + 1) * P],
                                        mem_scaled[:, mt, kt * P:(kt + 1) * P], identity[:])
                last.then_inc(mem_turned, 1)
            for u in range(8 * LAYERS):
                i, layer, bank = u // 4, u // 8, banks[:, u % 4 + 4 * (u // 8), :]
                pe.wait_ge(low_done, u + 1)
                pe.wait_ge(mem_low, MT * (1 + u // 8))
                if u == 8:
                    pe.wait_ge(mem_evac, 8)
                    turn_x(phases[0], 0)
                    turn_x(phases[0], 1)
                if u % 8 >= 4:
                    pe.wait_ge(mem_evac, u - 3)
                for half in range(2):
                    if i % 2 == 0:
                        last = column_chunk(u, block_of(half), bank[:, half * MEM:(half + 1) * MEM],
                                            slice(layer * MEM, (layer + 1) * MEM))
                    else:
                        m = layer * MEM + half * P
                        last = natural(u, bank[:, half * 256:(half + 1) * 256], slice(m, m + P), 0, 256)
                last.then_inc(unit_used, 1)
            pe.wait_ge(mem_evac, 8 * LAYERS)
            turn_x(phases[0], 2)
            first_units(phases[0])

            def ffn(ph):
                n0, u = ph.nth * FC, ph.unit
                all_tokens = slice(0, T)

                def gate_and_up(k, more=0):
                    pe.wait_ge(low_done, u + k + 1 + more)
                    pe.wait_ge(silu_done, CREDIT + n0 + k - RING + 1 + more)
                    column_chunk(u + k, ffn_gate, banks[:, 2 * (k % 4), :], all_tokens).then_inc(gate_done, 1)
                    pe.wait_ge(hidden_done, CREDIT + n0 + k - RING + 1 + more)
                    column_chunk(u + k, ffn_up, banks[:, 2 * (k % 4) + 1, :], all_tokens,
                                 chunks_read).then_inc(unit_used, 1)
                with pe.Fori(0, FC // RING - 1) as it:
                    for k in range(RING):
                        gate_and_up(2 + k, it * RING)
                gate_and_up(FC - 2)
                gate_and_up(FC - 1)
                u += FC
                a0 = ph.nth * (FC // 2)

                def whole(v, more=0, start=False):
                    pe.wait_ge(low_done, u + v + 1 + more)
                    pe.wait_ge(act_low, a0 + v + 1 + more)
                    for k in range(2):
                        for tt in range(TT):
                            if start and k == 0:
                                pe.wait_ge(hidden_done, CREDIT + n0 + FC - TT + tt + 1)
                            last = output_unit(u + v, tt, k, 2 * (v % 4) + k, start and k == 0, False)
                    last.then_inc(unit_used, 1)
                whole(0, start=True)
                with pe.Fori(0, FC // 2 // RING - 1) as it:
                    for k in range(RING):
                        whole(1 + k, it * RING)
                pe.wait_ge(act_low, a0 + FC // 2)
                last_units(ph, u + FC // 2 - 3, range(2, 8))

            def window(ph):
                u = ph.unit

                def scores(c):
                    k0 = max(c - 1, 0) * CHUNK
                    if c:
                        pe.wait_ge(AB["shifted"], c)
                    for kv in range(2):
                        rows = slice(kv * 64, kv * 64 + 64)
                        for pair in range(2):
                            last = pe.matmul(banks[:, 4 + kv, pair * P:(pair + 1) * P],
                                             qT[rows, c // 2, (c % 2) * 256 + pair * P:(c % 2) * 256 + (pair + 1) * P],
                                             kT[rows, k0:k0 + P], start=True, stop=True)
                    last.then_inc(AB["scores"], 1)

                def turn_probs(c):
                    pe.wait_ge(AB["normed"], c + 1)
                    if c:
                        pe.wait_ge(AB["p_evac"], c)
                    for g in range(4):
                        last = pe.transpose(banks[:, 6, g * P:(g + 1) * P], probs[c % 2][:, g, :], identity[:])
                    last.then_inc(AB["p_turned"], 1)

                def attend(c):
                    pe.wait_ge(AB["p_evac"], c + 1)
                    if c:
                        pe.wait_ge(AB["kept"], c)
                    else:
                        pe.wait_ge(AB["sguT_ready"], 1)
                    tile = max(c - 1, 0)
                    window_of = v_win[:, tile // 2 if tile % 2 == 0 else 4 + tile // 2, :]
                    pe.matmul(banks[:, 7, :], window_of, probsT[c % 2], start=True, stop=True)\
                      .then_inc(AB["attended"], 1)

                def mix(g):
                    for tt in range(TT):
                        last = pe.matmul(banks[:, 2 + g % 2, tt * P:(tt + 1) * P], vg[:, tt, g * P:(g + 1) * P],
                                         sguT[:, g, :], start=True, stop=True)
                    last.then_inc(AB["mixed"], 1)

                pe.wait_ge(low_done, u + 3)
                column_chunk(u + 2, block_of(0), banks[:, 4, :], slice(0, T))
                column_chunk(u + 2, block_of(1), banks[:, 5, :], slice(0, T)).then_inc(unit_used, 1)
                for s in range(NCH):
                    v, half = 3 + s // 2, s % 2
                    if half == 0:
                        pe.wait_ge(low_done, u + v + 1)
                        pe.wait_ge(AB["in_evac"], (1, 2, 4, 6)[v - 3])
                    bank = banks[:, 2 * (v == 4) + half, :]
                    if v < 5:
                        for tt in range(2 * half, 2 * half + 2):
                            last = natural(u + v, bank[:, (tt % 2) * 256:(tt % 2 + 1) * 256],
                                           slice(tt * P, (tt + 1) * P), 0, 256)
                    else:
                        last = column_chunk(u + v, block_of(half), bank, slice(0, T))
                    if half:
                        last.then_inc(unit_used, 1)
                    if s == 0:
                        pe.wait_ge(AB["tables"], AB_TABLES)
                        pe.wait_ge(AB["in_evac"], 3)
                    if s == 6:
                        pe.wait_ge(AB["masked"], 1)
                        pe.wait_ge(AB["ln_done"], 1)
                        pe.wait_ge(AB["in_evac"], 5)
                        mix(0)
                        mix(1)
                    if s >= 2:
                        attend(s - 2)
                    scores(s)
                    if s == 0:
                        for i in range(7):
                            start = i * P if i < 4 else (i - 4) * P + CHUNK
                            last = pe.transpose(banks[:, 6 + i // 4, (i % 4) * P:(i % 4 + 1) * P],
                                                vT[:, start:start + P], identity[:])
                        last.then_inc(AB["v_turned"], 1)
                    if s == 1:
                        pe.wait_ge(AB["v_ready"], 1)
                    if s:
                        turn_probs(s - 1)
                    if s == 1:
                        for g in range(SGU_GROUPS):
                            last = pe.transpose(banks[:, 7, g * P:(g + 1) * P], sgu_raw[:, g, :], identity[:])
                        last.then_inc(AB["sguT_psum"], 1)
                    if s == 7:
                        pe.wait_ge(AB["yb_done"], 2)
                        mix(2)
                        mix(3)
                attend(NCH - 2)
                pe.wait_ge(low_done, u + 8)
                for tt in range(TT):
                    if tt == 0:
                        pe.wait_ge(AB["in_evac"], 7)
                    elif tt == 1:
                        pe.wait_ge(AB["yb_done"], 4)
                    elif tt == 2:
                        turn_probs(NCH - 1)
                        pe.wait_ge(AB["shifted"], NCH)
                    else:
                        attend(NCH - 1)
                        pe.wait_ge(AB["kept"], NCH)
                    for k in range(2):
                        pe.wait_ge(AB["out_low"], k + 1)
                        last = output_unit(u + 7, tt, k, 4 + k, k == 0, False)
                last.then_inc(unit_used, 1)
                last_units(ph, u + 8, (6, 7, 0, 1, 2, 3), AB["out_low"], 2)

            def gated(ph):
                u = ph.unit

                def gate_inner():
                    pe.wait_ge(GL["gate_low"], 1)
                    for kt in range(KT):
                        last = three(banks[0:G_RANK, 6, :], gate_high[:, kt, :], gate_low[:, kt, :],
                                     operand_high[:, kt, :], operand_low[:, kt, :], kt == 0, kt == KT - 1)
                    last.then_inc(GL["g_done"], 1)

                def gate_z(tt):
                    pe.wait_ge(GL["gT_ready"], 1)
                    if tt >= 2:
                        pe.wait_ge(GL["z_copied"], tt - 1)
                    pe.matmul(banks[:, 6 + tt % 2, :], gT[0:G_RANK + 1, tt * P:(tt + 1) * P],
                              gate_w[0:G_RANK + 1, :], start=True, stop=True).then_inc(GL["z_done"], 1)

                def sums(h):
                    pe.wait_ge(GL["log_ready"], TT)
                    if h:
                        pe.wait_ge(GL["kend_ready"], h)
                    for bank, table in ((6, gcum), (7, gend)):
                        for tt in range(TT):
                            last = pe.matmul(banks[:, bank, tt * P:(tt + 1) * P],
                                             loga[:, tt, h * P:(h + 1) * P], table, start=True, stop=True)
                    last.then_inc(GL["cum_done"], 1)

                def turn_keys(h):
                    pe.wait_ge(GL["kend_made"], h + 1)
                    for tt in range(TT):
                        last = pe.transpose(banks[:, 6, tt * P:(tt + 1) * P], exps[2][:, tt * P:(tt + 1) * P],
                                            identity[:])
                    last.then_inc(GL["kend_turned"], 1)

                def key_values(h, chunks):
                    for c in chunks:
                        rows, half = slice((c % 2) * 64, (c % 2) * 64 + 64), (c // 2) % 2
                        last = pe.matmul(banks[:, 3 + c % 2, half * 256:(half + 1) * 256],
                                         loga[rows, c // 2, h * P:(h + 1) * P],
                                         gv[rows, c // 2, h * G_DV:(h + 1) * G_DV], start=True, stop=True)
                    last.then_inc(GL["kv_done"], 1)

                def scores(h):
                    pe.wait_ge(GL["dec_done"], h + 1)
                    if h >= 2:
                        pe.wait_ge(GL["y_ready"], 2 * (h - 1))
                    for tt in range(TT):
                        s = slice(tt * P, (tt + 1) * P)
                        last = pe.matmul(banks[:, 2, s], gk[:, h, s], gq[:, h, s], start=True, stop=True)
                    last.then_inc(GL["att_done"], 1)
                    if h:
                        pe.wait_ge(GL["state_ready"], h * (NCH - 1))
                    key_values(h, range(4))

                def outputs_of(h, tiles):
                    pe.wait_ge(GL["att_ready"], h + 1)
                    if h:
                        pe.wait_ge(GL["o_scaled"], h * TT)
                    for tt in tiles:
                        o = banks[:, 5 + tt // 2, (tt % 2) * 256:(tt % 2 + 1) * 256]
                        values = gv[:, tt, h * G_DV:(h + 1) * G_DV]
                        if tt == 0:
                            pe.matmul(o[0:64, :], att[:, 0:64], values, start=True, stop=True)
                            pe.matmul(o[64:P, :], att[:, 64:P], values, start=True, stop=False)
                        else:
                            pe.matmul(o, att[:, tt * P:(tt + 1) * P], values, start=True, stop=False)
                        for c in (2 * tt, 2 * tt + 1):
                            if c == 0:
                                continue
                            pe.wait_ge(GL["state_ready"], h * (NCH - 1) + c)
                            r = slice((c % 2) * 64, (c % 2) * 64 + 64)
                            last = pe.matmul(o[r, :], gq[:, h, c * CHUNK:(c + 1) * CHUNK], states[:, c % 4, :],
                                             start=False, stop=True)
                        last.then_inc(GL["o_done"], 1)

                def turn_outputs(h):
                    pe.wait_ge(GL["o_scaled"], (h + 1) * TT)
                    if h:
                        pe.wait_ge(GL["y_ready"], 2 * h)
                    pe.wait_ge(GL["att_ready"], min(h + 2, G_HEADS))
                    for tt in range(TT):
                        for j, bank in ((0, 7), (1, 2)):
                            last = pe.transpose(banks[:, bank, tt * P:(tt + 1) * P],
                                                o_nat[:, tt, j * P:(j + 1) * P], identity[:])
                        last.then_inc(GL["o_turned"], 1)

                gate_inner()
                for v in range(2, 8):
                    pe.wait_ge(low_done, u + v + 1)
                    if v >= 3:
                        pe.wait_ge(GL["in_evac"], v - 2)
                    for half in range(2):
                        bank = banks[:, 2 * (v % 3) + half, :]
                        if v >= 4:
                            for tt in range(2 * half, 2 * half + 2):
                                last = natural(u + v, bank[:, (tt % 2) * 256:(tt % 2 + 1) * 256],
                                               slice(tt * P, (tt + 1) * P), 0, 256)
                        else:
                            last = column_chunk(u + v, block_of(half), bank, slice(0, T))
                        if half:
                            last.then_inc(unit_used, 1)
                        if v == 2:
                            gate_z(2 * half)
                            gate_z(2 * half + 1)
                        elif v >= 4 and half == 0:
                            sums(v - 4)
                        elif v >= 4:
                            turn_keys(v - 4)
                for h in range(G_HEADS):
                    v = 8 + h
                    pe.wait_ge(low_done, u + v + 1)
                    pe.wait_ge(GL["in_evac"], 7 if h == 0 else 2 * h + 7)
                    column_chunk(u + v, block_of(0), banks[:, 0, :], slice(0, T)).then_inc(GL["r_done"], 1)
                    if h:
                        outputs_of(h - 1, (2, 3))
                    else:
                        pe.wait_ge(GL["in_evac"], 8)
                        pe.wait_ge(GL["kend_ready"], G_HEADS)
                    scores(h)
                    pe.wait_ge(GL["in_evac"], 8 if h == 0 else 2 * h + 8)
                    column_chunk(u + v, block_of(1), banks[:, 1, :], slice(0, T)).then_inc(unit_used, 1)
                    if h:
                        turn_outputs(h - 1)
                    outputs_of(h, (0, 1))
                    pe.wait_ge(GL["state_ready"], h * (NCH - 1) + 4)
                    key_values(h, range(4, NCH - 1))
                outputs_of(G_HEADS - 1, (2, 3))
                pe.wait_ge(low_done, u + 13)
                pe.wait_ge(GL["out_low"], 2)
                for tt in (0, 2, 1, 3):
                    if tt == 0:
                        pe.wait_ge(GL["in_evac"], 16)
                    elif tt == 2:
                        turn_outputs(G_HEADS - 1)
                        pe.wait_ge(GL["state_ready"], G_HEADS * (NCH - 1))
                    else:
                        pe.wait_ge(GL["y_ready"], KT)
                    for k in range(2):
                        last = output_unit(u + 12, tt, k, k, k == 0, False)
                last.then_inc(unit_used, 1)
                last_units(ph, u + 13, range(2, 8), GL["out_low"], 2)

            def cross(ph):
                u, base = ph.unit, 4 * ph.nth

                def scores(h):
                    pe.wait_ge(XA["in_evac"], base + h + 1)
                    for tt in range(TT):
                        for dc in range(2):
                            last = pe.matmul(head_banks(h)[:, tt * MEM:(tt + 1) * MEM],
                                             xq[:, 2 * h + dc, tt * P:(tt + 1) * P], xk[:, 2 * h + dc, :],
                                             start=dc == 0, stop=dc == 1)
                    last.then_inc(XA["scores"], 1)

                def turn_probs(h):
                    pe.wait_ge(XA["normed"], base + h + 1)
                    for mc in range(2):
                        for tt in range(TT):
                            last = pe.transpose(head_banks(h)[:, mc * T + tt * P:mc * T + (tt + 1) * P],
                                                xp[h % 2][:, tt, mc * P:(mc + 1) * P], identity[:])
                    last.then_inc(XA["p_turned"], 1)

                def attend(h):
                    pe.wait_ge(XA["p_evac"], base + h + 1)
                    for half in range(2):
                        j = 2 * h + half
                        for mc in range(MT):
                            last = pe.matmul(head_banks(h)[:, half * T:(half + 1) * T], xv[:, mc, j * P:(j + 1) * P],
                                             xpT[:, 2 * h + mc, :], start=mc == 0, stop=mc == MT - 1)
                        last.then_inc(XA["attended"], 1)

                pe.wait_ge(low_done, u + 3)
                column_chunk(u + 2, block_of(0), banks[:, 6, :], slice(0, T))
                pe.wait_ge(XA["kv_loaded"], 32 * (ph.nth + 1))
                scores(0)
                column_chunk(u + 2, block_of(1), banks[:, 7, :], slice(0, T)).then_inc(unit_used, 1)
                scores(1)
                pe.wait_ge(low_done, u + 4)
                column_chunk(u + 3, block_of(0), banks[:, 4, :], slice(0, T))
                turn_probs(0)
                scores(2)
                column_chunk(u + 3, block_of(1), banks[:, 5, :], slice(0, T)).then_inc(unit_used, 1)
                turn_probs(1)
                scores(3)
                turn_probs(2)
                attend(0)
                attend(1)
                turn_probs(3)
                attend(2)
                attend(3)
                pe.wait_ge(low_done, u + 5)
                for tt in range(TT):
                    pe.wait_ge(XA["out_low"], 8 * ph.nth + (2, 4, 8, 8)[tt])
                    for k in range(2):
                        last = output_unit(u + 4, tt, k, k, k == 0, False)
                last.then_inc(unit_used, 1)
                last_units(ph, u + 5, range(2, 8))

            for ph in phases:
                {"ffn": ffn, "ab": window, "gla": gated, "xattn": cross}[ph.name](ph)


_INS = ["x", "mem", "norm_g", "ffn1_w_in", "ffn1_w_out", "ffn2_w_in", "ffn2_w_out", "xattn_w_q",
        "xattn_w_kv", "xattn_w_o", "ab_w_in", "ab_sink", "ab_sgu_w", "ab_sgu_b", "ab_sgu_norm_g",
        "ab_w_out", "c_w_in", "c_gate_w", "c_gate_b", "c_head_norm_g", "c_w_out"]


def build(nc, shapes):
    args = [nc.dram_tensor(f"in_{name}_dram", shape, F32, kind="ExternalInput").ap()
            for name, shape in shapes]
    result = nc.dram_tensor("out_0_dram", (1, T, D), F32, kind="ExternalOutput").ap()
    trunk_kernel(nc, *args, result)


def kernel(**inputs):
    import concourse.bacc as bacc
    from concourse.bass_utils import run_bass_kernel_spmd

    arrays = {f"in_{name}_dram": np.ascontiguousarray(inputs[name]) for name in _INS}
    arrays["in_constants_dram"] = constant_table()
    nc = bacc.Bacc("TRN2", target_bir_lowering=False, num_devices=1)
    build(nc, [(n[3:-5], a.shape) for n, a in arrays.items()])
    return run_bass_kernel_spmd(nc, [arrays], core_ids=[0]).results[0]["out_0_dram"]
```
